# Optimizing a Trainium2 kernel written in Bass

```python
import jax, jax.numpy as jnp
from jax import lax
import numpy as np

D_MODEL = 1024
BATCH = 1
SEQ = 512
DEPTH = 2

GRID_W = 64
CTX_LEN = 256
N_MIXERS = 2
N_MLA_LAYERS = (DEPTH + 1) // 2
N_CONV_LAYERS = DEPTH // 2
MLA_HEADS = 8
QK_NOPE = 128
QK_ROPE = 64
QK_DIM = QK_NOPE + QK_ROPE
V_DIM = 128
Q_LORA = 384
KV_LORA = 256
ROPE_FREQS = QK_ROPE // 4
ROPE_THETA = 10000.0
ATTN_SCALE = QK_DIM ** -0.5
Q_BLOCK = 128
CONV_WIDTH = 3
N_EXPERTS = 16
EC_CAPACITY = 2
D_EXPERT = 1024
EPS = 1e-6
ADA_INIT = 0.5

kernel_name = "hybrid_mla_shortconv_ecmoe_dit"

def rmsnorm(x, g):
    xf = x.astype(jnp.float32)
    y = xf * lax.rsqrt(jnp.mean(xf * xf, axis=-1, keepdims=True) + EPS)
    return (y * g.astype(jnp.float32)).astype(x.dtype)

def modulate(x, g, shift, scale):
    return rmsnorm(x, g) * (1 + scale) + shift

def adaln(cond, w, b):
    m = jax.nn.silu(cond) @ w + b
    return jnp.split(m, 6, axis=-1)

def axial_rope_angles(n):
    rows = n // GRID_W
    row = jnp.broadcast_to(jnp.arange(rows, dtype=jnp.float32)[:, None], (rows, GRID_W)).reshape(-1)
    col = jnp.broadcast_to(jnp.arange(GRID_W, dtype=jnp.float32)[None, :], (rows, GRID_W)).reshape(-1)
    inv = ROPE_THETA ** (-jnp.arange(ROPE_FREQS, dtype=jnp.float32) / ROPE_FREQS)
    return jnp.stack([row, col], axis=-1)[:, :, None] * inv

def apply_axial_rope(x, ang):
    cos = jnp.cos(ang)[None, :, None].astype(x.dtype)
    sin = jnp.sin(ang)[None, :, None].astype(x.dtype)
    xr = x.reshape(x.shape[:-1] + (2, 2, ROPE_FREQS))
    x1, x2 = xr[..., 0, :], xr[..., 1, :]
    out = jnp.stack([x1 * cos - x2 * sin, x2 * cos + x1 * sin], axis=-2)
    return out.reshape(x.shape)

def mla_queries(q_lat, q_norm, w_qb, q_gain, ang):
    b, n, _ = q_lat.shape
    q = (rmsnorm(q_lat, q_norm) @ w_qb).reshape(b, n, MLA_HEADS, QK_DIM)
    q = rmsnorm(q, q_gain)
    if ang is not None:
        q = jnp.concatenate([q[..., :QK_NOPE], apply_axial_rope(q[..., QK_NOPE:], ang)], axis=-1)
    return q

def mla_keys_values(kv_lat, k_rope, kv_norm, w_kvb, k_gain, ang):
    b, n, _ = kv_lat.shape
    kv = (rmsnorm(kv_lat, kv_norm) @ w_kvb).reshape(b, n, MLA_HEADS, QK_NOPE + V_DIM)
    k_nope, v = kv[..., :QK_NOPE], kv[..., QK_NOPE:]
    k_pe = jnp.broadcast_to(k_rope[:, :, None, :], (b, n, MLA_HEADS, QK_ROPE))
    k = rmsnorm(jnp.concatenate([k_nope, k_pe], axis=-1), k_gain)
    if ang is not None:
        k = jnp.concatenate([k[..., :QK_NOPE], apply_axial_rope(k[..., QK_NOPE:], ang)], axis=-1)
    return k, v

def attend(q, k, v):
    s = jnp.einsum('bqhd,bkhd->bhqk', q, k, preferred_element_type=jnp.float32) * ATTN_SCALE
    p = jax.nn.softmax(s, axis=-1).astype(v.dtype)
    return jnp.einsum('bhqk,bkhv->bqhv', p, v)

def latent_attention(q, k, v):
    b, n, h, d = q.shape
    nb = n // Q_BLOCK
    qb = jnp.moveaxis(q.reshape(b, nb, Q_BLOCK, h, d), 1, 0)
    o = lax.map(lambda qi: attend(qi, k, v), qb)
    return jnp.moveaxis(o, 0, 1).reshape(b, n, h * V_DIM)

def short_conv_mixer(h, w_in, conv_w, w_out):
    b_gate, c_gate, val = jnp.split(h @ w_in, 3, axis=-1)
    u = c_gate * val
    y = lax.conv_general_dilated(
        u, conv_w[:, None, :].astype(u.dtype), window_strides=(1,),
        padding=((CONV_WIDTH // 2, CONV_WIDTH // 2),),
        dimension_numbers=('NWC', 'WIO', 'NWC'), feature_group_count=D_MODEL)
    return (b_gate * y) @ w_out

def ec_moe(h, w_router, w_gate, w_up, w_down):
    b, n, d = h.shape
    cap = EC_CAPACITY * n // N_EXPERTS
    logits = jnp.einsum('bnd,de->ben', h, w_router, preferred_element_type=jnp.float32)
    aff = jax.nn.softmax(logits, axis=1)
    g, idx = lax.top_k(aff, cap)
    xs = jax.vmap(lambda hb, ib: hb[ib])(h, idx)
    a = jnp.einsum('becd,edf->becf', xs, w_gate)
    u = jnp.einsum('becd,edf->becf', xs, w_up)
    y = jnp.einsum('becf,efd->becd', jax.nn.silu(a) * u, w_down) * g[..., None].astype(h.dtype)
    return jax.vmap(lambda yb, ib: jnp.zeros((n, d), yb.dtype).at[ib.reshape(-1)].add(yb.reshape(-1, d)))(y, idx)

def setup_inputs(seed: int = 0) -> dict:
    key = jax.random.key(seed)
    ks = jax.random.split(key, 24)

    def nrm(k, shape, scale):
        return jax.random.normal(k, shape, jnp.float32) * scale

    return {
        "x": nrm(ks[0], (BATCH, SEQ, D_MODEL), 1.0),
        "c": nrm(ks[1], (BATCH, D_MODEL), 1.0),
        "ctx": nrm(ks[2], (BATCH, CTX_LEN, D_MODEL), 1.0),
        "c_ctx": nrm(ks[3], (D_MODEL,), 1.0),
        "norm_mix": 1.0 + nrm(ks[4], (DEPTH, D_MODEL), 0.1),
        "norm_ffn": 1.0 + nrm(ks[5], (DEPTH, D_MODEL), 0.1),
        "ada_w": nrm(ks[6], (DEPTH, D_MODEL, 6 * D_MODEL), ADA_INIT * D_MODEL ** -0.5),
        "ada_b": nrm(ks[7], (DEPTH, 6 * D_MODEL), 0.01),
        "mla_w_in": nrm(ks[8], (N_MLA_LAYERS, D_MODEL, Q_LORA + KV_LORA + QK_ROPE), D_MODEL ** -0.5),
        "mla_q_norm": 1.0 + nrm(ks[9], (N_MLA_LAYERS, Q_LORA), 0.1),
        "mla_w_qb": nrm(ks[10], (N_MLA_LAYERS, Q_LORA, MLA_HEADS * QK_DIM), Q_LORA ** -0.5),
        "mla_kv_norm": 1.0 + nrm(ks[11], (N_MLA_LAYERS, KV_LORA), 0.1),
        "mla_w_kvb": nrm(ks[12], (N_MLA_LAYERS, KV_LORA, MLA_HEADS * (QK_NOPE + V_DIM)), KV_LORA ** -0.5),
        "mla_q_gain": 1.0 + nrm(ks[13], (N_MLA_LAYERS, QK_DIM), 0.1),
        "mla_k_gain": 1.0 + nrm(ks[14], (N_MLA_LAYERS, QK_DIM), 0.1),
        "mla_w_out": nrm(ks[15], (N_MLA_LAYERS, MLA_HEADS * V_DIM, D_MODEL), (MLA_HEADS * V_DIM) ** -0.5),
        "conv_w_in": nrm(ks[16], (N_CONV_LAYERS, D_MODEL, 3 * D_MODEL), D_MODEL ** -0.5),
        "conv_w": nrm(ks[17], (N_CONV_LAYERS, CONV_WIDTH, D_MODEL), CONV_WIDTH ** -0.5),
        "conv_w_out": nrm(ks[18], (N_CONV_LAYERS, D_MODEL, D_MODEL), D_MODEL ** -0.5),
        "router_w": nrm(ks[19], (DEPTH, D_MODEL, N_EXPERTS), D_MODEL ** -0.5),
        "exp_w_gate": nrm(ks[20], (DEPTH, N_EXPERTS, D_MODEL, D_EXPERT), D_MODEL ** -0.5),
        "exp_w_up": nrm(ks[21], (DEPTH, N_EXPERTS, D_MODEL, D_EXPERT), D_MODEL ** -0.5),
        "exp_w_down": nrm(ks[22], (DEPTH, N_EXPERTS, D_EXPERT, D_MODEL), D_EXPERT ** -0.5),
    }

def reference(x, c, ctx, c_ctx, norm_mix, norm_ffn, ada_w, ada_b,
              mla_w_in, mla_q_norm, mla_w_qb, mla_kv_norm, mla_w_kvb, mla_q_gain, mla_k_gain, mla_w_out,
              conv_w_in, conv_w, conv_w_out, router_w, exp_w_gate, exp_w_up, exp_w_down):
    b, n, _ = x.shape
    ang = axial_rope_angles(n)
    for i in range(DEPTH):
        m = i // N_MIXERS
        sh_m, sc_m, g_m, sh_f, sc_f, g_f = adaln(c[:, None, :], ada_w[i], ada_b[i])
        ctx_live = any(j % N_MIXERS == 0 for j in range(i + 1, DEPTH))
        ctx_read_here = (i % N_MIXERS == 0)
        if ctx_live or ctx_read_here:
            csh_m, csc_m, cg_m, csh_f, csc_f, cg_f = adaln(c_ctx[None, None, :], ada_w[i], ada_b[i])
            hc = modulate(ctx, norm_mix[i], csh_m, csc_m)
        hx = modulate(x, norm_mix[i], sh_m, sc_m)

        if i % N_MIXERS == 0:
            q_lat, kv_lat, k_rope = jnp.split(hx @ mla_w_in[m], [Q_LORA, Q_LORA + KV_LORA], axis=-1)
            qx = mla_queries(q_lat, mla_q_norm[m], mla_w_qb[m], mla_q_gain[m], ang)
            kx, vx = mla_keys_values(kv_lat, k_rope, mla_kv_norm[m], mla_w_kvb[m], mla_k_gain[m], ang)
            kv_lat_c, k_rope_c = jnp.split(hc @ mla_w_in[m][:, Q_LORA:], [KV_LORA], axis=-1)
            kc, vc = mla_keys_values(kv_lat_c, k_rope_c, mla_kv_norm[m], mla_w_kvb[m], mla_k_gain[m], None)
            ox = latent_attention(qx, jnp.concatenate([kc, kx], axis=1), jnp.concatenate([vc, vx], axis=1))
            x = x + g_m * (ox @ mla_w_out[m])
            if ctx_live:
                qc = mla_queries(hc @ mla_w_in[m][:, :Q_LORA], mla_q_norm[m], mla_w_qb[m], mla_q_gain[m], None)
                oc = attend(qc, kc, vc).reshape(b, ctx.shape[1], MLA_HEADS * V_DIM)
                ctx = ctx + cg_m * (oc @ mla_w_out[m])
        else:
            x = x + g_m * short_conv_mixer(hx, conv_w_in[m], conv_w[m], conv_w_out[m])
            if ctx_live:
                ctx = ctx + cg_m * short_conv_mixer(hc, conv_w_in[m], conv_w[m], conv_w_out[m])

        x = x + g_f * ec_moe(modulate(x, norm_ffn[i], sh_f, sc_f), router_w[i], exp_w_gate[i], exp_w_up[i], exp_w_down[i])
        if ctx_live:
            ctx = ctx + cg_f * ec_moe(modulate(ctx, norm_ffn[i], csh_f, csc_f), router_w[i], exp_w_gate[i], exp_w_up[i], exp_w_down[i])
    return x


_drawn_inputs = setup_inputs


def setup_inputs(seed=0):
    import zlib

    import numpy as np

    out = dict(_drawn_inputs(seed))
    spreads = {}
    factors = {'ctx': 4.267,
     'ada_b': 3.113,
     'mla_q_norm': 8.0,
     'mla_kv_norm': 5.673,
     'mla_q_gain': 8.0,
     'mla_k_gain': 8.0,
     'norm_ffn': 4.217}
    for name, (base, spread) in spreads.items():
        noise = np.random.default_rng([zlib.crc32(name.encode()), seed]).standard_normal(out[name].shape)
        drawn = base * np.exp(spread * noise) if base else spread * noise
        out[name] = __import__('jax').numpy.asarray(drawn.astype(out[name].dtype))
    for name, factor in factors.items():
        out[name] = (out[name] * factor).astype(out[name].dtype)
    return out
```

```python
from contextlib import ExitStack

import numpy as np

import concourse.bass as bass
from concourse import mybir

F32 = mybir.dt.float32
U32 = mybir.dt.uint32
ALU = mybir.AluOpType
ACT = mybir.ActivationFunctionType
AX = mybir.AxisListType

P = 128
BANK = 512
GRID_W = 64
ROPE_THETA = 10000.0
EPS = 1e-6
EC_CAPACITY = 2


class Chain:

    def __init__(self, eng, sem):
        self.eng, self.sem, self.n = eng, sem, 0

    def link(self, ins):
        self.n = self.n + 1
        ins.then_inc(self.sem, 1)
        self.eng.wait_ge(self.sem, self.n)


def wait(eng, sem, n):
    if not (isinstance(n, int) and n <= 0):
        eng.wait_ge(sem, n)


def first_then_loop(eng, body, n, last=0):
    body(0)
    with eng.Fori(1, n - last) as i:
        body(i)
    for i in range(n - last, n):
        body(i)


def build(nc, x, c, ctx, c_ctx, norm_mix, norm_ffn, ada_w, ada_b, mla_w_in, mla_q_norm, mla_w_qb,
          mla_kv_norm, mla_w_kvb, mla_q_gain, mla_k_gain, mla_w_out, conv_w_in, conv_w, conv_w_out,
          router_w, exp_w_gate, exp_w_up, exp_w_down, ident_in, rope_in, out):
    _, T, D = x.shape
    CX = ctx.shape[1]
    KEYS = CX + T
    KC = D // P
    XT, CT = T // P, CX // P
    NT = XT + CT
    QL, KVL = mla_q_norm.shape[1], mla_kv_norm.shape[1]
    QC, KVC = QL // P, KVL // P
    QK = mla_q_gain.shape[1]
    NOPE = P
    ROPE = QK - NOPE
    RF = ROPE // 4
    HEADS = mla_w_qb.shape[2] // QK
    PAIRS = HEADS // 2
    LAT = mla_w_in.shape[2]
    VD = mla_w_kvb.shape[2] // HEADS - NOPE
    E, FF = exp_w_gate.shape[1], exp_w_gate.shape[3]
    CAP = EC_CAPACITY * T // E
    SCALE = float(QK) ** -0.5
    HALF = D // 2
    SCR = KEYS // 2
    UNITS = 6 * D // BANK
    assert VD == P and D == FF == 2 * BANK and T == BANK and CAP * 2 == P and D == KC * P and LAT == QL + KVL + ROPE

    es = ExitStack()
    with es:
        def sb(name, cols, dt=F32, rows=P):
            return es.enter_context(nc.sbuf_tensor(name, [rows, cols], dt))[:, :]

        def sem(name):
            return es.enter_context(nc.semaphore(name))

        R = [sb(f"ring{n}", KC * FF) for n in range(3)]
        W = sb("work", 22528)
        PS = es.enter_context(nc.psum_tensor("ps", [P, 8, BANK], F32))

        def view(t, lo, *dims):
            n = int(np.prod(dims))
            v = t[:, lo:lo + n]
            if len(dims) == 2:
                v = v.rearrange("p (a b) -> p a b", b=dims[1])
            if len(dims) == 3:
                v = v.rearrange("p (a b c) -> p a b c", b=dims[1], c=dims[2])
            return v

        ident = sb("ident", P)
        cond_rows, vec_rows = W[:, 20736:20736 + P], W[:, 20864:20864 + P]
        vec = sb("vec", P)
        NR = 127
        V_NM, V_NF, V_ADA, V_QN, V_KVN, V_GQ, V_GK, V_CONV = 0, 16, 32, 96, 99, 101, 102, 103
        cond_T = view(sb("cond_T", KC * 32), 0, KC, 32)
        sel2 = sb("sel2", 2)
        selx = sb("selx", P)
        eps = sb("eps", 1)
        ada_part = view(sb("ada_part", 2 * BANK), 0, 2, BANK)
        junk = ada_part.rearrange("p a b -> p (a b)")
        modv = [[view(sb(f"mod{L}{n}", 2 * KC * 2), 0, 2, KC, 2) for n in "mf"] for L in range(2)]
        scl = [[view(sb(f"scl{L}{n}", KC * 2), 0, KC, 2) for n in "mf"] for L in range(2)]
        gate_mix = [sb(f"gate_mix{L}", D) for L in range(2)]
        gate_ffn = [sb(f"gate_ffn{L}", HALF) for L in range(2)]
        router = [view(sb(f"router{L}", KC * E), 0, KC, E) for L in range(2)]
        rope_cs = view(sb("rope_cs", 2 * XT * 2 * 2 * RF), 0, 2, XT * 2, 2 * RF)
        rope_gain = view(W, 22272, 2, ROPE)
        gqk = sb("gqk", 1)
        stat = sb("stat", 96)
        smal = sb("smal", 64)
        probs = sb("probs", E)
        aff = view(sb("aff", XT * E), 0, XT, E)
        affT = junk[0:E, :]
        at = (18944, 12288)
        top_v = [W[0:E, a:a + CAP] for a in at]
        top_i = [W[0:E, a + CAP:a + 2 * CAP].bitcast(U32) for a in at]
        slots_i = [W[0:E, a + P:a + 2 * P] for a in at]
        slots_v = [W[0:E, a + 2 * P:a + 3 * P] for a in at]
        row_no = sb("row_no", E, U32)
        gate_e = sb("gate_e", E)
        row_in = [sb(f"row_in{s}", 1, U32) for s in range(2)]
        row_out = sb("row_out", 1, U32)

        xn_dram = nc.dram_tensor("xn_rows", (T, D), F32, kind="Internal").ap()
        mid_dram = nc.dram_tensor("mid_rows", (T, D), F32, kind="Internal").ap()
        out_rows = out.rearrange("a t d -> (a t) d")
        acc_dram = [mid_dram, out_rows]

        w_qb = view(W, 0, QC, HEADS * QK)
        w_kvb = view(W, 4608, KVC, HEADS * (NOPE + VD))
        qlT = view(W, 8704, QC, T)
        kvlT = view(W, 10240, KVC, KEYS)
        krot = view(W, 11776, NT, ROPE)
        rows_in = view(W, 12288, NT, D)
        lat = view(W, 18432, 2, LAT)
        kraw = view(W, 19840, NT, ROPE)
        ktmp = view(W, 20224, 2, XT, 2 * RF)
        kvtok = view(W, 12288, NT, 2 * (NOPE + VD))
        qtok = view(W, 15360, XT, 2 * QK)
        qT = view(W, 16896, 2, T)
        qTr = view(W, 17920, T)
        kT = view(W, 18432, 2, KEYS)
        kTr = view(W, 19968, KEYS)
        prob = view(W, 20736, 2, KEYS)
        w_in = view(R[2], 0, KC, LAT)
        hT = view(R[1], 0, KC, KEYS)
        junk_in = view(R[1], 6144, D)
        pT = [view(R[0], j * 3072, NT, T) for j in range(2)]
        sqq = view(R[0], 6144, XT * 2, QK)
        oT = view(R[1], 0, HEADS, T)
        sqk = view(R[1], 4096, NT * 2, NOPE)
        kr_s = view(R[1], 5632, NT, 2 * ROPE)
        q_rot = view(R[1], 6400, XT, 2 * ROPE)
        rtmp = view(R[1], 6912, 4, XT * 2 * 2 * RF)
        w_mla_out = view(R[2], 0, KC, D)
        w_conv_out = view(W, 0, KC, D)
        w_cb = view(W, 8192, KC, D)
        w_cc = view(R[1], 0, KC, D)
        w_cv = view(R[2], 0, KC, D)
        hT1 = view(R[0], 0, KC, T)
        xnc = view(W, 16384, XT, D)
        zT = view(W, 16384, KC, T)
        c_sb = view(W, 20480, 2, T)
        u_pad = view(W, 21504, T + 2)
        y_sb = ada_part[:, 0, :]
        w_out = [w_mla_out, w_conv_out]
        mixT = [oT, zT]
        xres = [view(W, 12288, XT, D), view(R[0], 4096, XT, D)]
        hfT = view(W, 8192, 2, KC * P)
        mo_tmp = view(W, 10240, D)
        hf_tmp = view(W, 11264, D)
        xnt = view(W, 20480, 2, D)
        xs = view(W, 16384, 2, HALF)
        xs_m = view(W, 17408, HALF)
        xsT = view(W, 17920, 2, HALF)
        silu_a = view(W, 18944, BANK)
        hid = view(W, 19456, BANK)
        hidT = view(W, 19968, BANK)
        y_s = view(W, 20480, 2, BANK)
        wg, wu, wd = (view(r, 0, KC, FF) for r in R)

        cond_in, vec_in, ident_in_s, misc_in = sem("cond_in"), sem("vec_in"), sem("ident_in_s"), sem("misc_in")
        rows_in_s = [sem("ctx_in"), sem("x_in")]
        win_in, wqb_in, wkvb_in = sem("win_in"), sem("wqb_in"), sem("wkvb_in")
        mixw_in = [sem("mla_out_in"), sem("conv_out_in")]
        cb_in, cc_in, cv_in, mid_in, xres_in = sem("cb_in"), sem("cc_in"), sem("cv_in"), sem("mid_in"), sem("xres_in")
        silu_c, zeroed, setup_T, setup_out, sels = (sem(n) for n in ("silu_c", "zeroed", "setup_T", "setup_out", "sels"))
        sq_in, std_in, xn_in, inT, inT_a, inT_d = (sem(n) for n in ("sq_in", "std_in", "xn_in", "inT", "inT_a", "inT_d"))
        ada_in = [sem("ada_in0"), sem("ada_in1")]
        ada_main, ada_rows, ada_sum, ada_out, mod_ready = (sem(n) for n in (
            "ada_main", "ada_rows", "ada_sum", "ada_out", "mod_ready"))
        lat_done, lat_a, lat_d, lat_std, lat_n, latT, latT_d, krot_ready = (sem(n) for n in (
            "lat_done", "lat_a", "lat_d", "lat_std", "lat_n", "latT", "latT_d", "krot_ready"))
        proj, proj_a, proj_d, sq_ready, ss_ready, std_ready, rk_ready, kn_ready, krs_ready = (sem(n) for n in (
            "proj", "proj_a", "proj_d", "sq_ready", "ss_ready", "std_ready", "rk_ready", "kn_ready", "krs_ready"))
        qg_ready, qrot_d, qrot_p, trn, trn_a, trn_d = (sem(n) for n in (
            "qg_ready", "qrot_d", "qrot_p", "trn", "trn_a", "trn_d"))
        s_done, nmax, exp_done, p_norm, pT_done, pT_a, pT_d, pv_done, oT_ready = (sem(n) for n in (
            "s_done", "nmax", "exp_done", "p_norm", "pT_done", "pT_a", "pT_d", "pv_done", "oT_ready"))
        dve_step, act_step, pool_step, turn = sem("dve_step"), sem("act_step"), sem("pool_step"), sem("turn")
        cn_std, cn_xn, cn_T, cn_Ta, conv_mm, c_copied, z_ready = (sem(n) for n in (
            "cn_std", "cn_xn", "cn_T", "cn_Ta", "conv_mm", "c_copied", "z_ready"))

        def layer_sems(*names):
            return [[sem(f"{n}{L}") for L in range(2)] for n in names]

        (mo_done, mo_mul, x_new, x_std, xn_ready, xnT, hf_mul, hf_ready, lg_done, lg_neg, lg_exp, lg_aff,
         affT_ps, affT_sb) = layer_sems("mo_done", "mo_mul", "x_new", "x_std", "xn_ready", "xnT", "hf_mul",
                                        "hf_ready", "lg_done", "lg_neg", "lg_exp", "lg_aff", "affT_ps", "affT_sb")
        acc_stored, xn_st0, xn_st1, slots_f, slots_T, slots_ready = layer_sems(
            "acc_stored", "xn_st0_", "xn_st1_", "slots_f", "slots_T", "slots_ready")
        (wg_in, wu_in, wd_in, row_copied, row_out_ok, xs_in0, xs_in1, xs_T, xs_mod, gate_mm, up_mm, silu_ok, hid_ok, hid_T, hidT_ok,
         down_mm, y_ok, scattered) = layer_sems(
            "wg_in", "wu_in", "wd_in", "row_copied", "row_out_ok", "xs_in0_", "xs_in1_", "xs_T", "xs_mod", "gate_mm", "up_mm",
            "silu_ok", "hid_ok", "hid_T", "hidT_ok", "down_mm", "y_ok", "scattered")

        TILES = [CT + t for t in range(XT)] + list(range(CT))
        UNITS_AFTER = [3, 3, 3, 3, 4, 4]
        PARTS = 4
        FIRST_UNITS = 4
        T_BANKS = [0, 1, 3, 4, 5]
        ADA_BANKS = [2, 6]

        def units_after(n):
            lo = FIRST_UNITS + sum(UNITS_AFTER[:n])
            return range(lo, lo + UNITS_AFTER[n])

        block = es.enter_context(nc.Block())

        @block.sync
        def _(sp):
            def load_ada(u):
                L, n = u // UNITS, u % UNITS
                if u >= 2:
                    sp.wait_ge(ada_main, u - 1)
                sp.dma_start(view(R[0], (u % 2) * 4096, KC, BANK),
                             ada_w[L, :, n * BANK:(n + 1) * BANK].rearrange("(k p) n -> p k n", p=P)
                             ).then_inc(ada_in[u % 2], 16)

            sp.dma_start(rows_in[:, 0:CT, :], ctx[0].rearrange("(t p) d -> p t d", p=P)).then_inc(rows_in_s[0], 16)
            sp.dma_start(rows_in[:, CT:NT, :], x[0].rearrange("(t p) d -> p t d", p=P)).then_inc(rows_in_s[1], 16)
            for u in range(FIRST_UNITS):
                load_ada(u)
            sp.dma_start(w_in, mla_w_in[0].rearrange("(k p) n -> p k n", p=P)).then_inc(win_in, 16)
            for u in range(FIRST_UNITS, 2 * UNITS):
                load_ada(u)
                if u == 8:
                    sp.dma_start(w_kvb, mla_w_kvb[0].rearrange("(k p) n -> p k n", p=P)).then_inc(wkvb_in, 16)
                    sp.dma_start(w_qb, mla_w_qb[0].rearrange("(k p) n -> p k n", p=P)).then_inc(wqb_in, 16)
            sp.wait_ge(lat_done, NT)
            sp.dma_start(w_mla_out, mla_w_out[0].rearrange("(k p) n -> p k n", p=P)).then_inc(mixw_in[0], 16)

            def load_expert(w, dst, L, e, done):
                for k in range(0, KC, KC // PARTS):
                    sp.dma_start(dst[:, k:k + KC // PARTS, :],
                                 w[L, e][k * P:(k + KC // PARTS) * P, :].rearrange("(k p) n -> p k n", p=P)).then_inc(done[L], 16)

            def stores(L):
                for t in range(XT):
                    sp.wait_ge(x_new[L], t + 1)
                    sp.dma_start(acc_dram[L][t * P:(t + 1) * P, :], xres[L][:, t, :]).then_inc(acc_stored[L], 16)
                    sp.wait_ge(xn_ready[L], t + 1)
                    sp.dma_start(xn_dram[t * P:(t + 1) * P, :], xnt[:, t % 2, :]).then_inc((xn_st0, xn_st1)[t % 2][L], 16)

            def expert_stream(L):
                with sp.Fori(1, E) as e:
                    sp.wait_ge(gate_mm[L], e)
                    load_expert(exp_w_gate, wg, L, e, wg_in)
                    sp.wait_ge(up_mm[L], e)
                    load_expert(exp_w_up, wu, L, e, wu_in)
                    sp.wait_ge(down_mm[L], e)
                    load_expert(exp_w_down, wd, L, e, wd_in)

            sp.wait_ge(pv_done, HEADS)
            sp.wait_ge(oT_ready, HEADS)
            sp.dma_start(xres[0], x[0].rearrange("(t p) d -> p t d", p=P)).then_inc(xres_in, 16)
            load_expert(exp_w_gate, wg, 0, 0, wg_in)
            stores(0)
            sp.wait_ge(mo_done[0], XT)
            load_expert(exp_w_up, wu, 0, 0, wu_in)
            load_expert(exp_w_down, wd, 0, 0, wd_in)
            expert_stream(0)
            sp.wait_ge(up_mm[0], E)
            sp.dma_start(w_cc, conv_w_in[0, :, D:2 * D].rearrange("(k p) n -> p k n", p=P)).then_inc(cc_in, 16)
            sp.wait_ge(scattered[0], 16 * E)
            sp.dma_start(xres[1], mid_dram.rearrange("(t p) d -> p t d", p=P)).then_inc(mid_in, 16)
            sp.dma_start(w_cv, conv_w_in[0, :, 2 * D:3 * D].rearrange("(k p) n -> p k n", p=P)).then_inc(cv_in, 16)
            sp.wait_ge(conv_mm, KC)
            load_expert(exp_w_up, wu, 1, 0, wu_in)
            load_expert(exp_w_down, wd, 1, 0, wd_in)
            stores(1)
            sp.wait_ge(acc_stored[1], 16 * XT)
            load_expert(exp_w_gate, wg, 1, 0, wg_in)
            expert_stream(1)
            sp.wait_ge(scattered[1], 16 * E)

        @block.tensor
        def _(pe):
            mm, tr = nc.tensor.matmul, nc.tensor.transpose

            def ada_product(u):
                b = ADA_BANKS[u % 2]
                pe.wait_ge(ada_in[u % 2], 16 * (u // 2 + 1))
                if u >= 2:
                    pe.wait_ge(ada_rows, u - 1)
                wv = view(R[0], (u % 2) * 4096, KC, BANK)
                for kk in range(2):
                    for g in range(4):
                        k = 2 * g + kk
                        last = mm(PS[32 * g:32 * g + 32, b, :], cond_T[:, k, :], wv[:, k, :], start=kk == 0, stop=kk == 1)
                last.then_inc(ada_main, 1)

            def ada_collect(u):
                n, half = (u % UNITS) // 2, u % 2
                pe.wait_ge(ada_rows, u + 1)
                if u >= 1:
                    pe.wait_ge(ada_out, u)
                part = ada_part[:, u % 2, :]
                if n == 2:
                    last = mm(PS[:, 7, :], selx, part, start=True, stop=True)
                elif n == 5:
                    last = mm(PS[64 * half:64 * half + 64, 7, :], selx[:, 0:64], part, start=True, stop=True)
                else:
                    for q in range(4):
                        last = mm(PS[:, 7, 2 * q:2 * q + 2], part[:, q * P:(q + 1) * P], sel2, start=True, stop=True)
                last.then_inc(ada_sum, 1)

            pe.wait_ge(ident_in_s, 16)
            pe.wait_ge(silu_c, 1)
            tr(PS[:, 7, 0:2 * KC], cond_rows[0:2 * KC, :], ident[0:2 * KC, 0:2 * KC]).then_inc(setup_T, 1)
            pe.wait_ge(vec_in, 16 * 12)
            tr(PS[:, 6, 0:NR], vec_rows[0:NR, :], ident[0:NR, 0:NR]).then_inc(setup_T, 1)

            def input_T(g):
                b = T_BANKS[g % 5]
                if g >= 5:
                    pe.wait_ge(inT_a, g - 4)
                for q in range(4):
                    k, t = (g, CT + q) if g < KC else (2 * (g - KC) + q // 2, q % 2)
                    last = tr(PS[:, b, q * P:(q + 1) * P], rows_in[:, t, k * P:(k + 1) * P], ident)
                last.then_inc(inT, 1)

            pe.wait_ge(xn_in, NT)
            for g in range(5):
                input_T(g)
            pe.wait_ge(setup_out, 2)
            pe.wait_ge(sels, 1)
            for u in range(FIRST_UNITS):
                ada_product(u)
                if u >= 1:
                    ada_collect(u - 1)
            ada_collect(FIRST_UNITS - 1)
            for g in range(5, 12):
                input_T(g)

            pe.wait_ge(win_in, 16)
            pe.wait_ge(inT_a, KC)
            pe.wait_ge(inT_d, 4)
            for n, j in enumerate(TILES):
                if n >= 1:
                    pe.wait_ge(lat_a, n)
                    pe.wait_ge(lat_d, min(n, XT))
                cuts = [(4, 0, BANK), (5, BANK, LAT)] if j >= CT else [(4, QL, LAT)]
                for b, lo, hi in cuts:
                    for k in range(KC):
                        last = mm(PS[:, b, 0:hi - lo], hT[:, k, j * P:(j + 1) * P], w_in[:, k, lo:hi],
                                  start=k == 0, stop=k == KC - 1)
                last.then_inc(lat_done, 1)
                for u in units_after(n):
                    ada_product(u)
                    if u > FIRST_UNITS:
                        ada_collect(u - 1)
                pe.wait_ge(lat_n, n + 1)
                if n >= 1:
                    pe.wait_ge(latT_d, n)
                if j >= CT:
                    for q in range(QC):
                        tr(PS[:, 0, q * P:(q + 1) * P], lat[:, n % 2, q * P:(q + 1) * P], ident)
                for q in range(KVC):
                    last = tr(PS[:, 1, q * P:(q + 1) * P], lat[:, n % 2, QL + q * P:QL + (q + 1) * P], ident)
                last.then_inc(latT, 1)
            ada_collect(2 * UNITS - 1)

            pe.wait_ge(latT_d, NT)
            pe.wait_ge(krot_ready, 1)
            pe.wait_ge(wqb_in, 16)
            pe.wait_ge(wkvb_in, 16)
            pe.wait_ge(ada_rows, 2 * UNITS)
            pe.wait_ge(ada_out, 2 * UNITS)
            def pair(i):
                for s in range(NT + XT):
                    b = 6 + s % 2
                    if s < 2:
                        wait(pe, oT_ready, 2 * i)
                    elif s % 2 == 0:
                        pe.wait_ge(proj_a, 5 * i + s // 2)
                    else:
                        pe.wait_ge(proj_d, 5 * i + s // 2)
                    if s < NT:
                        for q in range(KVC):
                            last = mm(PS[:, b, :], kvlT[:, q, s * P:(s + 1) * P],
                                      w_kvb[:, q, bass.ds(i * BANK, BANK)], start=q == 0, stop=q == KVC - 1)
                    else:
                        for q in range(QC):
                            last = mm(PS[:, b, 0:2 * QK], qlT[:, q, (s - NT) * P:(s - NT + 1) * P],
                                      w_qb[:, q, bass.ds(i * 2 * QK, 2 * QK)], start=q == 0, stop=q == QC - 1)
                    last.then_inc(proj, 1)
                groups = ([[(kvtok[:, t, 0:P]) for t in range(4)]]
                          + [[kvtok[:, t, 256:256 + P] for t in range(4)]]
                          + [[kvtok[:, 4 + q % 2, 256 * (q // 2):256 * (q // 2) + P] for q in range(4)]]
                          + [[kr_s[:, t, :] for t in range(4)]]
                          + [[kr_s[:, t, :] for t in range(4, 6)]]
                          + [[qtok[:, t, h * QK:h * QK + P] for t in range(XT)] for h in range(2)]
                          + [[q_rot[:, t, :] for t in range(XT)]])
                for g, srcs in enumerate(groups):
                    if g == 0:
                        pe.wait_ge(kn_ready, i + 1)
                    if g == 3:
                        pe.wait_ge(krs_ready, i + 1)
                    if g == 5:
                        pe.wait_ge(qg_ready, i + 1)
                    if g == 7:
                        pe.wait_ge(qrot_d, i + 1)
                        pe.wait_ge(qrot_p, i + 1)
                    if g >= 2:
                        pe.wait_ge((trn_a, trn_d)[g % 2], 4 * i + g // 2)
                    for q, src in enumerate(srcs):
                        last = tr(PS[:, 4 + g % 2, q * P:(q + 1) * P], src, ident)
                    last.then_inc(trn, 1)

                def scores(r):
                    j, t = r // XT, r % XT
                    if r == 0:
                        pe.wait_ge(trn_a, 4 * i + 4)
                        pe.wait_ge(trn_d, 4 * i + 4)
                    if r >= 2:
                        pe.wait_ge(exp_done, 8 * i + r - 1)
                    for h in range(2):
                        o = PS[:, 2 * (r % 2) + h, 0:SCR]
                        mm(o, qT[:, j, t * P:(t + 1) * P], kT[:, j, h * SCR:(h + 1) * SCR], start=True, stop=False)
                        last = mm(o, qTr[64 * j:64 * j + 64, t * P:(t + 1) * P],
                                  kTr[64 * j:64 * j + 64, h * SCR:(h + 1) * SCR], start=False, stop=True)
                    last.then_inc(s_done, 1)

                def probs_T(r):
                    pe.wait_ge(p_norm, 8 * i + r + 1)
                    wait(pe, pT_a, 8 * i + r)
                    wait(pe, pT_d, 8 * i + r)
                    for q in range(NT):
                        last = tr(PS[:, 4 + q // 4, (q % 4) * P:(q % 4 + 1) * P], prob[:, r % 2, q * P:(q + 1) * P], ident)
                    last.then_inc(pT_done, 1)

                def values(j):
                    pe.wait_ge(pT_a, 8 * i + 4 * j + 4)
                    pe.wait_ge(pT_d, 8 * i + 4 * j + 4)
                    for q in range(NT):
                        last = mm(PS[:, 6 + j, :], kvtok[:, q, 256 * j + NOPE:256 * j + NOPE + VD], pT[j][:, q, :],
                                  start=q == 0, stop=q == NT - 1)
                    last.then_inc(pv_done, 1)

                for r in range(2 * XT):
                    scores(r)
                    if r >= 1:
                        probs_T(r - 1)
                    if r == 5:
                        values(0)
                probs_T(2 * XT - 1)
                values(1)

            first_then_loop(pe, pair, PAIRS)

            def mixer_out(L):
                pe.wait_ge(mixw_in[L], 16)
                if L == 0:
                    pe.wait_ge(oT_ready, HEADS)
                else:
                    pe.wait_ge(z_ready, KC)
                for t in range(XT + 3):
                    if t < XT:
                        if t >= 2:
                            pe.wait_ge(x_std[L], t - 1)
                        for h in range(2):
                            for k in range(KC):
                                last = mm(PS[:, 2 * (t % 2) + h, :], mixT[L][:, k, t * P:(t + 1) * P],
                                          w_out[L][:, k, h * BANK:(h + 1) * BANK], start=k == 0, stop=k == KC - 1)
                        last.then_inc(mo_done[L], 1)
                    if 1 <= t <= XT:
                        v = t - 1
                        pe.wait_ge(xn_ready[L], v + 1)
                        pe.wait_ge(hf_mul[L], v)
                        for k in range(KC):
                            last = tr(PS[:, 4 + k // 4, (k % 4) * P:(k % 4 + 1) * P], xnt[:, v % 2, k * P:(k + 1) * P], ident)
                        last.then_inc(xnT[L], 1)
                    if 2 <= t <= XT + 1:
                        v = t - 2
                        pe.wait_ge(hf_ready[L], v + 1)
                        pe.wait_ge(lg_exp[L], v)
                        for k in range(KC):
                            last = mm(PS[:, 6, 0:E], hfT[:, v % 2, k * P:(k + 1) * P], router[L][:, k, :],
                                      start=k == 0, stop=k == KC - 1)
                        last.then_inc(lg_done[L], 1)
                    if 3 <= t:
                        v = t - 3
                        pe.wait_ge(lg_aff[L], v + 1)
                        pe.wait_ge(affT_sb[L], v)
                        tr(PS[0:E, 7, 0:P], aff[:, v, :], ident).then_inc(affT_ps[L], 1)
                pe.wait_ge(slots_f[L], 1)
                tr(PS[:, 7, 0:E], slots_i[L], ident[0:E, 0:E])
                tr(PS[:, 7, E:2 * E], slots_v[L], ident[0:E, 0:E]).then_inc(slots_T[L], 1)

            def experts(L):
                def rows_T(i, s):
                    pe.wait_ge((xs_in0, xs_in1)[s][L], 16 * i + 16)
                    wait(pe, xs_mod[L], 2 * i + s)
                    for q in range(4):
                        last = tr(PS[:, 4, q * P:(q + 1) * P], xs[:, s, q * P:(q + 1) * P], ident)
                    last.then_inc(xs_T[L], 1)

                def halves(bank, lhsT, w, done):
                    for k in range(KC):
                        lhs = lhsT[:, (k % 4) * P + 64 * (k // 4):(k % 4) * P + 64 * (k // 4) + 64]
                        for h in range(2):
                            last = mm(PS[64 * h:64 * h + 64, bank, :], lhs, w[:, k, h * BANK:(h + 1) * BANK],
                                      start=k == 0, stop=k == KC - 1)
                    last.then_inc(done, 1)

                def two_experts(i):
                    for s in range(2):
                        e = 2 * i + s
                        pe.wait_ge(xs_mod[L], e + 1)
                        pe.wait_ge(wg_in[L], 16 * PARTS * (e + 1))
                        wait(pe, silu_ok[L], e)
                        halves(0, xsT[:, s, :], wg, gate_mm[L])
                        pe.wait_ge(wu_in[L], 16 * PARTS * (e + 1))
                        wait(pe, hid_ok[L], e)
                        halves(1, xsT[:, s, :], wu, up_mm[L])
                        if not (isinstance(e, int) and e == E - 1):
                            rows_T(i + s, 1 - s)
                        pe.wait_ge(hid_ok[L], e + 1)
                        wait(pe, hidT_ok[L], e)
                        for q in range(4):
                            last = tr(PS[:, 3, q * P:(q + 1) * P], hid[:, q * P:(q + 1) * P], ident)
                        last.then_inc(hid_T[L], 1)
                        pe.wait_ge(wd_in[L], 16 * PARTS * (e + 1))
                        pe.wait_ge(hidT_ok[L], e + 1)
                        wait(pe, y_ok[L], e)
                        halves(2, hidT, wd, down_mm[L])

                rows_T(0, 0)
                first_then_loop(pe, two_experts, E // 2, last=1)

            mixer_out(0)
            experts(0)

            pe.wait_ge(cn_xn, XT)
            for g in range(KC):
                if g >= 4:
                    pe.wait_ge(cn_Ta, g - 3)
                for t in range(XT):
                    last = tr(PS[:, g % 4, t * P:(t + 1) * P], xnc[:, t, g * P:(g + 1) * P], ident)
                last.then_inc(cn_T, 1)
            pe.wait_ge(cn_Ta, KC)
            pe.wait_ge(cb_in, 16)
            for n in range(KC):
                if n >= 2:
                    pe.wait_ge(z_ready, n - 1)
                for m, w in enumerate((w_cb, w_cc, w_cv)):
                    if n == 0 and m == 1:
                        pe.wait_ge(cc_in, 16)
                    if n == 0 and m == 2:
                        pe.wait_ge(cv_in, 16)
                    for k in range(KC):
                        last = mm(PS[:, 3 * (n % 2) + m, :], w[:, k, n * P:(n + 1) * P], hT1[:, k, :],
                                  start=k == 0, stop=k == KC - 1)
                last.then_inc(conv_mm, 1)

            mixer_out(1)
            experts(1)

        @block.scalar
        def _(act):
            f = nc.scalar.activation
            own = Chain(act, act_step)
            act.dma_start(cond_rows[0:KC, :], c.rearrange("a (k p) -> (a k) p", p=P)).then_inc(cond_in, 16)
            act.dma_start(cond_rows[KC:2 * KC, :], c_ctx.rearrange("(k p) -> k p", p=P)).then_inc(cond_in, 16)
            act.dma_start(ident, ident_in).then_inc(ident_in_s, 16)
            vecs = [(V_NM, norm_mix.rearrange("a (k p) -> (a k) p", p=P)), (V_NF, norm_ffn.rearrange("a (k p) -> (a k) p", p=P)),
                    (V_QN, mla_q_norm.rearrange("a (k p) -> (a k) p", p=P)), (V_KVN, mla_kv_norm.rearrange("a (k p) -> (a k) p", p=P)),
                    (V_GQ, mla_q_gain[:, 0:NOPE]), (V_GK, mla_k_gain[:, 0:NOPE]),
                    (V_CONV, conv_w.rearrange("a j (k p) -> (a j k) p", p=P))]
            for L in range(2):
                for m in range(2):
                    vecs.append((V_ADA + 32 * L + 16 * m,
                                 ada_b[L, 3 * D * m:3 * D * m + 2 * D].rearrange("(k p) -> k p", p=P)))
            for lo, src in vecs:
                act.dma_start(vec_rows[lo:lo + src.shape[0], :], src).then_inc(vec_in, 16)
            act.dma_start(vec_rows[NR:P, :], ident_in[0:1, :]).then_inc(vec_in, 16)
            for L in range(2):
                act.dma_start(gate_mix[L], ada_b[L:L + 1, 2 * D:3 * D].to_broadcast([P, D])).then_inc(misc_in, 16)
                for h in range(2):
                    act.dma_start(gate_ffn[L][64 * h:64 * h + 64, :],
                                  ada_b[L:L + 1, 5 * D + HALF * h:5 * D + HALF * (h + 1)].to_broadcast([64, HALF])
                                  ).then_inc(misc_in, 16)
                act.dma_start(router[L], router_w[L].rearrange("(k p) e -> p k e", p=P)).then_inc(misc_in, 16)
            for h in range(2):
                act.dma_start(rope_gain[:, h, :], (mla_q_gain, mla_k_gain)[h][:, NOPE:QK].to_broadcast([P, ROPE])).then_inc(misc_in, 16)
                for m in range(2):
                    act.dma_start(rope_cs[:, m, :, :].rearrange("p (t h) f -> p t h f", h=2)[:, :, h, :],
                                  rope_in[m].rearrange("(t p) f -> p t f", p=P)).then_inc(misc_in, 16)
            act.wait_ge(cond_in, 32)
            f(cond_rows[0:2 * KC, :], cond_rows[0:2 * KC, :], ACT.Silu).then_inc(silu_c, 1)
            act.wait_ge(rows_in_s[0], 16)
            for j in range(NT):
                if j == CT:
                    act.wait_ge(rows_in_s[1], 16)
                own.link(f(junk_in, rows_in[:, j, :], ACT.Square, accum_out=stat[:, j:j + 1]))
            act.wait_ge(zeroed, 3)
            f(stat[:, 8:8 + NT], stat[:, 0:NT], ACT.Sqrt, bias=eps, scale=1.0 / D).then_inc(std_in, 1)

            def ada_copy(u):
                act.wait_ge(ada_main, u + 1)
                if u >= 2:
                    act.wait_ge(ada_sum, u - 1)
                f(ada_part[:, u % 2, :], PS[:, ADA_BANKS[u % 2], :], ACT.Copy).then_inc(ada_rows, 1)

            for u in range(FIRST_UNITS):
                ada_copy(u)
            act.wait_ge(mod_ready, 1)
            for g in range(KC):
                act.wait_ge(inT, g + 1)
                f(hT[:, g, CX:KEYS], PS[:, T_BANKS[g % 5], :], ACT.Identity, bias=modv[0][0][:, 0, g, 0:1],
                  scale=scl[0][0][:, g, 0:1]).then_inc(inT_a, 1)
            for n, j in enumerate(TILES):
                act.wait_ge(lat_done, n + 1)
                if n >= 2:
                    act.wait_ge(latT, n - 1)
                if j >= CT:
                    own.link(f(lat[:, n % 2, 0:BANK], PS[:, 4, :], ACT.Copy))
                    act.sem_inc(lat_a, 1)
                    act.wait_ge(lat_d, n + 1)
                    own.link(f(junk_in[:, 0:QL], lat[:, n % 2, 0:QL], ACT.Square, accum_out=stat[:, 16 + j:17 + j]))
                else:
                    own.link(f(lat[:, n % 2, QL:LAT], PS[:, 4, 0:LAT - QL], ACT.Copy))
                    act.sem_inc(lat_a, 1)
                own.link(f(junk_in[:, 0:KVL], lat[:, n % 2, QL:QL + KVL], ACT.Square, accum_out=stat[:, 24 + j:25 + j]))
                own.link(f(junk_in[:, 0:ROPE], lat[:, n % 2, QL + KVL:LAT], ACT.Square, accum_out=stat[:, 32 + j:33 + j]))
                if j >= CT:
                    f(stat[:, 40 + j:41 + j], stat[:, 16 + j:17 + j], ACT.Sqrt, bias=eps, scale=1.0 / QL)
                f(stat[:, 48 + j:49 + j], stat[:, 24 + j:25 + j], ACT.Sqrt, bias=eps, scale=1.0 / KVL).then_inc(lat_std, 1)
                for u in units_after(n):
                    ada_copy(u)

            act.wait_ge(lat_n, NT)
            def pair(i):
                def take(s):
                    act.wait_ge(proj, 10 * i + s + 1)
                    dst = kvtok[:, s, :] if s < NT else qtok[:, s - NT, :]
                    f(dst, PS[:, 6, 0:dst.shape[1]], ACT.Copy).then_inc(proj_a, 1)

                for s in (0, 2, 4):
                    take(s)
                act.wait_ge(proj_a, 5 * i + 3)
                act.wait_ge(proj_d, 5 * i + 3)
                f(sqk, kvtok.rearrange("p t (h n) -> p (t h) n", h=2)[:, :, 0:NOPE], ACT.Square).then_inc(sq_ready, 1)
                take(6)
                act.wait_ge(ss_ready, 2 * i + 1)
                f(smal[:, 16:28], smal[:, 0:12], ACT.Sqrt, bias=eps, scale=1.0 / QK).then_inc(std_ready, 1)
                take(8)
                act.wait_ge(proj_a, 5 * i + 5)
                act.wait_ge(proj_d, 5 * i + 5)
                f(sqq, qtok.rearrange("p t (h n) -> p (t h) n", h=2), ACT.Square).then_inc(sq_ready, 1)
                act.wait_ge(ss_ready, 2 * i + 2)
                f(smal[:, 40:48], smal[:, 32:40], ACT.Sqrt, bias=eps, scale=1.0 / QK).then_inc(std_ready, 1)
                for g in (0, 2, 4, 6):
                    act.wait_ge(trn, 8 * i + g + 1)
                    if g == 0:
                        ins = f(kT[:, 0, 0:BANK], PS[:, 4, :], ACT.Copy)
                    elif g == 2:
                        ins = f(kT[:, :, BANK:KEYS], PS[:, 4, :].rearrange("p (a b) -> p a b", a=2), ACT.Copy)
                    elif g == 4:
                        ins = f(kTr[:, BANK:KEYS], PS[:, 4, 0:KEYS - BANK], ACT.Copy)
                    else:
                        ins = f(qT[:, 1, :], PS[:, 4, :], ACT.Copy, scale=gqk)
                    ins.then_inc(trn_a, 1)

                def take_pT(r):
                    act.wait_ge(pT_done, 8 * i + r + 1)
                    f(pT[r // XT][:, 0:4, (r % XT) * P:(r % XT + 1) * P], PS[:, 4, :].rearrange("p (a b) -> p a b", a=4),
                      ACT.Copy).then_inc(pT_a, 1)

                def take_o(j):
                    act.wait_ge(pv_done, 2 * i + j + 1)
                    f(oT[:, bass.ds(2 * i + j, 1), :].rearrange("p a t -> p (a t)"), PS[:, 6 + j, :], ACT.Copy).then_inc(oT_ready, 1)

                for r in range(2 * XT):
                    if r == 6:
                        take_o(0)
                    if r >= 1:
                        take_pT(r - 1)
                    act.wait_ge(nmax, 8 * i + r + 1)
                    f(prob[:, r % 2, :].rearrange("p (a b) -> p a b", a=2), PS[:, 2 * (r % 2):2 * (r % 2) + 2, 0:SCR], ACT.Exp,
                      bias=stat[:, 64 + r % 2:65 + r % 2], scale=SCALE,
                      accum_out=stat[:, 68 + r % 2:69 + r % 2]).then_inc(exp_done, 1)
                take_pT(2 * XT - 1)
                take_o(1)

            first_then_loop(act, pair, PAIRS)

            def router_part(L):
                for t in range(XT + 2):
                    if t < XT:
                        act.wait_ge(x_new[L], t + 1)
                        own.link(f(PS[:, 2 * (t % 2):2 * (t % 2) + 2, :], xres[L][:, t, :].rearrange("p (a b) -> p a b", a=2), ACT.Square, accum_out=stat[:, t:t + 1]))
                        f(stat[:, 8 + t:9 + t], stat[:, t:t + 1], ACT.Sqrt, bias=eps, scale=1.0 / D).then_inc(x_std[L], 1)
                    if t >= 2:
                        v = t - 2
                        act.wait_ge(lg_neg[L], v + 1)
                        f(probs, PS[:, 6, 0:E], ACT.Exp, bias=stat[:, 16:17], accum_out=stat[:, 17:18]).then_inc(lg_exp[L], 1)

            def experts(L):
                def expert(e):
                    act.wait_ge(gate_mm[L], e + 1)
                    wait(act, hid_ok[L], e)
                    f(silu_a, PS[:, 0, :], ACT.Silu).then_inc(silu_ok[L], 1)
                    act.wait_ge(hid_T[L], e + 1)
                    wait(act, down_mm[L], e)
                    f(hidT, PS[:, 3, :], ACT.Copy).then_inc(hidT_ok[L], 1)

                first_then_loop(act, expert, E)

            act.wait_ge(ada_sum, 2 * UNITS)
            router_part(0)
            act.wait_ge(hf_ready[0], XT)
            act.wait_ge(lg_done[0], XT)
            act.wait_ge(acc_stored[0], 16 * XT)
            act.dma_start(w_conv_out, conv_w_out[0].rearrange("(k p) n -> p k n", p=P)).then_inc(mixw_in[1], 16)
            act.dma_start(w_cb, conv_w_in[0, :, 0:D].rearrange("(k p) n -> p k n", p=P)).then_inc(cb_in, 16)
            experts(0)

            act.wait_ge(mid_in, 16)
            for t in range(XT):
                own.link(f(junk, xres[1][:, t, :], ACT.Square, accum_out=stat[:, t:t + 1]))
            f(stat[:, 8:8 + XT], stat[:, 0:XT], ACT.Sqrt, bias=eps, scale=1.0 / D).then_inc(cn_std, 1)
            for g in range(KC):
                act.wait_ge(cn_T, g + 1)
                f(hT1[:, g, :], PS[:, g % 4, :], ACT.Identity, bias=modv[1][0][:, 0, g, 0:1],
                  scale=scl[1][0][:, g, 0:1]).then_inc(cn_Ta, 1)
            for n in range(KC):
                act.wait_ge(conv_mm, n + 1)
                if n >= 2:
                    act.wait_ge(z_ready, n - 1)
                f(c_sb[:, n % 2, :], PS[:, 3 * (n % 2) + 1, :], ACT.Copy).then_inc(c_copied, 1)
            act.wait_ge(z_ready, KC)
            router_part(1)
            experts(1)

        @block.vector
        def _(dve):
            v = nc.vector
            own = Chain(dve, dve_step)
            v.memset(cond_T, 0.0).then_inc(zeroed, 1)
            v.memset(eps, EPS).then_inc(zeroed, 1)
            dve.wait_ge(ident_in_s, 16)
            v.tensor_reduce(sel2, ident.rearrange("p (a b) -> p b a", a=4)[:, 0:2, :], AX.X, ALU.add).then_inc(zeroed, 1)
            dve.wait_ge(zeroed, 3)
            v.tensor_copy(selx, sel2[:, 0:1].to_broadcast([P, P])).then_inc(sels, 1)
            dve.wait_ge(setup_T, 1)
            v.tensor_copy(cond_T[:, :, 0:2], PS[:, 7, 0:2 * KC].rearrange("p (r k) -> p k r", r=2)).then_inc(setup_out, 1)
            dve.wait_ge(setup_T, 2)
            v.tensor_copy(vec[:, 0:NR], PS[:, 6, 0:NR]).then_inc(setup_out, 1)
            dve.wait_ge(setup_out, 2)
            own.link(v.tensor_tensor(gqk, vec[:, V_GQ:V_GQ + 1], vec[:, V_GK:V_GK + 1], ALU.mult))
            dve.wait_ge(std_in, 1)
            own.link(v.reciprocal(stat[:, 8:8 + NT], stat[:, 8:8 + NT]))
            for j in range(NT):
                v.tensor_scalar(rows_in[:, j, :], rows_in[:, j, :], stat[:, 8 + j:9 + j], None, ALU.mult).then_inc(xn_in, 1)
            dve.wait_ge(misc_in, 16 * 14)

            def col(lo, n, m):
                return vec[:, lo:lo + n].unsqueeze(2).to_broadcast([P, n, m])

            def ada_take(u):
                L, n, half = u // UNITS, (u % UNITS) // 2, u % 2
                dve.wait_ge(ada_sum, u + 1)
                if n == 2:
                    g = gate_mix[L][:, half * BANK:(half + 1) * BANK]
                    v.tensor_tensor(g, PS[:, 7, :], g, ALU.add).then_inc(ada_out, 1)
                elif n == 5:
                    g = gate_ffn[L][64 * half:64 * half + 64, :]
                    v.tensor_tensor(g, PS[64 * half:64 * half + 64, 7, :], g, ALU.add).then_inc(ada_out, 1)
                else:
                    m, kind = n // 3, n % 3
                    v.tensor_tensor(modv[L][m][:, kind, 4 * half:4 * half + 4, :],
                                    PS[:, 7, 0:8].rearrange("p (k r) -> p k r", r=2),
                                    col(V_ADA + 32 * L + 16 * m + KC * kind + 4 * half, 4, 2), ALU.add).then_inc(ada_out, 1)
                    if kind == 1 and half == 1:
                        dve.wait_ge(ada_out, u + 1)
                        v.scalar_tensor_tensor(out=scl[L][m], in0=modv[L][m][:, 1], scalar=1.0,
                                               in1=col((V_NM, V_NF)[m] + KC * L, KC, 2), op0=ALU.add,
                                               op1=ALU.mult).then_inc(mod_ready, 1)

            for u in range(FIRST_UNITS):
                ada_take(u)
            dve.wait_ge(mod_ready, 1)
            for g in range(KC, 12):
                dve.wait_ge(inT, g + 1)
                for q in range(2):
                    k = 2 * (g - KC) + q
                    last = v.tensor_scalar(hT[:, k, 0:CX], PS[:, T_BANKS[g % 5], q * CX:(q + 1) * CX],
                                           scl[0][0][:, k, 1:2], modv[0][0][:, 0, k, 1:2], ALU.mult, ALU.add)
                last.then_inc(inT_d, 1)
            for n, j in enumerate(TILES):
                row = lat[:, n % 2, :]
                if j >= CT:
                    dve.wait_ge(lat_done, n + 1)
                    if n >= 2:
                        dve.wait_ge(latT, n - 1)
                    v.tensor_copy(row[:, BANK:LAT], PS[:, 5, 0:LAT - BANK]).then_inc(lat_d, 1)
                dve.wait_ge(lat_std, n + 1)
                v.tensor_copy(kraw[:, j, :], row[:, QL + KVL:LAT])
                own.link(v.reciprocal(stat[:, 48 + j:49 + j], stat[:, 48 + j:49 + j]))
                last = v.tensor_scalar(row[:, QL:QL + KVL], row[:, QL:QL + KVL], stat[:, 48 + j:49 + j], None, ALU.mult)
                if j >= CT:
                    own.link(v.reciprocal(stat[:, 40 + j:41 + j], stat[:, 40 + j:41 + j]))
                    last = v.tensor_scalar(row[:, 0:QL], row[:, 0:QL], stat[:, 40 + j:41 + j], None, ALU.mult)
                last.then_inc(lat_n, 1)
                for u in units_after(n):
                    if u > FIRST_UNITS:
                        ada_take(u - 1)
                dve.wait_ge(latT, n + 1)
                if j >= CT:
                    v.tensor_tensor(qlT[:, :, (j - CT) * P:(j - CT + 1) * P],
                                    PS[:, 0, 0:QL].rearrange("p (a b) -> p a b", b=P), col(V_QN, QC, P), ALU.mult)
                v.tensor_tensor(kvlT[:, :, j * P:(j + 1) * P], PS[:, 1, 0:KVL].rearrange("p (a b) -> p a b", b=P),
                                col(V_KVN, KVC, P), ALU.mult).then_inc(latT_d, 1)
            ada_take(2 * UNITS - 1)

            dve.wait_ge(latT_d, NT)
            own.link(v.tensor_tensor(krot, kraw, rope_gain[:, 1:2, :].to_broadcast([P, NT, ROPE]), ALU.mult))
            k4 = krot[:, CT:NT, :].rearrange("p t (a b f) -> p t a b f", a=2, b=2)
            k1, k2 = k4[:, :, :, 0, :], k4[:, :, :, 1, :]
            cs = [rope_cs[:, m, :, :].rearrange("p (t h) (a f) -> p t h a f", h=2, a=2)[:, :, 0] for m in range(2)]
            r4 = kraw[:, CT:NT, :].rearrange("p t (a b f) -> p t a b f", a=2, b=2)
            tm = [ktmp[:, m].rearrange("p t (a f) -> p t a f", a=2) for m in range(2)]
            v.tensor_tensor(tm[0], k1, cs[0], ALU.mult)
            own.link(v.tensor_tensor(tm[1], k2, cs[1], ALU.mult))
            own.link(v.tensor_tensor(r4[:, :, :, 0, :], tm[0], tm[1], ALU.subtract))
            v.tensor_tensor(tm[0], k2, cs[0], ALU.mult)
            own.link(v.tensor_tensor(tm[1], k1, cs[1], ALU.mult))
            own.link(v.tensor_tensor(r4[:, :, :, 1, :], tm[0], tm[1], ALU.add))
            v.tensor_copy(krot[:, CT:NT, :], kraw[:, CT:NT, :]).then_inc(krot_ready, 1)
            dve.wait_ge(krot_ready, 1)

            base = own.n
            STEPS_IN_PAIR = 4 + 4 * XT
            def pair(i):
                def take(s):
                    dve.wait_ge(proj, 10 * i + s + 1)
                    dst = kvtok[:, s, :] if s < NT else qtok[:, s - NT, :]
                    v.tensor_copy(dst, PS[:, 7, 0:dst.shape[1]]).then_inc(proj_d, 1)

                own.n = base + STEPS_IN_PAIR * i
                for s in (1, 3, 5):
                    take(s)
                dve.wait_ge(sq_ready, 2 * i + 1)
                own.link(v.tensor_reduce(smal[:, 0:12], sqk, AX.X, ALU.add))
                v.tensor_tensor(smal[:, 0:12].rearrange("p (t h) -> p t h", h=2), smal[:, 0:12].rearrange("p (t h) -> p t h", h=2),
                                stat[:, 32:32 + NT].unsqueeze(2).to_broadcast([P, NT, 2]), ALU.add).then_inc(ss_ready, 1)
                take(7)
                dve.wait_ge(std_ready, 2 * i + 1)
                v.reciprocal(smal[:, 16:28], smal[:, 16:28]).then_inc(rk_ready, 1)
                dve.wait_ge(rk_ready, i + 1)
                kk = kvtok.rearrange("p t (h n) -> p (t h) n", h=2)[:, :, 0:NOPE]
                v.tensor_tensor(kk, kk, smal[:, 16:28].unsqueeze(2).to_broadcast([P, 12, NOPE]), ALU.mult).then_inc(kn_ready, 1)
                take(9)
                dve.wait_ge(sq_ready, 2 * i + 2)
                v.tensor_reduce(smal[:, 32:40], sqq, AX.X, ALU.add).then_inc(ss_ready, 1)
                dve.wait_ge(std_ready, 2 * i + 2)
                own.link(v.reciprocal(smal[:, 40:48], smal[:, 40:48]))
                q8 = qtok.rearrange("p t (h n) -> p (t h) n", h=2)
                own.link(v.tensor_tensor(q8, q8, smal[:, 40:48].unsqueeze(2).to_broadcast([P, 8, QK]), ALU.mult))
                qr = q8[:, :, NOPE:QK]
                v.tensor_tensor(qr, qr, rope_gain[:, 0:1, :].to_broadcast([P, 8, ROPE]), ALU.mult).then_inc(qg_ready, 1)
                dve.wait_ge(qg_ready, i + 1)
                q5 = qr.rearrange("p t (a b f) -> p t a b f", a=2, b=2)
                o5 = q_rot.rearrange("p t (h n) -> p (t h) n", h=2).rearrange("p t (a b f) -> p t a b f", a=2, b=2)
                c8 = [rope_cs[:, m].rearrange("p t (a f) -> p t a f", a=2) for m in range(2)]
                t8 = [rtmp[:, m].rearrange("p (t a f) -> p t a f", a=2, f=RF) for m in range(2)]
                v.tensor_tensor(t8[0], q5[:, :, :, 0, :], c8[0], ALU.mult)
                own.link(v.tensor_tensor(t8[1], q5[:, :, :, 1, :], c8[1], ALU.mult))
                v.tensor_tensor(o5[:, :, :, 0, :], t8[0], t8[1], ALU.subtract).then_inc(qrot_d, 1)
                for g in (1, 3, 5, 7):
                    dve.wait_ge(trn, 8 * i + g + 1)
                    if g == 1:
                        ins = v.tensor_copy(kT[:, 1, 0:BANK], PS[:, 5, :])
                    elif g == 3:
                        ins = v.tensor_copy(kTr[:, 0:BANK], PS[:, 5, :])
                    elif g == 5:
                        ins = v.tensor_scalar(qT[:, 0, :], PS[:, 5, :], gqk, None, ALU.mult)
                    else:
                        ins = v.tensor_copy(qTr, PS[:, 5, :])
                    ins.then_inc(trn_d, 1)

                def norm(r):
                    dve.wait_ge(exp_done, 8 * i + r + 1)
                    own.link(v.reciprocal(stat[:, 70 + r % 2:71 + r % 2], stat[:, 68 + r % 2:69 + r % 2]))
                    v.tensor_scalar(prob[:, r % 2, :], prob[:, r % 2, :], stat[:, 70 + r % 2:71 + r % 2], None,
                                    ALU.mult).then_inc(p_norm, 1)

                def top(r):
                    dve.wait_ge(s_done, 8 * i + r + 1)
                    own.link(v.tensor_reduce(stat[:, 66 + r % 2:67 + r % 2], PS[:, 2 * (r % 2):2 * (r % 2) + 2, 0:SCR], AX.XY, ALU.max))
                    v.tensor_scalar(stat[:, 64 + r % 2:65 + r % 2], stat[:, 66 + r % 2:67 + r % 2], -SCALE, None,
                                    ALU.mult).then_inc(nmax, 1)

                def take_pT(r):
                    dve.wait_ge(pT_done, 8 * i + r + 1)
                    v.tensor_copy(pT[r // XT][:, 4:6, (r % XT) * P:(r % XT + 1) * P],
                                  PS[:, 5, 0:2 * P].rearrange("p (a b) -> p a b", a=2)).then_inc(pT_d, 1)

                for r in range(2 * XT):
                    if r >= 1:
                        norm(r - 1)
                    top(r)
                    if r >= 1:
                        take_pT(r - 1)
                norm(2 * XT - 1)
                take_pT(2 * XT - 1)

            first_then_loop(dve, pair, PAIRS)
            own.n = base + STEPS_IN_PAIR * PAIRS

            def router_part(L):
                A = scl[L][1]
                for t in range(XT + 3):
                    if t < XT:
                        dve.wait_ge(mo_done[L], t + 1)
                        if t >= 1:
                            dve.wait_ge(x_new[L], t)
                        v.tensor_tensor(mo_tmp.rearrange("p (a b) -> p a b", a=2), PS[:, 2 * (t % 2):2 * (t % 2) + 2, :],
                                        gate_mix[L].rearrange("p (a b) -> p a b", a=2), ALU.mult).then_inc(mo_mul[L], 1)
                    if 1 <= t <= XT:
                        w = t - 1
                        dve.wait_ge(xnT[L], w + 1)
                        if w >= 1:
                            dve.wait_ge(hf_ready[L], w)
                        v.tensor_tensor(hf_tmp.rearrange("p (k m) -> p k m", k=KC),
                                        PS[:, 4:6, :].rearrange("p a (k m) -> p (a k) m", k=4),
                                        A[:, :, 0:1].to_broadcast([P, KC, P]), ALU.mult).then_inc(hf_mul[L], 1)
                    if t < XT:
                        dve.wait_ge(x_std[L], t + 1)
                        if t >= 2:
                            dve.wait_ge(xnT[L], t - 1)
                            dve.wait_ge((xn_st0, xn_st1)[t % 2][L], 16 * (t // 2))
                        own.link(v.reciprocal(stat[:, 8 + t:9 + t], stat[:, 8 + t:9 + t]))
                        v.tensor_scalar(xnt[:, t % 2, :], xres[L][:, t, :], stat[:, 8 + t:9 + t], None, ALU.mult).then_inc(xn_ready[L], 1)
                    if 2 <= t <= XT + 1:
                        w = t - 2
                        dve.wait_ge(lg_done[L], w + 1)
                        own.link(v.tensor_reduce(stat[:, 18:19], PS[:, 6, 0:E], AX.X, ALU.max))
                        v.tensor_scalar(stat[:, 16:17], stat[:, 18:19], -1.0, None, ALU.mult).then_inc(lg_neg[L], 1)
                        dve.wait_ge(lg_exp[L], w + 1)
                        own.link(v.reciprocal(stat[:, 19:20], stat[:, 17:18]))
                        v.tensor_scalar(aff[:, w, :], probs, stat[:, 19:20], None, ALU.mult).then_inc(lg_aff[L], 1)
                    if t >= 3:
                        w = t - 3
                        dve.wait_ge(affT_ps[L], w + 1)
                        v.tensor_copy(affT[:, w * P:(w + 1) * P], PS[0:E, 7, 0:P]).then_inc(affT_sb[L], 1)
                dve.wait_ge(affT_sb[L], XT)
                for r in range(CAP // 8):
                    now, nxt = (affT[:, (r + m) % 2 * T:((r + m) % 2 + 1) * T] for m in range(2))
                    best = top_v[L][:, 8 * r:8 * r + 8]
                    own.link(v.max(best, now))
                    v.max_index(top_i[L][:, 8 * r:8 * r + 8], best, now)
                    if r < CAP // 8 - 1:
                        own.link(v.match_replace(nxt, best, now, -1.0))
                    else:
                        own.link(v.tensor_copy(slots_v[L][:, 0:CAP], top_v[L]))
                v.tensor_copy(slots_v[L][:, CAP:P], top_v[L])
                v.tensor_scalar(slots_i[L][:, 0:CAP], top_i[L], 2.0, None, ALU.mult)
                own.link(v.tensor_scalar(slots_i[L][:, CAP:P], top_i[L], 2.0, 1.0, ALU.mult, ALU.add))
                dve.sem_inc(slots_f[L], 1)
                dve.wait_ge(slots_T[L], 1)
                v.tensor_copy(row_no, PS[:, 7, 0:E])
                v.tensor_copy(gate_e, PS[:, 7, E:2 * E]).then_inc(slots_ready[L], 1)

            def experts(L):
                A, B = scl[L][1], modv[L][1]

                def modulate(e, s):
                    dve.wait_ge(xs_T[L], e + 1)
                    a = A[:, :, 0].rearrange("p (h q) -> p q h", h=2).unsqueeze(3).to_broadcast([P, 4, 2, CAP])
                    b = B[:, 0, :, 0].rearrange("p (h q) -> p q h", h=2).unsqueeze(3).to_broadcast([P, 4, 2, CAP])
                    own.link(v.tensor_tensor(xs_m.rearrange("p (q h m) -> p q h m", q=4, h=2),
                                             PS[:, 4, :].rearrange("p (q h m) -> p q h m", q=4, h=2), a, ALU.mult))
                    v.tensor_tensor(xsT[:, s, :].rearrange("p (q h m) -> p q h m", q=4, h=2),
                                    xs_m.rearrange("p (q h m) -> p q h m", q=4, h=2), b, ALU.add).then_inc(xs_mod[L], 1)

                def two_experts(i):
                    own.n = base + 2 * i
                    for s in range(2):
                        e = 2 * i + s
                        dve.wait_ge(silu_ok[L], e + 1)
                        dve.wait_ge(up_mm[L], e + 1)
                        wait(dve, hid_T[L], e)
                        v.tensor_tensor(hid, silu_a, PS[:, 1, :], ALU.mult).then_inc(hid_ok[L], 1)
                        if not (isinstance(e, int) and e == E - 1):
                            modulate(e + 1, 1 - s)
                        dve.wait_ge(down_mm[L], e + 1)
                        wait(dve, scattered[L], 16 * (e - 1))
                        v.scalar_tensor_tensor(out=y_s[:, s, :], in0=PS[:, 2, :], scalar=gate_e[:, bass.ds(e, 1)],
                                               in1=gate_ffn[L], op0=ALU.mult, op1=ALU.mult).then_inc(y_ok[L], 1)

                modulate(0, 0)
                base = own.n
                first_then_loop(dve, two_experts, E // 2, last=1)
                own.n = base + E - 1

            router_part(0)
            experts(0)

            dve.wait_ge(cn_std, 1)
            own.link(v.reciprocal(stat[:, 8:8 + XT], stat[:, 8:8 + XT]))
            for t in range(XT):
                v.tensor_scalar(xnc[:, t, :], xres[1][:, t, :], stat[:, 8 + t:9 + t], None, ALU.mult).then_inc(cn_xn, 1)
            v.memset(u_pad[:, 0:1], 0.0)
            own.link(v.memset(u_pad[:, T + 1:T + 2], 0.0))
            for n in range(KC):
                w3 = [vec[:, V_CONV + m * KC + n:V_CONV + m * KC + n + 1] for m in range(3)]
                dve.wait_ge(conv_mm, n + 1)
                dve.wait_ge(c_copied, n + 1)
                own.link(v.tensor_tensor(u_pad[:, 1:T + 1], PS[:, 3 * (n % 2) + 2, :], c_sb[:, n % 2, :], ALU.mult))
                own.link(v.tensor_scalar(y_sb, u_pad[:, 0:T], w3[0], None, ALU.mult))
                for m in (1, 2):
                    own.link(v.scalar_tensor_tensor(out=y_sb, in0=u_pad[:, m:T + m], scalar=w3[m], in1=y_sb,
                                                    op0=ALU.mult, op1=ALU.add))
                v.tensor_tensor(zT[:, n, :], PS[:, 3 * (n % 2), :], y_sb, ALU.mult).then_inc(z_ready, 1)
            router_part(1)
            experts(1)

        @block.gpsimd
        def _(pool):
            g = nc.gpsimd
            own = Chain(pool, pool_step)
            pool.wait_ge(krot_ready, 1)
            base = 0
            def pair(i):
                own.n = base + i
                pool.wait_ge(rk_ready, i + 1)
                g.tensor_tensor(kr_s.rearrange("p t (h n) -> p t h n", h=2),
                                krot.unsqueeze(2).to_broadcast([P, NT, 2, ROPE]),
                                smal[:, 16:28].rearrange("p (t h) -> p t h", h=2).unsqueeze(3).to_broadcast([P, NT, 2, ROPE]),
                                ALU.mult).then_inc(krs_ready, 1)
                pool.wait_ge(qg_ready, i + 1)
                q5 = qtok.rearrange("p t (h n) -> p (t h) n", h=2)[:, :, NOPE:QK].rearrange("p t (a b f) -> p t a b f", a=2, b=2)
                o5 = q_rot.rearrange("p t (h n) -> p (t h) n", h=2).rearrange("p t (a b f) -> p t a b f", a=2, b=2)
                c8 = [rope_cs[:, m].rearrange("p t (a f) -> p t a f", a=2) for m in range(2)]
                t8 = [rtmp[:, 2 + m].rearrange("p (t a f) -> p t a f", a=2, f=RF) for m in range(2)]
                g.tensor_tensor(t8[0], q5[:, :, :, 1, :], c8[0], ALU.mult)
                own.link(g.tensor_tensor(t8[1], q5[:, :, :, 0, :], c8[1], ALU.mult))
                g.tensor_tensor(o5[:, :, :, 1, :], t8[0], t8[1], ALU.add).then_inc(qrot_p, 1)

            first_then_loop(pool, pair, PAIRS)
            own.n = base + PAIRS

            def router_part(L):
                B = modv[L][1]
                if L == 0:
                    pool.wait_ge(xres_in, 16)
                for t in range(XT + 1):
                    if t < XT:
                        pool.wait_ge(mo_mul[L], t + 1)
                        g.tensor_tensor(xres[L][:, t, :], xres[L][:, t, :], mo_tmp, ALU.add).then_inc(x_new[L], 1)
                    if t >= 1:
                        w = t - 1
                        pool.wait_ge(hf_mul[L], w + 1)
                        if w >= 2:
                            pool.wait_ge(lg_done[L], w - 1)
                        g.tensor_tensor(hfT[:, w % 2, :].rearrange("p (k m) -> p k m", k=KC),
                                        hf_tmp.rearrange("p (k m) -> p k m", k=KC),
                                        B[:, 0, :, 0:1].to_broadcast([P, KC, P]), ALU.add).then_inc(hf_ready[L], 1)

            def experts(L):
                xn_half = xn_dram.rearrange("t (h d) -> (t h) d", h=2)
                acc_half = acc_dram[L].rearrange("t (h d) -> (t h) d", h=2)

                def gather(e, s):
                    g.tensor_copy(row_in[s], row_no[:, bass.ds(e, 1)]).then_inc(row_copied[L], 1)
                    pool.wait_ge(row_copied[L], e + 1)
                    pool.sem_inc(turn, 1)
                    g.indirect_dma_start(out=xs[:, s, :], out_offset=None, in_=xn_half,
                                         in_offset=bass.IndirectOffsetOnAxis(ap=row_in[s], axis=0)
                                         ).then_inc((xs_in0, xs_in1)[s][L], 16)

                def two_experts(i):
                    for s in range(2):
                        e = 2 * i + s
                        if not (isinstance(e, int) and e >= E - 2):
                            pool.wait_ge(xs_T[L], e + 1)
                            gather(e + 2, s)
                        wait(pool, scattered[L], 16 * e)
                        g.tensor_copy(row_out, row_no[:, bass.ds(e, 1)]).then_inc(row_out_ok[L], 1)
                        pool.wait_ge(row_out_ok[L], e + 1)
                        pool.wait_ge(y_ok[L], e + 1)
                        pool.sem_inc(turn, 1)
                        g.indirect_dma_start(out=acc_half, out_offset=bass.IndirectOffsetOnAxis(ap=row_out, axis=0),
                                             in_=y_s[:, s, :], in_offset=None, compute_op=ALU.add).then_inc(scattered[L], 16)

                pool.wait_ge(slots_ready[L], 1)
                pool.wait_ge(acc_stored[L], 16 * XT)
                pool.wait_ge(xn_st0[L], 16 * XT // 2)
                pool.wait_ge(xn_st1[L], 16 * XT // 2)
                gather(0, 0)
                gather(1, 1)
                first_then_loop(pool, two_experts, E // 2, last=1)

            router_part(0)
            experts(0)
            router_part(1)
            experts(1)


_INS = ["x", "c", "ctx", "c_ctx", "norm_mix", "norm_ffn", "ada_w", "ada_b", "mla_w_in", "mla_q_norm", "mla_w_qb",
        "mla_kv_norm", "mla_w_kvb", "mla_q_gain", "mla_k_gain", "mla_w_out", "conv_w_in", "conv_w", "conv_w_out",
        "router_w", "exp_w_gate", "exp_w_up", "exp_w_down"]


def rope_tables(tokens, freqs):
    n = np.arange(tokens)
    pos = np.stack([n // GRID_W, n % GRID_W], axis=-1).astype(np.float32)
    inv = np.float32(ROPE_THETA) ** (-np.arange(freqs, dtype=np.float32) / np.float32(freqs))
    ang = (pos[:, :, None] * inv).astype(np.float32).reshape(tokens, 2 * freqs)
    return np.stack([np.cos(ang), np.sin(ang)]).astype(np.float32)


def kernel(**inputs):
    import concourse.bacc as bacc
    from concourse.bass_utils import run_bass_kernel_spmd

    nc = bacc.Bacc("TRN2", target_bir_lowering=False, num_devices=1)
    host = {name: np.ascontiguousarray(inputs[name]) for name in _INS}
    host["ident"] = np.eye(P, dtype=np.float32)
    host["rope"] = rope_tables(host["x"].shape[1], (host["mla_q_gain"].shape[1] - P) // 4)
    arrays, args = {}, []
    for name, a in host.items():
        arrays[f"in_{name}_dram"] = a
        args.append(nc.dram_tensor(f"in_{name}_dram", a.shape, mybir.dt.from_np(a.dtype), kind="ExternalInput").ap())
    args.append(nc.dram_tensor("out_0_dram", host["x"].shape, F32, kind="ExternalOutput").ap())
    build(nc, *args)
    r = run_bass_kernel_spmd(nc, [arrays], core_ids=[0])
    return r.results[0]["out_0_dram"]
```

```python
from contextlib import ExitStack

import numpy as np

import concourse.bass as bass
from concourse import mybir

F32 = mybir.dt.float32
U32 = mybir.dt.uint32
ALU = mybir.AluOpType
ACT = mybir.ActivationFunctionType
AX = mybir.AxisListType

P = 128
BANK = 512
GRID_W = 64
ROPE_THETA = 10000.0
EPS = 1e-6
EC_CAPACITY = 2


class Chain:

    def __init__(self, eng, sem):
        self.eng, self.sem, self.n = eng, sem, 0

    def link(self, ins):
        self.n = self.n + 1
        ins.then_inc(self.sem, 1)
        self.eng.wait_ge(self.sem, self.n)


def wait(eng, sem, n):
    if not (isinstance(n, int) and n <= 0):
        eng.wait_ge(sem, n)


def first_then_loop(eng, body, n, last=0):
    body(0)
    with eng.Fori(1, n - last) as i:
        body(i)
    for i in range(n - last, n):
        body(i)


def build(nc, x, c, ctx, c_ctx, norm_mix, norm_ffn, ada_w, ada_b, mla_w_in, mla_q_norm, mla_w_qb,
          mla_kv_norm, mla_w_kvb, mla_q_gain, mla_k_gain, mla_w_out, conv_w_in, conv_w, conv_w_out,
          router_w, exp_w_gate, exp_w_up, exp_w_down, ident_in, rope_in, out):
    _, T, D = x.shape
    CX = ctx.shape[1]
    KEYS = CX + T
    KC = D // P
    XT, CT = T // P, CX // P
    NT = XT + CT
    QL, KVL = mla_q_norm.shape[1], mla_kv_norm.shape[1]
    QC, KVC = QL // P, KVL // P
    QK = mla_q_gain.shape[1]
    NOPE = P
    ROPE = QK - NOPE
    RF = ROPE // 4
    HEADS = mla_w_qb.shape[2] // QK
    PAIRS = HEADS // 2
    LAT = mla_w_in.shape[2]
    VD = mla_w_kvb.shape[2] // HEADS - NOPE
    E, FF = exp_w_gate.shape[1], exp_w_gate.shape[3]
    CAP = EC_CAPACITY * T // E
    SCALE = float(QK) ** -0.5
    HALF = D // 2
    SCR = KEYS // 2
    UNITS = 6 * D // BANK
    FIRST_UNITS = 4
    assert VD == P and D == FF == 2 * BANK and T == BANK and CAP * 2 == P and D == KC * P and LAT == QL + KVL + ROPE

    es = ExitStack()
    with es:
        def sb(name, cols, dt=F32, rows=P):
            return es.enter_context(nc.sbuf_tensor(name, [rows, cols], dt))[:, :]

        def sem(name):
            return es.enter_context(nc.semaphore(name))

        R = [sb(f"ring{n}", KC * FF) for n in range(3)]
        W = sb("work", 22528)
        PS = es.enter_context(nc.psum_tensor("ps", [P, 8, BANK], F32))

        def view(t, lo, *dims):
            n = int(np.prod(dims))
            v = t[:, lo:lo + n]
            if len(dims) == 2:
                v = v.rearrange("p (a b) -> p a b", b=dims[1])
            if len(dims) == 3:
                v = v.rearrange("p (a b c) -> p a b c", b=dims[1], c=dims[2])
            return v

        ident = sb("ident", P)
        cond_rows, vec_rows = W[:, 20736:20736 + P], W[:, 20864:20864 + P]
        vec = sb("vec", P)
        NR = 127
        V_NM, V_NF, V_ADA, V_QN, V_KVN, V_GQ, V_GK, V_CONV = 0, 16, 32, 96, 99, 101, 102, 103
        cond_T = view(sb("cond_T", KC * 32), 0, KC, 32)
        sel2 = sb("sel2", 2)
        selx = sb("selx", P)
        eps = sb("eps", 1)
        ada_part = view(sb("ada_part", 2 * BANK), 0, 2, BANK)
        junk = ada_part.rearrange("p a b -> p (a b)")
        modv = [[view(sb(f"mod{L}{n}", 2 * KC * 2), 0, 2, KC, 2) for n in "mf"] for L in range(2)]
        scl = [[view(sb(f"scl{L}{n}", KC * 2), 0, KC, 2) for n in "mf"] for L in range(2)]
        gate_mix = [sb(f"gate_mix{L}", D) for L in range(2)]
        gate_ffn = [sb(f"gate_ffn{L}", HALF) for L in range(2)]
        router = [view(sb(f"router{L}", KC * E), 0, KC, E) for L in range(2)]
        rope_cs = view(sb("rope_cs", 2 * XT * 2 * 2 * RF), 0, 2, XT * 2, 2 * RF)
        rope_gain = view(W, 22272, 2, ROPE)
        gqk = sb("gqk", 1)
        stat = sb("stat", 96)
        smal = sb("smal", 64)
        probs = sb("probs", E)
        aff = view(sb("aff", XT * E), 0, XT, E)
        affT = junk[0:E, :]
        at = 18944
        top_v = W[0:E, at:at + CAP]
        top_i = W[0:E, at + CAP:at + 2 * CAP].bitcast(U32)
        slots_i = W[0:E, at + P:at + 2 * P]
        slots_v = W[0:E, at + 2 * P:at + 3 * P]
        row_no = sb("row_no", E, U32)
        gate_e = sb("gate_e", E)
        row_in = [sb(f"row_in{s}", 1, U32) for s in range(2)]
        row_out = sb("row_out", 1, U32)

        xn_dram = nc.dram_tensor("xn_rows", (T, D), F32, kind="Internal").ap()
        mid_dram = nc.dram_tensor("mid_rows", (T, D), F32, kind="Internal").ap()
        parts_dram = [nc.dram_tensor(f"ada_parts{L}", (UNITS, P, BANK), F32, kind="Internal").ap() for L in range(2)]
        out_rows = out.rearrange("a t d -> (a t) d")
        acc_dram = [mid_dram, out_rows]

        w_qb = view(W, 0, QC, HEADS * QK)
        w_kvb = view(W, 4608, KVC, HEADS * (NOPE + VD))
        qlT = view(W, 8704, QC, T)
        kvlT = view(W, 10240, KVC, KEYS)
        krot = view(W, 11776, NT, ROPE)
        rows_in = view(W, 12288, NT, D)
        lat = view(W, 18432, 2, LAT)
        kraw = view(W, 19840, NT, ROPE)
        ktmp = view(W, 20224, 2, XT, 2 * RF)
        kvtok = view(W, 12288, NT, 2 * (NOPE + VD))
        qtok = view(W, 15360, XT, 2 * QK)
        qT = view(W, 16896, 2, T)
        qTr = view(W, 17920, T)
        kT = view(W, 18432, 2, KEYS)
        kTr = view(W, 19968, KEYS)
        prob = view(W, 20736, 2, KEYS)
        w_in = view(R[2], 0, KC, LAT)
        hT = view(R[1], 0, KC, KEYS)
        junk_in = view(R[1], 6144, D)
        pT = [view(R[0], j * 3072, NT, T) for j in range(2)]
        sqq = view(R[0], 6144, XT * 2, QK)
        oT = view(R[1], 0, HEADS, T)
        sqk = view(R[1], 4096, NT * 2, NOPE)
        kr_s = view(R[1], 5632, NT, 2 * ROPE)
        q_rot = view(R[1], 6400, XT, 2 * ROPE)
        rtmp = view(R[1], 6912, 4, XT * 2 * 2 * RF)
        mla_out = [view(R[2], h * KC * BANK, KC, BANK) for h in range(2)]
        ada_buf = mla_out[1]
        parts_sb = [view(W, 0, UNITS - FIRST_UNITS, BANK), view(W, 0, UNITS, BANK)]
        w_conv_out = view(W, 0, KC, D)
        w_cb = view(W, 8192, KC, D)
        w_cc = view(R[1], 0, KC, D)
        w_cv = view(R[2], 0, KC, D)
        hT1 = view(R[0], 0, KC, T)
        xnc = view(W, 16384, XT, D)
        zT = view(W, 16384, KC, T)
        c_sb = view(W, 20480, 2, T)
        u_pad = view(W, 21504, T + 2)
        y_sb = ada_part[:, 0, :]
        w_out = [mla_out, [w_conv_out[:, :, h * BANK:(h + 1) * BANK] for h in range(2)]]
        mixT = [oT, zT]
        xres = [view(W, 12288, XT, D), view(R[0], 4096, XT, D)]
        hfT = view(W, 8192, 2, KC * P)
        mo_tmp = view(W, 10240, D)
        hf_tmp = view(W, 11264, D)
        xnt = view(W, 20480, 2, D)
        xs = view(W, 16384, 2, HALF)
        xs_m = view(W, 17408, HALF)
        xsT = view(W, 17920, 2, HALF)
        silu_a = view(W, 18944, BANK)
        hid = view(W, 19456, BANK)
        hidT = view(W, 19968, BANK)
        y_s = view(W, 20480, 2, BANK)
        wg, wu, wd = (view(r, 0, KC, FF) for r in R)
        wg1, wu1 = view(W, 0, KC, FF), view(W, 8192, KC, FF)

        cond_in, vec_in, misc_in = sem("cond_in"), sem("vec_in"), sem("misc_in")
        rows_in_s = [sem("ctx_in"), sem("x_in")]
        win_in, whead_in = sem("win_in"), sem("whead_in")
        mixw_in = [sem("mla_out_in"), sem("conv_out_in")]
        cb_in, xres_in = sem("cb_in"), sem("xres_in")
        cc_in, cv_in = ([sem(f"{n}_in{h}") for h in range(2)] for n in ("cc", "cv"))
        wg1_in, wu1_in = sem("wg1_in"), sem("wu1_in")
        silu_c, zeroed, setup_T, setup_out, sels = (sem(n) for n in ("silu_c", "zeroed", "setup_T", "setup_out", "sels"))
        sq_in, std_in, xn_in, inT, inT_a, inT_d = (sem(n) for n in ("sq_in", "std_in", "xn_in", "inT", "inT_a", "inT_d"))
        ada_in = [sem("ada_in0"), sem("ada_in1")]
        unit_in, unit_mm, unit_copied, parts_in, out_half_in = (sem(n) for n in (
            "unit_in", "unit_mm", "unit_copied", "parts_in", "out_half_in"))
        unit_stored = [sem("unit_stored0"), sem("unit_stored1")]
        ada_main, ada_rows, ada_sum, ada_out, mod_ready = (sem(n) for n in (
            "ada_main", "ada_rows", "ada_sum", "ada_out", "mod_ready"))
        lat_done, lat_a, lat_d, lat_std, lat_n, latT, latT_d, krot_ready = (sem(n) for n in (
            "lat_done", "lat_a", "lat_d", "lat_std", "lat_n", "latT", "latT_d", "krot_ready"))
        proj, proj_a, proj_d, sq_ready, ss_ready, std_ready, rk_ready, kn_ready, krs_ready = (sem(n) for n in (
            "proj", "proj_a", "proj_d", "sq_ready", "ss_ready", "std_ready", "rk_ready", "kn_ready", "krs_ready"))
        qg_ready, qrot_d, qrot_p, trn, trn_a, trn_d = (sem(n) for n in (
            "qg_ready", "qrot_d", "qrot_p", "trn", "trn_a", "trn_d"))
        s_done, nmax, exp_done, p_norm, pT_done, pT_a, pT_d, pv_done, oT_ready = (sem(n) for n in (
            "s_done", "nmax", "exp_done", "p_norm", "pT_done", "pT_a", "pT_d", "pv_done", "oT_ready"))
        dve_step, act_step, pool_step, turn = sem("dve_step"), sem("act_step"), sem("pool_step"), sem("turn")
        conv_mm, c_copied, z_ready = (sem(n) for n in ("conv_mm", "c_copied", "z_ready"))

        def layer_sems(*names):
            return [[sem(f"{n}{L}") for L in range(2)] for n in names]

        (mo_done, mo_mul, x_new, x_std, xn_ready, xnT, hf_mul, hf_ready, lg_done, lg_neg, lg_exp, lg_aff,
         affT_ps, affT_sb) = layer_sems("mo_done", "mo_mul", "x_new", "x_std", "xn_ready", "xnT", "hf_mul",
                                        "hf_ready", "lg_done", "lg_neg", "lg_exp", "lg_aff", "affT_ps", "affT_sb")
        acc_stored, xn_st0, xn_st1, slots_f, slots_T, slots_ready = layer_sems(
            "acc_stored", "xn_st0_", "xn_st1_", "slots_f", "slots_T", "slots_ready")
        (wg_in, wu_in, wd_in, row_copied, row_out_ok, xs_in0, xs_in1, xs_T, xs_mod, gate_mm, up_mm, silu_ok, hid_ok, hid_T, hidT_ok,
         down_mm, y_ok, scattered) = layer_sems(
            "wg_in", "wu_in", "wd_in", "row_copied", "row_out_ok", "xs_in0_", "xs_in1_", "xs_T", "xs_mod", "gate_mm", "up_mm",
            "silu_ok", "hid_ok", "hid_T", "hidT_ok", "down_mm", "y_ok", "scattered")

        TILES = [CT + t for t in range(XT)] + list(range(CT))
        PARTS = 4
        U0, U1 = (UNITS - FIRST_UNITS) // PAIRS, UNITS // PAIRS
        UP = U0 + U1
        T_BANKS = [0, 1, 3, 4, 5]
        ADA_BANKS = [2, 6]

        PAIR_BANKS = [0, 2, 7, 7, 7]
        BEHIND = {1: 2, 4: 3, 7: 4}
        assert UP == len(PAIR_BANKS)

        def unit_of(i, q):
            return (0, FIRST_UNITS + U0 * i + q) if q < U0 else (1, U1 * i + q - U0)

        LATER = [(0, n) for n in range(FIRST_UNITS, UNITS)] + [(1, n) for n in range(UNITS)]

        def later_units(L):
            return range(FIRST_UNITS, UNITS) if L == 0 else range(UNITS, 2 * UNITS)

        def collect_bank(g):
            return 7 if g < FIRST_UNITS else 6 + g % 2

        block = es.enter_context(nc.Block())

        @block.sync
        def _(sp):
            def load_ada(u):
                L, n = u // UNITS, u % UNITS
                if u >= 2:
                    sp.wait_ge(ada_main, u - 1)
                sp.dma_start(view(R[0], (u % 2) * 4096, KC, BANK),
                             ada_w[L, :, n * BANK:(n + 1) * BANK].rearrange("(k p) n -> p k n", p=P)
                             ).then_inc(ada_in[u % 2], 16)

            sp.dma_start(rows_in[:, 0:CT, :], ctx[0].rearrange("(t p) d -> p t d", p=P)).then_inc(rows_in_s[0], 16)
            sp.dma_start(rows_in[:, CT:NT, :], x[0].rearrange("(t p) d -> p t d", p=P)).then_inc(rows_in_s[1], 16)
            for u in range(FIRST_UNITS):
                load_ada(u)
            sp.dma_start(w_in, mla_w_in[0].rearrange("(k p) n -> p k n", p=P)).then_inc(win_in, 16)
            sp.dma_start(w_kvb, mla_w_kvb[0].rearrange("(k p) n -> p k n", p=P)).then_inc(whead_in, 16)
            sp.dma_start(w_qb, mla_w_qb[0].rearrange("(k p) n -> p k n", p=P)).then_inc(whead_in, 16)
            sp.wait_ge(lat_done, NT)
            sp.dma_start(mla_out[0], mla_w_out[0, :, 0:BANK].rearrange("(k p) n -> p k n", p=P)).then_inc(mixw_in[0], 16)

            def store_unit(i, q):
                L, n = unit_of(i, q)
                sp.wait_ge(unit_copied, UP * i + q + 1)
                sp.dma_start(parts_dram[L][n], ada_part[:, q % 2, :]).then_inc(unit_stored[q % 2], 16)

            def pair_units(i):
                for q in range(UP):
                    wait(sp, unit_mm, UP * i + q)
                    L, n = unit_of(i, q)
                    sp.dma_start(ada_buf, ada_w[L, :, bass.ds(n * BANK, BANK)].rearrange("(k p) n -> p k n", p=P)
                                 ).then_inc(unit_in, 16)
                    if q >= 1:
                        store_unit(i, q - 1)
                    elif not isinstance(i, int):
                        store_unit(i - 1, UP - 1)

            first_then_loop(sp, pair_units, PAIRS)
            store_unit(PAIRS - 1, UP - 1)
            sp.wait_ge(unit_mm, UP * PAIRS)
            sp.dma_start(mla_out[1], mla_w_out[0, :, BANK:D].rearrange("(k p) n -> p k n", p=P)).then_inc(out_half_in, 16)
            sp.wait_ge(unit_stored[0], 16 * 3 * PAIRS)
            sp.wait_ge(unit_stored[1], 16 * 2 * PAIRS)

            def load_parts(L, n0):
                sp.dma_start(parts_sb[L], parts_dram[L][n0:UNITS].rearrange("n p c -> p n c")).then_inc(parts_in, 16)

            sp.wait_ge(proj, 10 * PAIRS)
            load_parts(0, FIRST_UNITS)

            def load_expert(w, dst, L, e, done):
                for k in range(0, KC, KC // PARTS):
                    sp.dma_start(dst[:, k:k + KC // PARTS, :],
                                 w[L, e][k * P:(k + KC // PARTS) * P, :].rearrange("(k p) n -> p k n", p=P)).then_inc(done, 16)

            def stores(L):
                for t in range(XT):
                    if L == 0 and t == XT // 2:
                        sp.wait_ge(ada_sum, 2 * UNITS)
                        load_expert(exp_w_gate, wg1, 0, 1, wg1_in)
                    if L == 1 and t == XT - 1:
                        sp.wait_ge(mo_done[1], XT)
                        load_expert(exp_w_gate, wg1, 1, 1, wg1_in)
                    sp.wait_ge(x_new[L], t + 1)
                    sp.dma_start(acc_dram[L][t * P:(t + 1) * P, :], xres[L][:, t, :]).then_inc(acc_stored[L], 16)
                    sp.wait_ge(xn_ready[L], t + 1)
                    sp.dma_start(xn_dram[t * P:(t + 1) * P, :], xnt[:, t % 2, :]).then_inc((xn_st0, xn_st1)[t % 2][L], 16)

            def expert_stream(L):
                sp.wait_ge(xs_in0[L], 16)
                load_expert(exp_w_up, wu1, L, 1, wu1_in)
                sp.wait_ge(gate_mm[L], 1)
                load_expert(exp_w_gate, wg, L, 2, wg_in[L])
                sp.wait_ge(up_mm[L], 1)
                load_expert(exp_w_up, wu, L, 2, wu_in[L])
                for e in (1, 2):
                    sp.wait_ge(down_mm[L], e)
                    load_expert(exp_w_down, wd, L, e, wd_in[L])
                with sp.Fori(3, E) as e:
                    sp.wait_ge(gate_mm[L], e)
                    load_expert(exp_w_gate, wg, L, e, wg_in[L])
                    sp.wait_ge(up_mm[L], e)
                    load_expert(exp_w_up, wu, L, e, wu_in[L])
                    sp.wait_ge(down_mm[L], e)
                    load_expert(exp_w_down, wd, L, e, wd_in[L])

            sp.wait_ge(pv_done, HEADS)
            sp.wait_ge(oT_ready, HEADS)
            sp.dma_start(xres[0], x[0].rearrange("(t p) d -> p t d", p=P)).then_inc(xres_in, 16)
            load_expert(exp_w_gate, wg, 0, 0, wg_in[0])
            sp.wait_ge(ada_sum, UNITS)
            load_parts(1, 0)
            stores(0)
            sp.wait_ge(mo_done[0], XT)
            load_expert(exp_w_up, wu, 0, 0, wu_in[0])
            load_expert(exp_w_down, wd, 0, 0, wd_in[0])
            expert_stream(0)

            def load_conv(w, dst, m, h, done):
                sp.dma_start(dst[:, :, h * HALF:(h + 1) * HALF],
                             w[0, :, m * D + h * HALF:m * D + (h + 1) * HALF].rearrange("(k p) n -> p k n", p=P)
                             ).then_inc(done, 16)

            for h in range(2):
                load_conv(conv_w_in, w_cb, 0, h, cb_in)
            sp.wait_ge(up_mm[0], E)
            sp.wait_ge(scattered[0], 16 * E)
            sp.dma_start(xres[1], mid_dram.rearrange("(t p) d -> p t d", p=P)).then_inc(xres_in, 16)
            for h in range(2):
                load_conv(conv_w_in, w_cc, 1, h, cc_in[h])
                load_conv(conv_w_in, w_cv, 2, h, cv_in[h])
            sp.dma_start(w_conv_out, conv_w_out[0].rearrange("(k p) n -> p k n", p=P)).then_inc(mixw_in[1], 16)
            sp.wait_ge(conv_mm, KC)
            load_expert(exp_w_up, wu, 1, 0, wu_in[1])
            load_expert(exp_w_down, wd, 1, 0, wd_in[1])
            stores(1)
            sp.wait_ge(acc_stored[1], 16 * XT)
            load_expert(exp_w_gate, wg, 1, 0, wg_in[1])
            expert_stream(1)
            sp.wait_ge(scattered[1], 16 * E)

        @block.tensor
        def _(pe):
            mm, tr = nc.tensor.matmul, nc.tensor.transpose

            def ada_product(u):
                b = ADA_BANKS[u % 2]
                pe.wait_ge(ada_in[u % 2], 16 * (u // 2 + 1))
                if u >= 2:
                    pe.wait_ge(ada_rows, u - 1)
                wv = view(R[0], (u % 2) * 4096, KC, BANK)
                for kk in range(2):
                    for g in range(4):
                        k = 2 * g + kk
                        last = mm(PS[32 * g:32 * g + 32, b, :], cond_T[:, k, :], wv[:, k, :], start=kk == 0, stop=kk == 1)
                last.then_inc(ada_main, 1)

            def ada_collect(g):
                L, n = (0, g) if g < FIRST_UNITS else LATER[g - FIRST_UNITS]
                kind, half, b = n // 2, n % 2, collect_bank(g)
                if g < FIRST_UNITS:
                    pe.wait_ge(ada_rows, g + 1)
                    part = ada_part[:, g % 2, :]
                    if g >= 1:
                        pe.wait_ge(ada_out, g)
                else:
                    pe.wait_ge(parts_in, 16 * (L + 1))
                    part = parts_sb[L][:, n - (0 if L else FIRST_UNITS), :]
                    pe.wait_ge(ada_out, g - 1)
                if kind == 2:
                    last = mm(PS[:, b, :], selx, part, start=True, stop=True)
                elif kind == 5:
                    last = mm(PS[64 * half:64 * half + 64, b, :], selx[:, 0:64], part, start=True, stop=True)
                else:
                    for q in range(4):
                        last = mm(PS[:, b, 2 * q:2 * q + 2], part[:, q * P:(q + 1) * P], sel2, start=True, stop=True)
                last.then_inc(ada_sum, 1)

            pe.wait_ge(cond_in, 48)
            pe.wait_ge(silu_c, 1)
            tr(PS[:, 7, 0:2 * KC], cond_rows[0:2 * KC, :], ident[0:2 * KC, 0:2 * KC]).then_inc(setup_T, 1)
            pe.wait_ge(vec_in, 16 * 12)
            tr(PS[:, 6, 0:NR], vec_rows[0:NR, :], ident[0:NR, 0:NR]).then_inc(setup_T, 1)

            def input_T(g):
                b = T_BANKS[g % 5]
                if g >= 5:
                    pe.wait_ge(inT_a, g - 4)
                for q in range(4):
                    k, t = (g, CT + q) if g < KC else (2 * (g - KC) + q // 2, q % 2)
                    last = tr(PS[:, b, q * P:(q + 1) * P], rows_in[:, t, k * P:(k + 1) * P], ident)
                last.then_inc(inT, 1)

            pe.wait_ge(setup_out, 2)
            pe.wait_ge(sels, 1)
            ada_product(0)
            ada_product(1)
            pe.wait_ge(xn_in, NT)
            for g in range(5):
                input_T(g)
            for u in range(2, FIRST_UNITS):
                ada_collect(u - 2)
                ada_product(u)
            for u in range(FIRST_UNITS - 2, FIRST_UNITS):
                ada_collect(u)
            for g in range(5, 12):
                input_T(g)

            pe.wait_ge(win_in, 16)
            pe.wait_ge(inT_a, KC)
            pe.wait_ge(inT_d, 4)
            for n, j in enumerate(TILES):
                if n >= 1:
                    pe.wait_ge(lat_a, n)
                    pe.wait_ge(lat_d, min(n, XT))
                cuts = [(4, 0, BANK), (5, BANK, LAT)] if j >= CT else [(4, QL, LAT)]
                for b, lo, hi in cuts:
                    for k in range(KC):
                        last = mm(PS[:, b, 0:hi - lo], hT[:, k, j * P:(j + 1) * P], w_in[:, k, lo:hi],
                                  start=k == 0, stop=k == KC - 1)
                last.then_inc(lat_done, 1)
                pe.wait_ge(lat_n, n + 1)
                if n >= 1:
                    pe.wait_ge(latT_d, n)
                if j >= CT:
                    for q in range(QC):
                        tr(PS[:, 0, q * P:(q + 1) * P], lat[:, n % 2, q * P:(q + 1) * P], ident)
                for q in range(KVC):
                    last = tr(PS[:, 1, q * P:(q + 1) * P], lat[:, n % 2, QL + q * P:QL + (q + 1) * P], ident)
                last.then_inc(latT, 1)

            pe.wait_ge(latT_d, NT)
            pe.wait_ge(krot_ready, 1)
            pe.wait_ge(whead_in, 32)
            pe.wait_ge(ada_rows, FIRST_UNITS)
            pe.wait_ge(ada_out, FIRST_UNITS)
            def pair(i):
                def unit(q):
                    pe.wait_ge(unit_in, 16 * (UP * i + q + 1))
                    if q >= 3:
                        pe.wait_ge(unit_copied, UP * i + q)
                    for kk in range(2):
                        for g in range(4):
                            k = 2 * g + kk
                            last = mm(PS[32 * g:32 * g + 32, PAIR_BANKS[q], :], cond_T[:, k, :], ada_buf[:, k, :],
                                      start=kk == 0, stop=kk == 1)
                    last.then_inc(unit_mm, 1)

                for s in range(NT + XT):
                    if s == 5:
                        unit(0)
                    b = 6 + s % 2
                    if s < 2:
                        wait(pe, oT_ready, 2 * i)
                    elif s % 2 == 0:
                        pe.wait_ge(proj_a, 5 * i + s // 2)
                    else:
                        pe.wait_ge(proj_d, 5 * i + s // 2)
                    if s < NT:
                        for q in range(KVC):
                            last = mm(PS[:, b, :], kvlT[:, q, s * P:(s + 1) * P],
                                      w_kvb[:, q, bass.ds(i * BANK, BANK)], start=q == 0, stop=q == KVC - 1)
                    else:
                        for q in range(QC):
                            last = mm(PS[:, b, 0:2 * QK], qlT[:, q, (s - NT) * P:(s - NT + 1) * P],
                                      w_qb[:, q, bass.ds(i * 2 * QK, 2 * QK)], start=q == 0, stop=q == QC - 1)
                    last.then_inc(proj, 1)
                groups = ([[(kvtok[:, t, 0:P]) for t in range(4)]]
                          + [[kvtok[:, t, 256:256 + P] for t in range(4)]]
                          + [[kvtok[:, 4 + q % 2, 256 * (q // 2):256 * (q // 2) + P] for q in range(4)]]
                          + [[kr_s[:, t, :] for t in range(4)]]
                          + [[kr_s[:, t, :] for t in range(4, 6)]]
                          + [[qtok[:, t, h * QK:h * QK + P] for t in range(XT)] for h in range(2)]
                          + [[q_rot[:, t, :] for t in range(XT)]])
                for g, srcs in enumerate(groups):
                    if g == 0:
                        pe.wait_ge(kn_ready, i + 1)
                    if g == 3:
                        pe.wait_ge(krs_ready, i + 1)
                    if g == 5:
                        unit(1)
                        pe.wait_ge(qg_ready, i + 1)
                    if g == 7:
                        pe.wait_ge(qrot_d, i + 1)
                        pe.wait_ge(qrot_p, i + 1)
                    if g >= 2:
                        pe.wait_ge((trn_a, trn_d)[g % 2], 4 * i + g // 2)
                    for q, src in enumerate(srcs):
                        last = tr(PS[:, 4 + g % 2, q * P:(q + 1) * P], src, ident)
                    last.then_inc(trn, 1)

                def scores(r):
                    j, t = r // XT, r % XT
                    if r == 0:
                        pe.wait_ge(trn_a, 4 * i + 4)
                        pe.wait_ge(trn_d, 4 * i + 4)
                    if r >= 2:
                        pe.wait_ge(exp_done, 8 * i + r - 1)
                    else:
                        pe.wait_ge(unit_copied, UP * i + r + 1)
                    for h in range(2):
                        o = PS[:, 2 * (r % 2) + h, 0:SCR]
                        mm(o, qT[:, j, t * P:(t + 1) * P], kT[:, j, h * SCR:(h + 1) * SCR], start=True, stop=False)
                        last = mm(o, qTr[64 * j:64 * j + 64, t * P:(t + 1) * P],
                                  kTr[64 * j:64 * j + 64, h * SCR:(h + 1) * SCR], start=False, stop=True)
                    last.then_inc(s_done, 1)

                def probs_T(r):
                    pe.wait_ge(p_norm, 8 * i + r + 1)
                    wait(pe, pT_a, 8 * i + r)
                    wait(pe, pT_d, 8 * i + r)
                    for q in range(NT):
                        last = tr(PS[:, 4 + q // 4, (q % 4) * P:(q % 4 + 1) * P], prob[:, r % 2, q * P:(q + 1) * P], ident)
                    last.then_inc(pT_done, 1)

                def values(j):
                    if j == 1:
                        pe.wait_ge(unit_copied, UP * i + UP)
                    pe.wait_ge(pT_a, 8 * i + 4 * j + 4)
                    pe.wait_ge(pT_d, 8 * i + 4 * j + 4)
                    for q in range(NT):
                        last = mm(PS[:, 6 + j, :], kvtok[:, q, 256 * j + NOPE:256 * j + NOPE + VD], pT[j][:, q, :],
                                  start=q == 0, stop=q == NT - 1)
                    last.then_inc(pv_done, 1)

                for r in range(2 * XT):
                    scores(r)
                    if r >= 1:
                        probs_T(r - 1)
                    if r in BEHIND:
                        unit(BEHIND[r])
                    if r == 5:
                        values(0)
                probs_T(2 * XT - 1)
                values(1)

            first_then_loop(pe, pair, PAIRS)

            def mixer_out(L):
                pe.wait_ge(mixw_in[L], 16)
                if L == 0:
                    pe.wait_ge(oT_ready, HEADS)
                else:
                    pe.wait_ge(z_ready, KC)
                for t in range(XT + 3):
                    if t < XT:
                        if t >= 2:
                            pe.wait_ge(x_std[L], t - 1)
                        for h in range(2):
                            if L == 0 and t == 0 and h == 1:
                                pe.wait_ge(out_half_in, 16)
                            for k in range(KC):
                                last = mm(PS[:, 2 * (t % 2) + h, :], mixT[L][:, k, t * P:(t + 1) * P],
                                          w_out[L][h][:, k, :], start=k == 0, stop=k == KC - 1)
                        last.then_inc(mo_done[L], 1)
                    if L == 0 and t < 2:
                        for g in later_units(t):
                            ada_collect(g)
                    if 1 <= t <= XT:
                        v = t - 1
                        pe.wait_ge(xn_ready[L], v + 1)
                        pe.wait_ge(hf_mul[L], v)
                        for k in range(KC):
                            last = tr(PS[:, 4 + k // 4, (k % 4) * P:(k % 4 + 1) * P], xnt[:, v % 2, k * P:(k + 1) * P], ident)
                        last.then_inc(xnT[L], 1)
                    if 2 <= t <= XT + 1:
                        v = t - 2
                        pe.wait_ge(hf_ready[L], v + 1)
                        pe.wait_ge(lg_exp[L], v)
                        for k in range(KC):
                            last = mm(PS[:, 6, 0:E], hfT[:, v % 2, k * P:(k + 1) * P], router[L][:, k, :],
                                      start=k == 0, stop=k == KC - 1)
                        last.then_inc(lg_done[L], 1)
                    if 3 <= t:
                        v = t - 3
                        pe.wait_ge(lg_aff[L], v + 1)
                        pe.wait_ge(affT_sb[L], v)
                        tr(PS[0:E, 7, 0:P], aff[:, v, :], ident).then_inc(affT_ps[L], 1)
                pe.wait_ge(slots_f[L], 1)
                tr(PS[:, 7, 0:E], slots_i, ident[0:E, 0:E])
                tr(PS[:, 7, E:2 * E], slots_v, ident[0:E, 0:E]).then_inc(slots_T[L], 1)

            def experts(L):
                def rows_T(i, s):
                    pe.wait_ge((xs_in0, xs_in1)[s][L], 16 * i + 16)
                    wait(pe, xs_mod[L], 2 * i + s)
                    for q in range(4):
                        last = tr(PS[:, 4, q * P:(q + 1) * P], xs[:, s, q * P:(q + 1) * P], ident)
                    last.then_inc(xs_T[L], 1)

                def halves(bank, lhsT, w, done):
                    for k in range(KC):
                        lhs = lhsT[:, (k % 4) * P + 64 * (k // 4):(k % 4) * P + 64 * (k // 4) + 64]
                        for h in range(2):
                            last = mm(PS[64 * h:64 * h + 64, bank, :], lhs, w[:, k, h * BANK:(h + 1) * BANK],
                                      start=k == 0, stop=k == KC - 1)
                    last.then_inc(done, 1)

                def ring_loads(e):
                    return 1 if isinstance(e, int) and e == 0 else e

                def two_experts(i):
                    for s in range(2):
                        e = 2 * i + s
                        pe.wait_ge(xs_mod[L], e + 1)
                        ahead = isinstance(e, int) and e == 1
                        if ahead:
                            pe.wait_ge(wg1_in, 16 * PARTS * (L + 1))
                        else:
                            pe.wait_ge(wg_in[L], 16 * PARTS * ring_loads(e))
                        wait(pe, silu_ok[L], e)
                        halves(0, xsT[:, s, :], wg1 if ahead else wg, gate_mm[L])
                        if ahead:
                            pe.wait_ge(wu1_in, 16 * PARTS * (L + 1))
                        else:
                            pe.wait_ge(wu_in[L], 16 * PARTS * ring_loads(e))
                        wait(pe, hid_ok[L], e)
                        halves(1, xsT[:, s, :], wu1 if ahead else wu, up_mm[L])
                        if not (isinstance(e, int) and e == E - 1):
                            rows_T(i + s, 1 - s)
                        pe.wait_ge(hid_ok[L], e + 1)
                        wait(pe, hidT_ok[L], e)
                        for q in range(4):
                            last = tr(PS[:, 3, q * P:(q + 1) * P], hid[:, q * P:(q + 1) * P], ident)
                        last.then_inc(hid_T[L], 1)
                        pe.wait_ge(wd_in[L], 16 * PARTS * (e + 1))
                        pe.wait_ge(hidT_ok[L], e + 1)
                        wait(pe, y_ok[L], e)
                        halves(2, hidT, wd, down_mm[L])

                rows_T(0, 0)
                first_then_loop(pe, two_experts, E // 2, last=1)

            mixer_out(0)
            experts(0)

            pe.wait_ge(xn_in, NT + XT)
            for g in range(KC):
                if g >= 4:
                    pe.wait_ge(inT_a, KC + g - 3)
                for t in range(XT):
                    last = tr(PS[:, g % 4, t * P:(t + 1) * P], xnc[:, t, g * P:(g + 1) * P], ident)
                last.then_inc(inT, 1)
            pe.wait_ge(inT_a, 2 * KC)
            pe.wait_ge(cb_in, 32)
            for n in range(KC):
                if n >= 2:
                    pe.wait_ge(z_ready, n - 1)
                for m, w in enumerate((w_cb, w_cc, w_cv)):
                    if n % 4 == 0 and m >= 1:
                        pe.wait_ge((cc_in, cv_in)[m - 1][n // 4], 16)
                    for k in range(KC):
                        last = mm(PS[:, 3 * (n % 2) + m, :], w[:, k, n * P:(n + 1) * P], hT1[:, k, :],
                                  start=k == 0, stop=k == KC - 1)
                last.then_inc(conv_mm, 1)

            mixer_out(1)
            experts(1)

        @block.scalar
        def _(act):
            f = nc.scalar.activation
            own = Chain(act, act_step)
            act.dma_start(cond_rows[0:KC, :], c.rearrange("a (k p) -> (a k) p", p=P)).then_inc(cond_in, 16)
            act.dma_start(cond_rows[KC:2 * KC, :], c_ctx.rearrange("(k p) -> k p", p=P)).then_inc(cond_in, 16)
            act.dma_start(ident, ident_in).then_inc(cond_in, 16)
            vecs = [(V_NM, norm_mix.rearrange("a (k p) -> (a k) p", p=P)), (V_NF, norm_ffn.rearrange("a (k p) -> (a k) p", p=P)),
                    (V_QN, mla_q_norm.rearrange("a (k p) -> (a k) p", p=P)), (V_KVN, mla_kv_norm.rearrange("a (k p) -> (a k) p", p=P)),
                    (V_GQ, mla_q_gain[:, 0:NOPE]), (V_GK, mla_k_gain[:, 0:NOPE]),
                    (V_CONV, conv_w.rearrange("a j (k p) -> (a j k) p", p=P))]
            for L in range(2):
                for m in range(2):
                    vecs.append((V_ADA + 32 * L + 16 * m,
                                 ada_b[L, 3 * D * m:3 * D * m + 2 * D].rearrange("(k p) -> k p", p=P)))
            for lo, src in vecs:
                act.dma_start(vec_rows[lo:lo + src.shape[0], :], src).then_inc(vec_in, 16)
            act.dma_start(vec_rows[NR:P, :], ident_in[0:1, :]).then_inc(vec_in, 16)
            for L in range(2):
                act.dma_start(gate_mix[L], ada_b[L:L + 1, 2 * D:3 * D].to_broadcast([P, D])).then_inc(misc_in, 16)
                for h in range(2):
                    act.dma_start(gate_ffn[L][64 * h:64 * h + 64, :],
                                  ada_b[L:L + 1, 5 * D + HALF * h:5 * D + HALF * (h + 1)].to_broadcast([64, HALF])
                                  ).then_inc(misc_in, 16)
                act.dma_start(router[L], router_w[L].rearrange("(k p) e -> p k e", p=P)).then_inc(misc_in, 16)
            for h in range(2):
                act.dma_start(rope_gain[:, h, :], (mla_q_gain, mla_k_gain)[h][:, NOPE:QK].to_broadcast([P, ROPE])).then_inc(misc_in, 16)
                for m in range(2):
                    act.dma_start(rope_cs[:, m, :, :].rearrange("p (t h) f -> p t h f", h=2)[:, :, h, :],
                                  rope_in[m].rearrange("(t p) f -> p t f", p=P)).then_inc(misc_in, 16)
            act.wait_ge(cond_in, 48)
            f(cond_rows[0:2 * KC, :], cond_rows[0:2 * KC, :], ACT.Silu).then_inc(silu_c, 1)
            act.wait_ge(rows_in_s[0], 16)
            for j in range(NT):
                if j == CT:
                    act.wait_ge(rows_in_s[1], 16)
                own.link(f(junk_in, rows_in[:, j, :], ACT.Square, accum_out=stat[:, j:j + 1]))
            act.wait_ge(zeroed, 3)
            f(stat[:, 8:8 + NT], stat[:, 0:NT], ACT.Sqrt, bias=eps, scale=1.0 / D).then_inc(std_in, 1)

            def ada_copy(u):
                act.wait_ge(ada_main, u + 1)
                if u >= 2:
                    act.wait_ge(ada_sum, u - 1)
                f(ada_part[:, u % 2, :], PS[:, ADA_BANKS[u % 2], :], ACT.Copy).then_inc(ada_rows, 1)

            for u in range(FIRST_UNITS):
                ada_copy(u)
            act.wait_ge(mod_ready, 1)
            for g in range(KC):
                act.wait_ge(inT, g + 1)
                f(hT[:, g, CX:KEYS], PS[:, T_BANKS[g % 5], :], ACT.Identity, bias=modv[0][0][:, 0, g, 0:1],
                  scale=scl[0][0][:, g, 0:1]).then_inc(inT_a, 1)
            for n, j in enumerate(TILES):
                act.wait_ge(lat_done, n + 1)
                if n >= 2:
                    act.wait_ge(latT, n - 1)
                if j >= CT:
                    own.link(f(lat[:, n % 2, 0:BANK], PS[:, 4, :], ACT.Copy))
                    act.sem_inc(lat_a, 1)
                    act.wait_ge(lat_d, n + 1)
                    own.link(f(junk_in[:, 0:QL], lat[:, n % 2, 0:QL], ACT.Square, accum_out=stat[:, 16 + j:17 + j]))
                else:
                    own.link(f(lat[:, n % 2, QL:LAT], PS[:, 4, 0:LAT - QL], ACT.Copy))
                    act.sem_inc(lat_a, 1)
                own.link(f(junk_in[:, 0:KVL], lat[:, n % 2, QL:QL + KVL], ACT.Square, accum_out=stat[:, 24 + j:25 + j]))
                own.link(f(junk_in[:, 0:ROPE], lat[:, n % 2, QL + KVL:LAT], ACT.Square, accum_out=stat[:, 32 + j:33 + j]))
                if j >= CT:
                    f(stat[:, 40 + j:41 + j], stat[:, 16 + j:17 + j], ACT.Sqrt, bias=eps, scale=1.0 / QL)
                f(stat[:, 48 + j:49 + j], stat[:, 24 + j:25 + j], ACT.Sqrt, bias=eps, scale=1.0 / KVL).then_inc(lat_std, 1)

            act.wait_ge(lat_n, NT)
            def pair(i):
                def copy_unit(q):
                    act.wait_ge(unit_mm, UP * i + q + 1)
                    wait(act, unit_stored[q % 2], 16 * ((3, 2)[q % 2] * i + q // 2))
                    f(ada_part[:, q % 2, :], PS[:, PAIR_BANKS[q], :], ACT.Copy).then_inc(unit_copied, 1)

                def take(s):
                    act.wait_ge(proj, 10 * i + s + 1)
                    dst = kvtok[:, s, :] if s < NT else qtok[:, s - NT, :]
                    f(dst, PS[:, 6, 0:dst.shape[1]], ACT.Copy).then_inc(proj_a, 1)

                for s in (0, 2, 4):
                    take(s)
                act.wait_ge(proj_a, 5 * i + 3)
                act.wait_ge(proj_d, 5 * i + 3)
                f(sqk, kvtok.rearrange("p t (h n) -> p (t h) n", h=2)[:, :, 0:NOPE], ACT.Square).then_inc(sq_ready, 1)
                copy_unit(0)
                take(6)
                act.wait_ge(ss_ready, 2 * i + 1)
                f(smal[:, 16:28], smal[:, 0:12], ACT.Sqrt, bias=eps, scale=1.0 / QK).then_inc(std_ready, 1)
                take(8)
                act.wait_ge(proj_a, 5 * i + 5)
                act.wait_ge(proj_d, 5 * i + 5)
                f(sqq, qtok.rearrange("p t (h n) -> p (t h) n", h=2), ACT.Square).then_inc(sq_ready, 1)
                act.wait_ge(ss_ready, 2 * i + 2)
                f(smal[:, 40:48], smal[:, 32:40], ACT.Sqrt, bias=eps, scale=1.0 / QK).then_inc(std_ready, 1)
                for g in (0, 2, 4, 6):
                    if g == 6:
                        copy_unit(1)
                    act.wait_ge(trn, 8 * i + g + 1)
                    if g == 0:
                        ins = f(kT[:, 0, 0:BANK], PS[:, 4, :], ACT.Copy)
                    elif g == 2:
                        ins = f(kT[:, :, BANK:KEYS], PS[:, 4, :].rearrange("p (a b) -> p a b", a=2), ACT.Copy)
                    elif g == 4:
                        ins = f(kTr[:, BANK:KEYS], PS[:, 4, 0:KEYS - BANK], ACT.Copy)
                    else:
                        ins = f(qT[:, 1, :], PS[:, 4, :], ACT.Copy, scale=gqk)
                    ins.then_inc(trn_a, 1)

                def take_pT(r):
                    act.wait_ge(pT_done, 8 * i + r + 1)
                    f(pT[r // XT][:, 0:4, (r % XT) * P:(r % XT + 1) * P], PS[:, 4, :].rearrange("p (a b) -> p a b", a=4),
                      ACT.Copy).then_inc(pT_a, 1)

                def take_o(j):
                    act.wait_ge(pv_done, 2 * i + j + 1)
                    f(oT[:, bass.ds(2 * i + j, 1), :].rearrange("p a t -> p (a t)"), PS[:, 6 + j, :], ACT.Copy).then_inc(oT_ready, 1)

                for r in range(2 * XT):
                    if r == 6:
                        take_o(0)
                    if r >= 1:
                        take_pT(r - 1)
                    act.wait_ge(nmax, 8 * i + r + 1)
                    f(prob[:, r % 2, :].rearrange("p (a b) -> p a b", a=2), PS[:, 2 * (r % 2):2 * (r % 2) + 2, 0:SCR], ACT.Exp,
                      bias=stat[:, 64 + r % 2:65 + r % 2], scale=SCALE,
                      accum_out=stat[:, 68 + r % 2:69 + r % 2]).then_inc(exp_done, 1)
                    if r in BEHIND:
                        copy_unit(BEHIND[r])
                take_pT(2 * XT - 1)
                take_o(1)

            first_then_loop(act, pair, PAIRS)

            def router_part(L):
                for t in range(XT + 2):
                    if t < XT:
                        act.wait_ge(x_new[L], t + 1)
                        own.link(f(PS[:, 2 * (t % 2):2 * (t % 2) + 2, :], xres[L][:, t, :].rearrange("p (a b) -> p a b", a=2), ACT.Square, accum_out=stat[:, t:t + 1]))
                        f(stat[:, 8 + t:9 + t], stat[:, t:t + 1], ACT.Sqrt, bias=eps, scale=1.0 / D).then_inc(x_std[L], 1)
                    if t >= 2:
                        v = t - 2
                        act.wait_ge(lg_neg[L], v + 1)
                        f(probs, PS[:, 6, 0:E], ACT.Exp, bias=stat[:, 16:17], accum_out=stat[:, 17:18]).then_inc(lg_exp[L], 1)

            def experts(L):
                def expert(e):
                    act.wait_ge(gate_mm[L], e + 1)
                    wait(act, hid_ok[L], e)
                    f(silu_a, PS[:, 0, :], ACT.Silu).then_inc(silu_ok[L], 1)
                    act.wait_ge(hid_T[L], e + 1)
                    wait(act, down_mm[L], e)
                    f(hidT, PS[:, 3, :], ACT.Copy).then_inc(hidT_ok[L], 1)

                first_then_loop(act, expert, E)

            router_part(0)
            experts(0)

            act.wait_ge(xres_in, 32)
            for t in range(XT):
                own.link(f(junk, xres[1][:, t, :], ACT.Square, accum_out=stat[:, t:t + 1]))
            f(stat[:, 8:8 + XT], stat[:, 0:XT], ACT.Sqrt, bias=eps, scale=1.0 / D).then_inc(std_in, 1)
            for g in range(KC):
                act.wait_ge(inT, 12 + g + 1)
                f(hT1[:, g, :], PS[:, g % 4, :], ACT.Identity, bias=modv[1][0][:, 0, g, 0:1],
                  scale=scl[1][0][:, g, 0:1]).then_inc(inT_a, 1)
            for n in range(KC):
                act.wait_ge(conv_mm, n + 1)
                if n >= 2:
                    act.wait_ge(z_ready, n - 1)
                f(c_sb[:, n % 2, :], PS[:, 3 * (n % 2) + 1, :], ACT.Copy).then_inc(c_copied, 1)
            act.wait_ge(z_ready, KC)
            router_part(1)
            experts(1)

        @block.vector
        def _(dve):
            v = nc.vector
            own = Chain(dve, dve_step)
            v.memset(cond_T, 0.0).then_inc(zeroed, 1)
            v.memset(eps, EPS).then_inc(zeroed, 1)
            dve.wait_ge(cond_in, 48)
            v.tensor_reduce(sel2, ident.rearrange("p (a b) -> p b a", a=4)[:, 0:2, :], AX.X, ALU.add).then_inc(zeroed, 1)
            dve.wait_ge(zeroed, 3)
            v.tensor_copy(selx, sel2[:, 0:1].to_broadcast([P, P])).then_inc(sels, 1)
            dve.wait_ge(setup_T, 1)
            v.tensor_copy(cond_T[:, :, 0:2], PS[:, 7, 0:2 * KC].rearrange("p (r k) -> p k r", r=2)).then_inc(setup_out, 1)
            dve.wait_ge(setup_T, 2)
            v.tensor_copy(vec[:, 0:NR], PS[:, 6, 0:NR]).then_inc(setup_out, 1)
            dve.wait_ge(setup_out, 2)
            own.link(v.tensor_tensor(gqk, vec[:, V_GQ:V_GQ + 1], vec[:, V_GK:V_GK + 1], ALU.mult))
            dve.wait_ge(std_in, 1)
            own.link(v.reciprocal(stat[:, 8:8 + NT], stat[:, 8:8 + NT]))
            for j in range(NT):
                v.tensor_scalar(rows_in[:, j, :], rows_in[:, j, :], stat[:, 8 + j:9 + j], None, ALU.mult).then_inc(xn_in, 1)
            dve.wait_ge(misc_in, 16 * 14)

            def col(lo, n, m):
                return vec[:, lo:lo + n].unsqueeze(2).to_broadcast([P, n, m])

            def ada_take(u):
                L, num = (0, u) if u < FIRST_UNITS else LATER[u - FIRST_UNITS]
                n, half, b = num // 2, num % 2, collect_bank(u)
                dve.wait_ge(ada_sum, u + 1)
                if n == 2:
                    g = gate_mix[L][:, half * BANK:(half + 1) * BANK]
                    v.tensor_tensor(g, PS[:, b, :], g, ALU.add).then_inc(ada_out, 1)
                elif n == 5:
                    g = gate_ffn[L][64 * half:64 * half + 64, :]
                    v.tensor_tensor(g, PS[64 * half:64 * half + 64, b, :], g, ALU.add).then_inc(ada_out, 1)
                else:
                    m, kind = n // 3, n % 3
                    v.tensor_tensor(modv[L][m][:, kind, 4 * half:4 * half + 4, :],
                                    PS[:, b, 0:8].rearrange("p (k r) -> p k r", r=2),
                                    col(V_ADA + 32 * L + 16 * m + KC * kind + 4 * half, 4, 2), ALU.add).then_inc(ada_out, 1)
                    if kind == 1 and half == 1:
                        dve.wait_ge(ada_out, u + 1)
                        v.scalar_tensor_tensor(out=scl[L][m], in0=modv[L][m][:, 1], scalar=1.0,
                                               in1=col((V_NM, V_NF)[m] + KC * L, KC, 2), op0=ALU.add,
                                               op1=ALU.mult).then_inc(mod_ready, 1)

            for u in range(FIRST_UNITS):
                ada_take(u)
            dve.wait_ge(mod_ready, 1)
            for g in range(KC, 12):
                dve.wait_ge(inT, g + 1)
                for q in range(2):
                    k = 2 * (g - KC) + q
                    last = v.tensor_scalar(hT[:, k, 0:CX], PS[:, T_BANKS[g % 5], q * CX:(q + 1) * CX],
                                           scl[0][0][:, k, 1:2], modv[0][0][:, 0, k, 1:2], ALU.mult, ALU.add)
                last.then_inc(inT_d, 1)
            for n, j in enumerate(TILES):
                row = lat[:, n % 2, :]
                if j >= CT:
                    dve.wait_ge(lat_done, n + 1)
                    if n >= 2:
                        dve.wait_ge(latT, n - 1)
                    v.tensor_copy(row[:, BANK:LAT], PS[:, 5, 0:LAT - BANK]).then_inc(lat_d, 1)
                dve.wait_ge(lat_std, n + 1)
                v.tensor_copy(kraw[:, j, :], row[:, QL + KVL:LAT])
                own.link(v.reciprocal(stat[:, 48 + j:49 + j], stat[:, 48 + j:49 + j]))
                last = v.tensor_scalar(row[:, QL:QL + KVL], row[:, QL:QL + KVL], stat[:, 48 + j:49 + j], None, ALU.mult)
                if j >= CT:
                    own.link(v.reciprocal(stat[:, 40 + j:41 + j], stat[:, 40 + j:41 + j]))
                    last = v.tensor_scalar(row[:, 0:QL], row[:, 0:QL], stat[:, 40 + j:41 + j], None, ALU.mult)
                last.then_inc(lat_n, 1)
                dve.wait_ge(latT, n + 1)
                if j >= CT:
                    v.tensor_tensor(qlT[:, :, (j - CT) * P:(j - CT + 1) * P],
                                    PS[:, 0, 0:QL].rearrange("p (a b) -> p a b", b=P), col(V_QN, QC, P), ALU.mult)
                v.tensor_tensor(kvlT[:, :, j * P:(j + 1) * P], PS[:, 1, 0:KVL].rearrange("p (a b) -> p a b", b=P),
                                col(V_KVN, KVC, P), ALU.mult).then_inc(latT_d, 1)

            dve.wait_ge(latT_d, NT)
            own.link(v.tensor_tensor(krot, kraw, rope_gain[:, 1:2, :].to_broadcast([P, NT, ROPE]), ALU.mult))
            k4 = krot[:, CT:NT, :].rearrange("p t (a b f) -> p t a b f", a=2, b=2)
            k1, k2 = k4[:, :, :, 0, :], k4[:, :, :, 1, :]
            cs = [rope_cs[:, m, :, :].rearrange("p (t h) (a f) -> p t h a f", h=2, a=2)[:, :, 0] for m in range(2)]
            r4 = kraw[:, CT:NT, :].rearrange("p t (a b f) -> p t a b f", a=2, b=2)
            tm = [ktmp[:, m].rearrange("p t (a f) -> p t a f", a=2) for m in range(2)]
            v.tensor_tensor(tm[0], k1, cs[0], ALU.mult)
            own.link(v.tensor_tensor(tm[1], k2, cs[1], ALU.mult))
            own.link(v.tensor_tensor(r4[:, :, :, 0, :], tm[0], tm[1], ALU.subtract))
            v.tensor_tensor(tm[0], k2, cs[0], ALU.mult)
            own.link(v.tensor_tensor(tm[1], k1, cs[1], ALU.mult))
            own.link(v.tensor_tensor(r4[:, :, :, 1, :], tm[0], tm[1], ALU.add))
            v.tensor_copy(krot[:, CT:NT, :], kraw[:, CT:NT, :]).then_inc(krot_ready, 1)
            dve.wait_ge(krot_ready, 1)

            base = own.n
            STEPS_IN_PAIR = 4 + 4 * XT
            def pair(i):
                def take(s):
                    dve.wait_ge(proj, 10 * i + s + 1)
                    dst = kvtok[:, s, :] if s < NT else qtok[:, s - NT, :]
                    v.tensor_copy(dst, PS[:, 7, 0:dst.shape[1]]).then_inc(proj_d, 1)

                own.n = base + STEPS_IN_PAIR * i
                for s in (1, 3, 5):
                    take(s)
                dve.wait_ge(sq_ready, 2 * i + 1)
                own.link(v.tensor_reduce(smal[:, 0:12], sqk, AX.X, ALU.add))
                v.tensor_tensor(smal[:, 0:12].rearrange("p (t h) -> p t h", h=2), smal[:, 0:12].rearrange("p (t h) -> p t h", h=2),
                                stat[:, 32:32 + NT].unsqueeze(2).to_broadcast([P, NT, 2]), ALU.add).then_inc(ss_ready, 1)
                take(7)
                dve.wait_ge(std_ready, 2 * i + 1)
                v.reciprocal(smal[:, 16:28], smal[:, 16:28]).then_inc(rk_ready, 1)
                dve.wait_ge(rk_ready, i + 1)
                kk = kvtok.rearrange("p t (h n) -> p (t h) n", h=2)[:, :, 0:NOPE]
                v.tensor_tensor(kk, kk, smal[:, 16:28].unsqueeze(2).to_broadcast([P, 12, NOPE]), ALU.mult).then_inc(kn_ready, 1)
                take(9)
                dve.wait_ge(sq_ready, 2 * i + 2)
                v.tensor_reduce(smal[:, 32:40], sqq, AX.X, ALU.add).then_inc(ss_ready, 1)
                dve.wait_ge(std_ready, 2 * i + 2)
                own.link(v.reciprocal(smal[:, 40:48], smal[:, 40:48]))
                q8 = qtok.rearrange("p t (h n) -> p (t h) n", h=2)
                own.link(v.tensor_tensor(q8, q8, smal[:, 40:48].unsqueeze(2).to_broadcast([P, 8, QK]), ALU.mult))
                qr = q8[:, :, NOPE:QK]
                v.tensor_tensor(qr, qr, rope_gain[:, 0:1, :].to_broadcast([P, 8, ROPE]), ALU.mult).then_inc(qg_ready, 1)
                dve.wait_ge(qg_ready, i + 1)
                q5 = qr.rearrange("p t (a b f) -> p t a b f", a=2, b=2)
                o5 = q_rot.rearrange("p t (h n) -> p (t h) n", h=2).rearrange("p t (a b f) -> p t a b f", a=2, b=2)
                c8 = [rope_cs[:, m].rearrange("p t (a f) -> p t a f", a=2) for m in range(2)]
                t8 = [rtmp[:, m].rearrange("p (t a f) -> p t a f", a=2, f=RF) for m in range(2)]
                v.tensor_tensor(t8[0], q5[:, :, :, 0, :], c8[0], ALU.mult)
                own.link(v.tensor_tensor(t8[1], q5[:, :, :, 1, :], c8[1], ALU.mult))
                v.tensor_tensor(o5[:, :, :, 0, :], t8[0], t8[1], ALU.subtract).then_inc(qrot_d, 1)
                for g in (1, 3, 5, 7):
                    dve.wait_ge(trn, 8 * i + g + 1)
                    if g == 1:
                        ins = v.tensor_copy(kT[:, 1, 0:BANK], PS[:, 5, :])
                    elif g == 3:
                        ins = v.tensor_copy(kTr[:, 0:BANK], PS[:, 5, :])
                    elif g == 5:
                        ins = v.tensor_scalar(qT[:, 0, :], PS[:, 5, :], gqk, None, ALU.mult)
                    else:
                        ins = v.tensor_copy(qTr, PS[:, 5, :])
                    ins.then_inc(trn_d, 1)

                def norm(r):
                    dve.wait_ge(exp_done, 8 * i + r + 1)
                    own.link(v.reciprocal(stat[:, 70 + r % 2:71 + r % 2], stat[:, 68 + r % 2:69 + r % 2]))
                    v.tensor_scalar(prob[:, r % 2, :], prob[:, r % 2, :], stat[:, 70 + r % 2:71 + r % 2], None,
                                    ALU.mult).then_inc(p_norm, 1)

                def top(r):
                    dve.wait_ge(s_done, 8 * i + r + 1)
                    own.link(v.tensor_reduce(stat[:, 66 + r % 2:67 + r % 2], PS[:, 2 * (r % 2):2 * (r % 2) + 2, 0:SCR], AX.XY, ALU.max))
                    v.tensor_scalar(stat[:, 64 + r % 2:65 + r % 2], stat[:, 66 + r % 2:67 + r % 2], -SCALE, None,
                                    ALU.mult).then_inc(nmax, 1)

                def take_pT(r):
                    dve.wait_ge(pT_done, 8 * i + r + 1)
                    v.tensor_copy(pT[r // XT][:, 4:6, (r % XT) * P:(r % XT + 1) * P],
                                  PS[:, 5, 0:2 * P].rearrange("p (a b) -> p a b", a=2)).then_inc(pT_d, 1)

                for r in range(2 * XT):
                    if r >= 1:
                        norm(r - 1)
                    top(r)
                    if r >= 1:
                        take_pT(r - 1)
                norm(2 * XT - 1)
                take_pT(2 * XT - 1)

            first_then_loop(dve, pair, PAIRS)
            own.n = base + STEPS_IN_PAIR * PAIRS

            def router_part(L):
                A = scl[L][1]
                for t in range(XT + 3):
                    if L == 0 and t == 0:
                        for u in later_units(0):
                            ada_take(u)
                        dve.wait_ge(ada_out, UNITS)
                    if t < XT:
                        dve.wait_ge(mo_done[L], t + 1)
                        if t >= 1:
                            dve.wait_ge(x_new[L], t)
                        v.tensor_tensor(mo_tmp.rearrange("p (a b) -> p a b", a=2), PS[:, 2 * (t % 2):2 * (t % 2) + 2, :],
                                        gate_mix[L].rearrange("p (a b) -> p a b", a=2), ALU.mult).then_inc(mo_mul[L], 1)
                    if L == 0 and t == 1:
                        for u in later_units(1):
                            ada_take(u)
                        dve.wait_ge(mod_ready, 4)
                    if 1 <= t <= XT:
                        w = t - 1
                        dve.wait_ge(xnT[L], w + 1)
                        if w >= 1:
                            dve.wait_ge(hf_ready[L], w)
                        v.tensor_tensor(hf_tmp.rearrange("p (k m) -> p k m", k=KC),
                                        PS[:, 4:6, :].rearrange("p a (k m) -> p (a k) m", k=4),
                                        A[:, :, 0:1].to_broadcast([P, KC, P]), ALU.mult).then_inc(hf_mul[L], 1)
                    if t < XT:
                        dve.wait_ge(x_std[L], t + 1)
                        if t >= 2:
                            dve.wait_ge(xnT[L], t - 1)
                            dve.wait_ge((xn_st0, xn_st1)[t % 2][L], 16 * (t // 2))
                        own.link(v.reciprocal(stat[:, 8 + t:9 + t], stat[:, 8 + t:9 + t]))
                        v.tensor_scalar(xnt[:, t % 2, :], xres[L][:, t, :], stat[:, 8 + t:9 + t], None, ALU.mult).then_inc(xn_ready[L], 1)
                    if 2 <= t <= XT + 1:
                        w = t - 2
                        dve.wait_ge(lg_done[L], w + 1)
                        own.link(v.tensor_reduce(stat[:, 18:19], PS[:, 6, 0:E], AX.X, ALU.max))
                        v.tensor_scalar(stat[:, 16:17], stat[:, 18:19], -1.0, None, ALU.mult).then_inc(lg_neg[L], 1)
                        dve.wait_ge(lg_exp[L], w + 1)
                        own.link(v.reciprocal(stat[:, 19:20], stat[:, 17:18]))
                        v.tensor_scalar(aff[:, w, :], probs, stat[:, 19:20], None, ALU.mult).then_inc(lg_aff[L], 1)
                    if t >= 3:
                        w = t - 3
                        dve.wait_ge(affT_ps[L], w + 1)
                        v.tensor_copy(affT[:, w * P:(w + 1) * P], PS[0:E, 7, 0:P]).then_inc(affT_sb[L], 1)
                dve.wait_ge(affT_sb[L], XT)
                for r in range(CAP // 8):
                    now, nxt = (affT[:, (r + m) % 2 * T:((r + m) % 2 + 1) * T] for m in range(2))
                    best = top_v[:, 8 * r:8 * r + 8]
                    own.link(v.max(best, now))
                    v.max_index(top_i[:, 8 * r:8 * r + 8], best, now)
                    if r < CAP // 8 - 1:
                        own.link(v.match_replace(nxt, best, now, -1.0))
                    else:
                        own.link(v.tensor_copy(slots_v[:, 0:CAP], top_v))
                v.tensor_copy(slots_v[:, CAP:P], top_v)
                v.tensor_scalar(slots_i[:, 0:CAP], top_i, 2.0, None, ALU.mult)
                own.link(v.tensor_scalar(slots_i[:, CAP:P], top_i, 2.0, 1.0, ALU.mult, ALU.add))
                dve.sem_inc(slots_f[L], 1)
                dve.wait_ge(slots_T[L], 1)
                v.tensor_copy(row_no, PS[:, 7, 0:E])
                v.tensor_copy(gate_e, PS[:, 7, E:2 * E]).then_inc(slots_ready[L], 1)

            def experts(L):
                A, B = scl[L][1], modv[L][1]

                def modulate(e, s):
                    dve.wait_ge(xs_T[L], e + 1)
                    a = A[:, :, 0].rearrange("p (h q) -> p q h", h=2).unsqueeze(3).to_broadcast([P, 4, 2, CAP])
                    b = B[:, 0, :, 0].rearrange("p (h q) -> p q h", h=2).unsqueeze(3).to_broadcast([P, 4, 2, CAP])
                    own.link(v.tensor_tensor(xs_m.rearrange("p (q h m) -> p q h m", q=4, h=2),
                                             PS[:, 4, :].rearrange("p (q h m) -> p q h m", q=4, h=2), a, ALU.mult))
                    v.tensor_tensor(xsT[:, s, :].rearrange("p (q h m) -> p q h m", q=4, h=2),
                                    xs_m.rearrange("p (q h m) -> p q h m", q=4, h=2), b, ALU.add).then_inc(xs_mod[L], 1)

                def two_experts(i):
                    own.n = base + 2 * i
                    for s in range(2):
                        e = 2 * i + s
                        dve.wait_ge(silu_ok[L], e + 1)
                        dve.wait_ge(up_mm[L], e + 1)
                        wait(dve, hid_T[L], e)
                        v.tensor_tensor(hid, silu_a, PS[:, 1, :], ALU.mult).then_inc(hid_ok[L], 1)
                        if not (isinstance(e, int) and e == E - 1):
                            modulate(e + 1, 1 - s)
                        dve.wait_ge(down_mm[L], e + 1)
                        wait(dve, scattered[L], 16 * (e - 1))
                        v.scalar_tensor_tensor(out=y_s[:, s, :], in0=PS[:, 2, :], scalar=gate_e[:, bass.ds(e, 1)],
                                               in1=gate_ffn[L], op0=ALU.mult, op1=ALU.mult).then_inc(y_ok[L], 1)

                modulate(0, 0)
                base = own.n
                first_then_loop(dve, two_experts, E // 2, last=1)
                own.n = base + E - 1

            router_part(0)
            experts(0)

            dve.wait_ge(std_in, 2)
            own.link(v.reciprocal(stat[:, 8:8 + XT], stat[:, 8:8 + XT]))
            for t in range(XT):
                v.tensor_scalar(xnc[:, t, :], xres[1][:, t, :], stat[:, 8 + t:9 + t], None, ALU.mult).then_inc(xn_in, 1)
            v.memset(u_pad[:, 0:1], 0.0)
            own.link(v.memset(u_pad[:, T + 1:T + 2], 0.0))
            for n in range(KC):
                w3 = [vec[:, V_CONV + m * KC + n:V_CONV + m * KC + n + 1] for m in range(3)]
                dve.wait_ge(conv_mm, n + 1)
                dve.wait_ge(c_copied, n + 1)
                own.link(v.tensor_tensor(u_pad[:, 1:T + 1], PS[:, 3 * (n % 2) + 2, :], c_sb[:, n % 2, :], ALU.mult))
                own.link(v.tensor_scalar(y_sb, u_pad[:, 0:T], w3[0], None, ALU.mult))
                for m in (1, 2):
                    own.link(v.scalar_tensor_tensor(out=y_sb, in0=u_pad[:, m:T + m], scalar=w3[m], in1=y_sb,
                                                    op0=ALU.mult, op1=ALU.add))
                v.tensor_tensor(zT[:, n, :], PS[:, 3 * (n % 2), :], y_sb, ALU.mult).then_inc(z_ready, 1)
            router_part(1)
            experts(1)

        @block.gpsimd
        def _(pool):
            g = nc.gpsimd
            own = Chain(pool, pool_step)
            pool.wait_ge(krot_ready, 1)
            base = 0
            def pair(i):
                own.n = base + i
                pool.wait_ge(rk_ready, i + 1)
                g.tensor_tensor(kr_s.rearrange("p t (h n) -> p t h n", h=2),
                                krot.unsqueeze(2).to_broadcast([P, NT, 2, ROPE]),
                                smal[:, 16:28].rearrange("p (t h) -> p t h", h=2).unsqueeze(3).to_broadcast([P, NT, 2, ROPE]),
                                ALU.mult).then_inc(krs_ready, 1)
                pool.wait_ge(qg_ready, i + 1)
                q5 = qtok.rearrange("p t (h n) -> p (t h) n", h=2)[:, :, NOPE:QK].rearrange("p t (a b f) -> p t a b f", a=2, b=2)
                o5 = q_rot.rearrange("p t (h n) -> p (t h) n", h=2).rearrange("p t (a b f) -> p t a b f", a=2, b=2)
                c8 = [rope_cs[:, m].rearrange("p t (a f) -> p t a f", a=2) for m in range(2)]
                t8 = [rtmp[:, 2 + m].rearrange("p (t a f) -> p t a f", a=2, f=RF) for m in range(2)]
                g.tensor_tensor(t8[0], q5[:, :, :, 1, :], c8[0], ALU.mult)
                own.link(g.tensor_tensor(t8[1], q5[:, :, :, 0, :], c8[1], ALU.mult))
                g.tensor_tensor(o5[:, :, :, 1, :], t8[0], t8[1], ALU.add).then_inc(qrot_p, 1)

            first_then_loop(pool, pair, PAIRS)
            own.n = base + PAIRS

            def router_part(L):
                B = modv[L][1]
                if L == 0:
                    pool.wait_ge(xres_in, 16)
                for t in range(XT + 1):
                    if t < XT:
                        pool.wait_ge(mo_mul[L], t + 1)
                        g.tensor_tensor(xres[L][:, t, :], xres[L][:, t, :], mo_tmp, ALU.add).then_inc(x_new[L], 1)
                    if t >= 1:
                        w = t - 1
                        pool.wait_ge(hf_mul[L], w + 1)
                        if w >= 2:
                            pool.wait_ge(lg_done[L], w - 1)
                        g.tensor_tensor(hfT[:, w % 2, :].rearrange("p (k m) -> p k m", k=KC),
                                        hf_tmp.rearrange("p (k m) -> p k m", k=KC),
                                        B[:, 0, :, 0:1].to_broadcast([P, KC, P]), ALU.add).then_inc(hf_ready[L], 1)

            def experts(L):
                xn_half = xn_dram.rearrange("t (h d) -> (t h) d", h=2)
                acc_half = acc_dram[L].rearrange("t (h d) -> (t h) d", h=2)

                def gather(e, s):
                    g.tensor_copy(row_in[s], row_no[:, bass.ds(e, 1)]).then_inc(row_copied[L], 1)
                    pool.wait_ge(row_copied[L], e + 1)
                    pool.sem_inc(turn, 1)
                    g.indirect_dma_start(out=xs[:, s, :], out_offset=None, in_=xn_half,
                                         in_offset=bass.IndirectOffsetOnAxis(ap=row_in[s], axis=0)
                                         ).then_inc((xs_in0, xs_in1)[s][L], 16)

                def two_experts(i):
                    for s in range(2):
                        e = 2 * i + s
                        if not (isinstance(e, int) and e >= E - 2):
                            pool.wait_ge(xs_T[L], e + 1)
                            gather(e + 2, s)
                        wait(pool, scattered[L], 16 * e)
                        g.tensor_copy(row_out, row_no[:, bass.ds(e, 1)]).then_inc(row_out_ok[L], 1)
                        pool.wait_ge(row_out_ok[L], e + 1)
                        pool.wait_ge(y_ok[L], e + 1)
                        pool.sem_inc(turn, 1)
                        g.indirect_dma_start(out=acc_half, out_offset=bass.IndirectOffsetOnAxis(ap=row_out, axis=0),
                                             in_=y_s[:, s, :], in_offset=None, compute_op=ALU.add).then_inc(scattered[L], 16)

                pool.wait_ge(slots_ready[L], 1)
                pool.wait_ge(acc_stored[L], 16 * XT)
                pool.wait_ge(xn_st0[L], 16 * XT // 2)
                pool.wait_ge(xn_st1[L], 16 * XT // 2)
                gather(0, 0)
                gather(1, 1)
                first_then_loop(pool, two_experts, E // 2, last=1)

            router_part(0)
            experts(0)
            router_part(1)
            experts(1)


_INS = ["x", "c", "ctx", "c_ctx", "norm_mix", "norm_ffn", "ada_w", "ada_b", "mla_w_in", "mla_q_norm", "mla_w_qb",
        "mla_kv_norm", "mla_w_kvb", "mla_q_gain", "mla_k_gain", "mla_w_out", "conv_w_in", "conv_w", "conv_w_out",
        "router_w", "exp_w_gate", "exp_w_up", "exp_w_down"]


def rope_tables(tokens, freqs):
    n = np.arange(tokens)
    pos = np.stack([n // GRID_W, n % GRID_W], axis=-1).astype(np.float32)
    inv = np.float32(ROPE_THETA) ** (-np.arange(freqs, dtype=np.float32) / np.float32(freqs))
    ang = (pos[:, :, None] * inv).astype(np.float32).reshape(tokens, 2 * freqs)
    return np.stack([np.cos(ang), np.sin(ang)]).astype(np.float32)


def kernel(**inputs):
    import concourse.bacc as bacc
    from concourse.bass_utils import run_bass_kernel_spmd

    nc = bacc.Bacc("TRN2", target_bir_lowering=False, num_devices=1)
    host = {name: np.ascontiguousarray(inputs[name]) for name in _INS}
    host["ident"] = np.eye(P, dtype=np.float32)
    host["rope"] = rope_tables(host["x"].shape[1], (host["mla_q_gain"].shape[1] - P) // 4)
    arrays, args = {}, []
    for name, a in host.items():
        arrays[f"in_{name}_dram"] = a
        args.append(nc.dram_tensor(f"in_{name}_dram", a.shape, mybir.dt.from_np(a.dtype), kind="ExternalInput").ap())
    args.append(nc.dram_tensor("out_0_dram", host["x"].shape, F32, kind="ExternalOutput").ap())
    build(nc, *args)
    r = run_bass_kernel_spmd(nc, [arrays], core_ids=[0])
    return r.results[0]["out_0_dram"]
```

```python
from contextlib import ExitStack

import numpy as np

import concourse.bass as bass
from concourse import mybir

F32 = mybir.dt.float32
U32 = mybir.dt.uint32
ALU = mybir.AluOpType
ACT = mybir.ActivationFunctionType
AX = mybir.AxisListType

P = 128
BANK = 512
GRID_W = 64
ROPE_THETA = 10000.0
EPS = 1e-6
EC_CAPACITY = 2


class Chain:

    def __init__(self, eng, sem):
        self.eng, self.sem, self.n = eng, sem, 0

    def link(self, ins):
        self.n = self.n + 1
        ins.then_inc(self.sem, 1)
        self.eng.wait_ge(self.sem, self.n)


def wait(eng, sem, n):
    if not (isinstance(n, int) and n <= 0):
        eng.wait_ge(sem, n)


def first_then_loop(eng, body, n, last=0):
    body(0)
    with eng.Fori(1, n - last) as i:
        body(i)
    for i in range(n - last, n):
        body(i)


def build(nc, x, c, ctx, c_ctx, norm_mix, norm_ffn, ada_w, ada_b, mla_w_in, mla_q_norm, mla_w_qb,
          mla_kv_norm, mla_w_kvb, mla_q_gain, mla_k_gain, mla_w_out, conv_w_in, conv_w, conv_w_out,
          router_w, exp_w_gate, exp_w_up, exp_w_down, ident_in, rope_in, out):
    _, T, D = x.shape
    CX = ctx.shape[1]
    KEYS = CX + T
    KC = D // P
    XT, CT = T // P, CX // P
    NT = XT + CT
    QL, KVL = mla_q_norm.shape[1], mla_kv_norm.shape[1]
    QC, KVC = QL // P, KVL // P
    QK = mla_q_gain.shape[1]
    NOPE = P
    ROPE = QK - NOPE
    RF = ROPE // 4
    HEADS = mla_w_qb.shape[2] // QK
    PAIRS = HEADS // 2
    LAT = mla_w_in.shape[2]
    VD = mla_w_kvb.shape[2] // HEADS - NOPE
    E, FF = exp_w_gate.shape[1], exp_w_gate.shape[3]
    CAP = EC_CAPACITY * T // E
    SCALE = float(QK) ** -0.5
    HALF = D // 2
    SCR = KEYS // 2
    UNITS = 6 * D // BANK
    FIRST_UNITS = 4
    assert VD == P and D == FF == 2 * BANK and T == BANK and CAP * 2 == P and D == KC * P and LAT == QL + KVL + ROPE

    es = ExitStack()
    with es:
        def sb(name, cols, dt=F32, rows=P):
            return es.enter_context(nc.sbuf_tensor(name, [rows, cols], dt))[:, :]

        def sem(name):
            return es.enter_context(nc.semaphore(name))

        R = [sb(f"ring{n}", KC * FF) for n in range(3)]
        W = sb("work", 22528)
        PS = es.enter_context(nc.psum_tensor("ps", [P, 8, BANK], F32))

        def view(t, lo, *dims):
            n = int(np.prod(dims))
            v = t[:, lo:lo + n]
            if len(dims) == 2:
                v = v.rearrange("p (a b) -> p a b", b=dims[1])
            if len(dims) == 3:
                v = v.rearrange("p (a b c) -> p a b c", b=dims[1], c=dims[2])
            return v

        ident = sb("ident", P)
        cond_rows, vec_rows = W[:, 20736:20736 + P], W[:, 20864:20864 + P]
        vec = sb("vec", P)
        NR = 127
        V_NM, V_NF, V_ADA, V_QN, V_KVN, V_GQ, V_GK, V_CONV = 0, 16, 32, 96, 99, 101, 102, 103
        cond_T = view(sb("cond_T", KC * 32), 0, KC, 32)
        sel2 = sb("sel2", 2)
        selx = sb("selx", P)
        eps = sb("eps", 1)
        ada_part = view(sb("ada_part", 2 * BANK), 0, 2, BANK)
        junk = ada_part.rearrange("p a b -> p (a b)")
        modv = [[view(sb(f"mod{L}{n}", 2 * KC * 2), 0, 2, KC, 2) for n in "mf"] for L in range(2)]
        scl = [[view(sb(f"scl{L}{n}", KC * 2), 0, KC, 2) for n in "mf"] for L in range(2)]
        gate_mix = [sb(f"gate_mix{L}", D) for L in range(2)]
        gate_ffn = [sb(f"gate_ffn{L}", HALF) for L in range(2)]
        router = [view(sb(f"router{L}", KC * E), 0, KC, E) for L in range(2)]
        rope_cs = view(sb("rope_cs", 2 * XT * 2 * 2 * RF), 0, 2, XT * 2, 2 * RF)
        rope_gain = view(W, 22272, 2, ROPE)
        gqk = sb("gqk", 1)
        stat = sb("stat", 96)
        smal = sb("smal", 64)
        probs = sb("probs", E)
        aff = view(sb("aff", XT * E), 0, XT, E)
        affT = junk[0:E, :]
        at = 18944
        top_v = W[0:E, at:at + CAP]
        top_i = W[0:E, at + CAP:at + 2 * CAP].bitcast(U32)
        slots_i = W[0:E, at + P:at + 2 * P]
        slots_v = W[0:E, at + 2 * P:at + 3 * P]
        row_no = sb("row_no", E, U32)
        gate_e = sb("gate_e", E)
        row_in = [sb(f"row_in{s}", 1, U32) for s in range(2)]
        row_out = sb("row_out", 1, U32)

        xn_dram = nc.dram_tensor("xn_rows", (T, D), F32, kind="Internal").ap()
        mid_dram = nc.dram_tensor("mid_rows", (T, D), F32, kind="Internal").ap()
        parts_dram = [nc.dram_tensor(f"ada_parts{L}", (UNITS, P, BANK), F32, kind="Internal").ap() for L in range(2)]
        out_rows = out.rearrange("a t d -> (a t) d")
        acc_dram = [mid_dram, out_rows]

        w_qb = view(W, 0, QC, HEADS * QK)
        w_kvb = view(W, 4608, KVC, HEADS * (NOPE + VD))
        qlT = view(W, 8704, QC, T)
        kvlT = view(W, 10240, KVC, KEYS)
        krot = view(W, 11776, NT, ROPE)
        rows_in = view(W, 12288, NT, D)
        lat = view(W, 18432, 2, LAT)
        kraw = view(W, 19840, NT, ROPE)
        ktmp = view(W, 20224, 2, XT, 2 * RF)
        kvtok = view(W, 12288, NT, 2 * (NOPE + VD))
        qtok = view(W, 15360, XT, 2 * QK)
        qT = view(W, 16896, 2, T)
        qTr = view(W, 17920, T)
        kT = view(W, 18432, 2, KEYS)
        kTr = view(W, 19968, KEYS)
        prob = view(W, 20736, 2, KEYS)
        first_ada = [view((R[0], W)[u // 2], (u % 2) * KC * BANK, KC, BANK) for u in range(FIRST_UNITS)]
        w_in = view(R[2], 0, KC, LAT)
        hT = view(R[1], 0, KC, KEYS)
        junk_in = view(R[1], 6144, D)
        pT = [view(R[0], j * 3072, NT, T) for j in range(2)]
        sqq = view(R[0], 6144, XT * 2, QK)
        oT = view(R[1], 0, HEADS, T)
        sqk = view(R[1], 4096, NT * 2, NOPE)
        kr_s = view(R[1], 5632, NT, 2 * ROPE)
        q_rot = view(R[1], 6400, XT, 2 * ROPE)
        rtmp = view(R[1], 6912, 4, XT * 2 * 2 * RF)
        mla_out = [view(R[2], h * KC * BANK, KC, BANK) for h in range(2)]
        ada_buf = mla_out[1]
        parts_sb = [view(W, 0, UNITS - FIRST_UNITS, BANK), view(W, 0, UNITS, BANK)]
        w_conv_out = view(W, 0, KC, D)
        w_cb = view(W, 8192, KC, D)
        w_cc = view(R[1], 0, KC, D)
        w_cv = view(R[2], 0, KC, D)
        hT1 = view(R[0], 0, KC, T)
        xnc = view(W, 16384, XT, D)
        zT = view(W, 16384, KC, T)
        c_sb = view(W, 20480, 2, T)
        u_pad = view(W, 21504, T + 2)
        y_sb = ada_part[:, 0, :]
        w_out = [mla_out, [w_conv_out[:, :, h * BANK:(h + 1) * BANK] for h in range(2)]]
        mixT = [oT, zT]
        xres = [view(W, 12288, XT, D), view(R[0], 4096, XT, D)]
        hfT = view(W, 8192, 2, KC * P)
        mo_tmp = view(W, 10240, D)
        hf_tmp = view(W, 11264, D)
        xnt = view(W, 20480, 2, D)
        xs = view(W, 16384, 2, HALF)
        xs_m = view(W, 17408, HALF)
        xsT = view(W, 17920, 2, HALF)
        silu_a = view(W, 18944, BANK)
        hid = view(W, 19456, BANK)
        hidT = view(W, 19968, BANK)
        y_s = view(W, 20480, 2, BANK)
        wg, wu, wd = (view(r, 0, KC, FF) for r in R)
        wg1, wu1 = view(W, 0, KC, FF), view(W, 8192, KC, FF)
        wgs, wds = [wg, wu1], [wg1, wd]

        cond_in, vec_in, misc_in = sem("cond_in"), sem("vec_in"), sem("misc_in")
        rows_in_s = [sem("ctx_in"), sem("x_in")]
        win_in, whead_in = sem("win_in"), sem("whead_in")
        mixw_in = [sem("mla_out_in"), sem("conv_out_in")]
        cc_in, xres_in = sem("cc_in"), sem("xres_in")
        cb_in, cv_in = ([sem(f"{n}_in{h}") for h in range(2)] for n in ("cb", "cv"))
        wg_in, wd_in = ([sem(f"{n}_in{s}") for s in range(2)] for n in ("wg", "wd"))
        wu1_in = sem("wu1_in")
        silu_c, consts, setup_T, setup_out = (sem(n) for n in ("silu_c", "consts", "setup_T", "setup_out"))
        std_in, xn_in, inT, inT_a, inT_d = (sem(n) for n in ("std_in", "xn_in", "inT", "inT_a", "inT_d"))
        ada_in = [sem(f"ada_in{u}") for u in range(4)]
        unit_in, unit_mm, unit_copied, parts_in, out_half_in = (sem(n) for n in (
            "unit_in", "unit_mm", "unit_copied", "parts_in", "out_half_in"))
        unit_stored = [sem("unit_stored0"), sem("unit_stored1")]
        ada_main, ada_rows, ada_sum, ada_out, mod_ready = (sem(n) for n in (
            "ada_main", "ada_rows", "ada_sum", "ada_out", "mod_ready"))
        lat_done, lat_a, lat_d, lat_std, lat_n, latT, latT_d, krot_ready = (sem(n) for n in (
            "lat_done", "lat_a", "lat_d", "lat_std", "lat_n", "latT", "latT_d", "krot_ready"))
        proj, proj_a, proj_d, sq_ready, ss_ready, std_ready, rk_ready, kn_ready, krs_ready = (sem(n) for n in (
            "proj", "proj_a", "proj_d", "sq_ready", "ss_ready", "std_ready", "rk_ready", "kn_ready", "krs_ready"))
        qg_ready, qrot_d, qrot_p, trn, trn_a, trn_d = (sem(n) for n in (
            "qg_ready", "qrot_d", "qrot_p", "trn", "trn_a", "trn_d"))
        s_done, nmax, exp_done, p_norm, pT_done, pT_a, pT_d, pv_done, oT_ready = (sem(n) for n in (
            "s_done", "nmax", "exp_done", "p_norm", "pT_done", "pT_a", "pT_d", "pv_done", "oT_ready"))
        dve_step, act_step, pool_step, turn = sem("dve_step"), sem("act_step"), sem("pool_step"), sem("turn")
        cv_mm, conv_mm, c_copied, z_ready = (sem(n) for n in ("cv_mm", "conv_mm", "c_copied", "z_ready"))

        def layer_sems(*names):
            return [[sem(f"{n}{L}") for L in range(2)] for n in names]

        (mo_done, mo_mul, x_new, x_std, xn_ready, xnT, hf_mul, hf_ready, lg_done, lg_neg, lg_exp, lg_aff,
         affT_ps, affT_sb) = layer_sems("mo_done", "mo_mul", "x_new", "x_std", "xn_ready", "xnT", "hf_mul",
                                        "hf_ready", "lg_done", "lg_neg", "lg_exp", "lg_aff", "affT_ps", "affT_sb")
        acc_stored, xn_st0, xn_st1, slots_f, slots_T, slots_ready = layer_sems(
            "acc_stored", "xn_st0_", "xn_st1_", "slots_f", "slots_T", "slots_ready")
        (wu_in, row_copied, row_out_ok, xs_in0, xs_in1, xs_T, xs_mod, gate_mm, up_mm, silu_ok, hid_ok, hid_T, hidT_ok,
         down_mm, y_ok, scattered) = layer_sems(
            "wu_in", "row_copied", "row_out_ok", "xs_in0_", "xs_in1_", "xs_T", "xs_mod", "gate_mm", "up_mm",
            "silu_ok", "hid_ok", "hid_T", "hidT_ok", "down_mm", "y_ok", "scattered")

        TILES = [CT + t for t in range(XT)] + list(range(CT))
        PARTS = 4
        LOWER, UPPER = range(PARTS // 2), range(PARTS // 2, PARTS)
        U0, U1 = (UNITS - FIRST_UNITS) // PAIRS, UNITS // PAIRS
        UP = U0 + U1
        T_BANKS = [0, 1, 3, 4, 5]
        ADA_BANKS = [2, 6]
        LAT_BANKS = [4, 2]

        PAIR_BANKS = [0, 2, 7, 7, 7]
        K_PARTS = [(0, 8), (8, 2 * NT)]
        PROJ_BANKS = [6, 7, 1, 3]
        BEHIND = {1: 2, 4: 3, 7: 4}
        assert UP == len(PAIR_BANKS)

        def unit_of(i, q):
            return (0, FIRST_UNITS + U0 * i + q) if q < U0 else (1, U1 * i + q - U0)

        LATER = [(0, n) for n in range(FIRST_UNITS, UNITS)] + [(1, n) for n in range(UNITS)]

        def later_units(L):
            return range(FIRST_UNITS, UNITS) if L == 0 else range(UNITS, 2 * UNITS)

        def collect_bank(g):
            return 7 if g < FIRST_UNITS else 6 + g % 2

        block = es.enter_context(nc.Block())

        @block.sync
        def _(sp):
            sp.dma_start(rows_in[:, 0:CT, :], ctx[0].rearrange("(t p) d -> p t d", p=P)).then_inc(rows_in_s[0], 16)
            sp.dma_start(rows_in[:, CT:NT, :], x[0].rearrange("(t p) d -> p t d", p=P)).then_inc(rows_in_s[1], 16)
            for u in range(FIRST_UNITS):
                if u == FIRST_UNITS - 1:
                    sp.wait_ge(vec_in, 16 * 12)
                sp.dma_start(first_ada[u], ada_w[0, :, u * BANK:(u + 1) * BANK].rearrange("(k p) n -> p k n", p=P)
                             ).then_inc(ada_in[u], 16)
            sp.dma_start(w_in, mla_w_in[0].rearrange("(k p) n -> p k n", p=P)).then_inc(win_in, 16)
            for L in range(2):
                sp.dma_start(gate_mix[L], ada_b[L:L + 1, 2 * D:3 * D].to_broadcast([P, D])).then_inc(misc_in, 16)
                for h in range(2):
                    sp.dma_start(gate_ffn[L][64 * h:64 * h + 64, :],
                                  ada_b[L:L + 1, 5 * D + HALF * h:5 * D + HALF * (h + 1)].to_broadcast([64, HALF])
                                  ).then_inc(misc_in, 16)
                sp.dma_start(router[L], router_w[L].rearrange("(k p) e -> p k e", p=P)).then_inc(misc_in, 16)
            for h in range(2):
                sp.dma_start(rope_gain[:, h, :], (mla_q_gain, mla_k_gain)[h][:, NOPE:QK].to_broadcast([P, ROPE])).then_inc(misc_in, 16)
                for m in range(2):
                    sp.dma_start(rope_cs[:, m, :, :].rearrange("p (t h) f -> p t h f", h=2)[:, :, h, :],
                                  rope_in[m].rearrange("(t p) f -> p t f", p=P)).then_inc(misc_in, 16)
            sp.wait_ge(ada_main, FIRST_UNITS)
            sp.dma_start(w_kvb, mla_w_kvb[0].rearrange("(k p) n -> p k n", p=P)).then_inc(whead_in, 16)
            sp.dma_start(w_qb, mla_w_qb[0].rearrange("(k p) n -> p k n", p=P)).then_inc(whead_in, 16)
            sp.wait_ge(lat_done, NT)

            def store_unit(i, q):
                L, n = unit_of(i, q)
                sp.wait_ge(unit_copied, UP * i + q + 1)
                sp.dma_start(parts_dram[L][n], ada_part[:, q % 2, :]).then_inc(unit_stored[q % 2], 16)

            def pair_units(i):
                for q in range(UP):
                    wait(sp, unit_mm, UP * i + q)
                    L, n = unit_of(i, q)
                    sp.dma_start(ada_buf, ada_w[L, :, bass.ds(n * BANK, BANK)].rearrange("(k p) n -> p k n", p=P)
                                 ).then_inc(unit_in, 16)
                    if isinstance(i, int) and i == 0 and q == 2:
                        sp.dma_start(mla_out[0], mla_w_out[0, :, 0:BANK].rearrange("(k p) n -> p k n", p=P)).then_inc(mixw_in[0], 16)
                    if q >= 1:
                        store_unit(i, q - 1)
                    elif not isinstance(i, int):
                        store_unit(i - 1, UP - 1)

            first_then_loop(sp, pair_units, PAIRS)
            store_unit(PAIRS - 1, UP - 1)
            sp.wait_ge(unit_mm, UP * PAIRS)
            sp.dma_start(mla_out[1], mla_w_out[0, :, BANK:D].rearrange("(k p) n -> p k n", p=P)).then_inc(out_half_in, 16)
            sp.wait_ge(unit_stored[0], 16 * 3 * PAIRS)
            sp.wait_ge(unit_stored[1], 16 * 2 * PAIRS)

            def load_parts(L, n0):
                sp.dma_start(parts_sb[L], parts_dram[L][n0:UNITS].rearrange("n p c -> p n c")).then_inc(parts_in, 16)

            sp.wait_ge(proj, 10 * PAIRS)
            load_parts(0, FIRST_UNITS)

            def load_expert(w, dst, L, e, done, parts=range(PARTS)):
                for k in (m * KC // PARTS for m in parts):
                    sp.dma_start(dst[:, k:k + KC // PARTS, :],
                                 w[L, e][k * P:(k + KC // PARTS) * P, :].rearrange("(k p) n -> p k n", p=P)).then_inc(done, 16)

            def stores(L):
                for t in range(XT):
                    if L == 0 and t == XT // 2:
                        sp.wait_ge(ada_sum, 2 * UNITS)
                        load_expert(exp_w_gate, wg1, 0, 1, wg_in[1])
                    if L == 1 and t == XT - 1:
                        sp.wait_ge(mo_done[1], XT)
                        load_expert(exp_w_gate, wg1, 1, 1, wg_in[1])
                    sp.wait_ge(x_new[L], t + 1)
                    sp.dma_start(acc_dram[L][t * P:(t + 1) * P, :], xres[L][:, t, :]).then_inc(acc_stored[L], 16)
                    sp.wait_ge(xn_ready[L], t + 1)
                    sp.dma_start(xn_dram[t * P:(t + 1) * P, :], xnt[:, t % 2, :]).then_inc((xn_st0, xn_st1)[t % 2][L], 16)

            def expert_stream(L):
                def gate(e, s, used, n):
                    sp.wait_ge(used[L], n)
                    load_expert(exp_w_gate, wgs[s], L, e, wg_in[s])

                def up(e, n):
                    sp.wait_ge(up_mm[L], n)
                    load_expert(exp_w_up, wu, L, e, wu_in[L])

                def down(e, s, dst, used, n):
                    sp.wait_ge(used[L], n)
                    load_expert(exp_w_down, dst, L, e, wd_in[s])

                sp.wait_ge(xs_in0[L], 16)
                load_expert(exp_w_up, wu1, L, 1, wu1_in, LOWER)
                gate(2, 0, gate_mm, 1)
                up(2, 1)
                down(1, 1, wds[1], down_mm, 1)
                down(2, 0, wds[0], gate_mm, 2)
                gate(3, 1, up_mm, 2)
                up(3, 3)
                down(3, 1, wds[1], down_mm, 2)
                with sp.Fori(2, E // 2) as i:
                    for s in range(2):
                        gate(2 * i + s, s, gate_mm, 2 * i + s - 1)
                        up(2 * i + s, 2 * i + s)
                        down(2 * i + s, s, wds[s], down_mm, 2 * i + s - 1)

            sp.wait_ge(pv_done, HEADS)
            sp.wait_ge(oT_ready, HEADS)
            sp.dma_start(xres[0], x[0].rearrange("(t p) d -> p t d", p=P)).then_inc(xres_in, 16)
            load_expert(exp_w_gate, wg, 0, 0, wg_in[0])
            sp.wait_ge(ada_sum, UNITS)
            load_parts(1, 0)
            load_expert(exp_w_up, wu, 0, 0, wu_in[0], UPPER)
            stores(0)
            sp.wait_ge(mo_done[0], XT)
            load_expert(exp_w_up, wu, 0, 0, wu_in[0], LOWER)
            load_expert(exp_w_down, wd, 0, 0, wd_in[0])
            sp.wait_ge(acc_stored[0], 16 * XT)
            load_expert(exp_w_up, wu1, 0, 1, wu1_in, UPPER)
            expert_stream(0)

            def load_conv(w, dst, m, h, done):
                sp.dma_start(dst[:, :, h * HALF:(h + 1) * HALF],
                             w[0, :, m * D + h * HALF:m * D + (h + 1) * HALF].rearrange("(k p) n -> p k n", p=P)
                             ).then_inc(done, 16)

            sp.wait_ge(up_mm[0], E)
            for h in range(2):
                load_conv(conv_w_in, w_cc, 1, h, cc_in)
            sp.wait_ge(scattered[0], 16 * E)
            for h in range(2):
                sp.dma_start(xres[1][:, 2 * h:2 * h + 2, :], mid_dram[2 * h * P:(2 * h + 2) * P, :].rearrange("(t p) d -> p t d", p=P)
                             ).then_inc(rows_in_s[h], 16)
            for h in range(2):
                load_conv(conv_w_in, w_cv, 2, h, cv_in[h])
                load_conv(conv_w_in, w_cb, 0, h, cb_in[h])
            sp.dma_start(w_conv_out, conv_w_out[0].rearrange("(k p) n -> p k n", p=P)).then_inc(mixw_in[1], 16)
            sp.wait_ge(conv_mm, KC)
            load_expert(exp_w_up, wu, 1, 0, wu_in[1])
            load_expert(exp_w_down, wd, 1, 0, wd_in[0])
            load_expert(exp_w_gate, wg, 1, 0, wg_in[0], LOWER)
            load_expert(exp_w_up, wu1, 1, 1, wu1_in, UPPER)
            stores(1)
            sp.wait_ge(acc_stored[1], 16 * XT)
            load_expert(exp_w_gate, wg, 1, 0, wg_in[0], UPPER)
            expert_stream(1)
            sp.wait_ge(scattered[1], 16 * E)

        @block.tensor
        def _(pe):
            mm, tr = nc.tensor.matmul, nc.tensor.transpose

            def ada_product(u):
                b = ADA_BANKS[u % 2]
                pe.wait_ge(ada_in[u], 16)
                if u >= 2:
                    pe.wait_ge(ada_rows, u - 1)
                for kk in range(2):
                    for g in range(4):
                        k = 2 * g + kk
                        last = mm(PS[32 * g:32 * g + 32, b, :], cond_T[:, k, :], first_ada[u][:, k, :], start=kk == 0, stop=kk == 1)
                last.then_inc(ada_main, 1)

            def ada_collect(g):
                L, n = (0, g) if g < FIRST_UNITS else LATER[g - FIRST_UNITS]
                kind, half, b = n // 2, n % 2, collect_bank(g)
                if g < FIRST_UNITS:
                    pe.wait_ge(ada_rows, g + 1)
                    part = ada_part[:, g % 2, :]
                    if g >= 1:
                        pe.wait_ge(ada_out, g)
                else:
                    pe.wait_ge(parts_in, 16 * (L + 1))
                    part = parts_sb[L][:, n - (0 if L else FIRST_UNITS), :]
                    pe.wait_ge(ada_out, g - 1)
                if kind == 2:
                    last = mm(PS[:, b, :], selx, part, start=True, stop=True)
                elif kind == 5:
                    last = mm(PS[64 * half:64 * half + 64, b, :], selx[:, 0:64], part, start=True, stop=True)
                else:
                    for q in range(4):
                        last = mm(PS[:, b, 2 * q:2 * q + 2], part[:, q * P:(q + 1) * P], sel2, start=True, stop=True)
                last.then_inc(ada_sum, 1)

            pe.wait_ge(cond_in, 48)
            pe.wait_ge(silu_c, 1)
            tr(PS[:, 7, 0:2 * KC], cond_rows[0:2 * KC, :], ident[0:2 * KC, 0:2 * KC]).then_inc(setup_T, 1)

            def input_T(g):
                b = T_BANKS[g % 5]
                if g >= 5:
                    pe.wait_ge(inT_a, g - 4)
                for q in range(4):
                    k, t = (g, CT + q) if g < KC else (2 * (g - KC) + q // 2, q % 2)
                    last = tr(PS[:, b, q * P:(q + 1) * P], rows_in[:, t, k * P:(k + 1) * P], ident)
                last.then_inc(inT, 1)

            pe.wait_ge(setup_out, 1)
            ada_product(0)
            ada_product(1)
            pe.wait_ge(xn_in, NT)
            for g in range(5):
                input_T(g)
            pe.wait_ge(vec_in, 16 * 12)
            tr(PS[:, 7, P:P + NR], vec_rows[0:NR, :], ident[0:NR, 0:NR]).then_inc(setup_T, 1)
            pe.wait_ge(consts, 4)
            pe.wait_ge(setup_out, 2)
            for u in range(2, FIRST_UNITS):
                ada_collect(u - 2)
                ada_product(u)
            for u in range(FIRST_UNITS - 2, FIRST_UNITS):
                ada_collect(u)
            for g in range(5, 12):
                input_T(g)

            pe.wait_ge(win_in, 16)
            pe.wait_ge(inT_a, KC)
            pe.wait_ge(inT_d, 4)

            def low_rank(n):
                j, b0 = TILES[n], LAT_BANKS[n % 2]
                if n >= 2:
                    pe.wait_ge(lat_a, n - 1)
                    pe.wait_ge(lat_d, min(n - 1, XT))
                cuts = [(b0, 0, BANK), (b0 + 1, BANK, LAT)] if j >= CT else [(b0, QL, LAT)]
                for b, lo, hi in cuts:
                    for k in range(KC):
                        last = mm(PS[:, b, 0:hi - lo], hT[:, k, j * P:(j + 1) * P], w_in[:, k, lo:hi],
                                  start=k == 0, stop=k == KC - 1)
                last.then_inc(lat_done, 1)

            def low_rank_T(n):
                pe.wait_ge(lat_n, n + 1)
                if n >= 1:
                    pe.wait_ge(latT_d, n)
                if TILES[n] >= CT:
                    for q in range(QC):
                        tr(PS[:, 0, q * P:(q + 1) * P], lat[:, n % 2, q * P:(q + 1) * P], ident)
                for q in range(KVC):
                    last = tr(PS[:, 1, q * P:(q + 1) * P], lat[:, n % 2, QL + q * P:QL + (q + 1) * P], ident)
                last.then_inc(latT, 1)

            for n in range(NT + 1):
                if n < NT:
                    low_rank(n)
                if n >= 1:
                    low_rank_T(n - 1)

            pe.wait_ge(latT_d, NT)
            pe.wait_ge(krot_ready, 1)
            pe.wait_ge(whead_in, 32)
            pe.wait_ge(ada_rows, FIRST_UNITS)
            pe.wait_ge(ada_out, FIRST_UNITS)
            def pair(i):
                def unit(q):
                    pe.wait_ge(unit_in, 16 * (UP * i + q + 1))
                    if q >= 3:
                        pe.wait_ge(unit_copied, UP * i + q)
                    for kk in range(2):
                        for g in range(4):
                            k = 2 * g + kk
                            last = mm(PS[32 * g:32 * g + 32, PAIR_BANKS[q], :], cond_T[:, k, :], ada_buf[:, k, :],
                                      start=kk == 0, stop=kk == 1)
                    last.then_inc(unit_mm, 1)

                for s in range(XT + NT):
                    if s == XT - 1:
                        unit(0)
                    b = PROJ_BANKS[s % 4]
                    if s < 2:
                        wait(pe, oT_ready, 2 * i)
                    elif s >= 4 and s % 2 == 0:
                        pe.wait_ge(proj_a, 5 * i + s // 2 - 1)
                    elif s >= 4:
                        pe.wait_ge(proj_d, 5 * i + s // 2 - 1)
                    if s >= XT:
                        for q in range(KVC):
                            last = mm(PS[:, b, :], kvlT[:, q, (s - XT) * P:(s - XT + 1) * P],
                                      w_kvb[:, q, bass.ds(i * BANK, BANK)], start=q == 0, stop=q == KVC - 1)
                    else:
                        for q in range(QC):
                            last = mm(PS[:, b, 0:2 * QK], qlT[:, q, s * P:(s + 1) * P],
                                      w_qb[:, q, bass.ds(i * 2 * QK, 2 * QK)], start=q == 0, stop=q == QC - 1)
                    last.then_inc(proj, 1)
                groups = ([[qtok[:, t, h * QK:h * QK + P] for t in range(XT)] for h in range(2)]
                          + [[q_rot[:, t, :] for t in range(XT)]]
                          + [[kvtok[:, t, 256 * h:256 * h + P] for t in range(4)] for h in range(2)]
                          + [[kvtok[:, 4 + q % 2, 256 * (q // 2):256 * (q // 2) + P] for q in range(4)]]
                          + [[kr_s[:, t, :] for t in range(4)]]
                          + [[kr_s[:, t, :] for t in range(4, 6)]])
                unit(1)
                for g, srcs in enumerate(groups):
                    if g == 0:
                        pe.wait_ge(qg_ready, i + 1)
                    if g == 2:
                        pe.wait_ge(qrot_d, i + 1)
                        pe.wait_ge(qrot_p, i + 1)
                    if g == 3:
                        pe.wait_ge(kn_ready, 2 * i + 1)
                    if g == 5:
                        pe.wait_ge(kn_ready, 2 * i + 2)
                    if g == 6:
                        pe.wait_ge(krs_ready, i + 1)
                    if g >= 2:
                        pe.wait_ge((trn_a, trn_d)[g % 2], 4 * i + g // 2)
                    for q, src in enumerate(srcs):
                        last = tr(PS[:, 4 + g % 2, q * P:(q + 1) * P], src, ident)
                    last.then_inc(trn, 1)

                def scores(r):
                    j, t = r // XT, r % XT
                    if r == 0:
                        pe.wait_ge(trn_a, 4 * i + 4)
                        pe.wait_ge(trn_d, 4 * i + 4)
                    if r >= 2:
                        pe.wait_ge(exp_done, 8 * i + r - 1)
                    else:
                        pe.wait_ge(unit_copied, UP * i + r + 1)
                    for h in range(2):
                        o = PS[:, 2 * (r % 2) + h, 0:SCR]
                        mm(o, qT[:, j, t * P:(t + 1) * P], kT[:, j, h * SCR:(h + 1) * SCR], start=True, stop=False)
                        last = mm(o, qTr[64 * j:64 * j + 64, t * P:(t + 1) * P],
                                  kTr[64 * j:64 * j + 64, h * SCR:(h + 1) * SCR], start=False, stop=True)
                    last.then_inc(s_done, 1)

                def probs_T(r):
                    pe.wait_ge(p_norm, 8 * i + r + 1)
                    wait(pe, pT_a, 8 * i + r)
                    wait(pe, pT_d, 8 * i + r)
                    for q in range(NT):
                        last = tr(PS[:, 4 + q // 4, (q % 4) * P:(q % 4 + 1) * P], prob[:, r % 2, q * P:(q + 1) * P], ident)
                    last.then_inc(pT_done, 1)

                def values(j):
                    if j == 1:
                        pe.wait_ge(unit_copied, UP * i + UP)
                    pe.wait_ge(pT_a, 8 * i + 4 * j + 4)
                    pe.wait_ge(pT_d, 8 * i + 4 * j + 4)
                    for q in range(NT):
                        last = mm(PS[:, 6 + j, :], kvtok[:, q, 256 * j + NOPE:256 * j + NOPE + VD], pT[j][:, q, :],
                                  start=q == 0, stop=q == NT - 1)
                    last.then_inc(pv_done, 1)

                for r in range(2 * XT):
                    scores(r)
                    if r >= 1:
                        probs_T(r - 1)
                    if r in BEHIND:
                        unit(BEHIND[r])
                    if r == 5:
                        values(0)
                probs_T(2 * XT - 1)
                values(1)

            first_then_loop(pe, pair, PAIRS)

            def mixer_out(L):
                pe.wait_ge(mixw_in[L], 16)
                if L == 0:
                    pe.wait_ge(oT_ready, HEADS)
                else:
                    pe.wait_ge(z_ready, KC)
                for t in range(XT + 3):
                    if t < XT:
                        if t >= 2:
                            pe.wait_ge(x_std[L], t - 1)
                        for h in range(2):
                            if L == 0 and t == 0 and h == 1:
                                pe.wait_ge(out_half_in, 16)
                            for k in range(KC):
                                last = mm(PS[:, 2 * (t % 2) + h, :], mixT[L][:, k, t * P:(t + 1) * P],
                                          w_out[L][h][:, k, :], start=k == 0, stop=k == KC - 1)
                        last.then_inc(mo_done[L], 1)
                    if L == 0 and t < 2:
                        for g in later_units(t):
                            ada_collect(g)
                    if 1 <= t <= XT:
                        v = t - 1
                        pe.wait_ge(xn_ready[L], v + 1)
                        pe.wait_ge(hf_mul[L], v)
                        for k in range(KC):
                            last = tr(PS[:, 4 + k // 4, (k % 4) * P:(k % 4 + 1) * P], xnt[:, v % 2, k * P:(k + 1) * P], ident)
                        last.then_inc(xnT[L], 1)
                    if 2 <= t <= XT + 1:
                        v = t - 2
                        pe.wait_ge(hf_ready[L], v + 1)
                        pe.wait_ge(lg_exp[L], v)
                        for k in range(KC):
                            last = mm(PS[:, 6, 0:E], hfT[:, v % 2, k * P:(k + 1) * P], router[L][:, k, :],
                                      start=k == 0, stop=k == KC - 1)
                        last.then_inc(lg_done[L], 1)
                    if 3 <= t:
                        v = t - 3
                        pe.wait_ge(lg_aff[L], v + 1)
                        pe.wait_ge(affT_sb[L], v)
                        tr(PS[0:E, 7, 0:P], aff[:, v, :], ident).then_inc(affT_ps[L], 1)
                pe.wait_ge(slots_f[L], 1)
                tr(PS[:, 7, 0:E], slots_i, ident[0:E, 0:E])
                tr(PS[:, 7, E:2 * E], slots_v, ident[0:E, 0:E]).then_inc(slots_T[L], 1)

            def experts(L):
                def rows_T(i, s):
                    pe.wait_ge((xs_in0, xs_in1)[s][L], 16 * i + 16)
                    wait(pe, xs_mod[L], 2 * i + s)
                    for q in range(4):
                        last = tr(PS[:, 4, q * P:(q + 1) * P], xs[:, s, q * P:(q + 1) * P], ident)
                    last.then_inc(xs_T[L], 1)

                def halves(bank, lhsT, w, done):
                    for k in range(KC):
                        lhs = lhsT[:, (k % 4) * P + 64 * (k // 4):(k % 4) * P + 64 * (k // 4) + 64]
                        for h in range(2):
                            last = mm(PS[64 * h:64 * h + 64, bank, :], lhs, w[:, k, h * BANK:(h + 1) * BANK],
                                      start=k == 0, stop=k == KC - 1)
                    last.then_inc(done, 1)

                def two_experts(i):
                    for s in range(2):
                        e = 2 * i + s
                        pe.wait_ge(xs_mod[L], e + 1)
                        first = isinstance(i, int) and i == 0
                        loads = 16 * PARTS * (L * E // 2 + 1) + 16 * PARTS * i
                        pe.wait_ge(wg_in[s], loads)
                        wait(pe, silu_ok[L], e)
                        halves(0, xsT[:, s, :], (wg, wg1)[s] if first else wgs[s], gate_mm[L])
                        if first and s == 1:
                            pe.wait_ge(wu1_in, 16 * PARTS * (L + 1))
                        elif first:
                            pe.wait_ge(wu_in[L], 16 * PARTS)
                        else:
                            pe.wait_ge(wu_in[L], 16 * PARTS * e)
                        wait(pe, hid_ok[L], e)
                        halves(1, xsT[:, s, :], wu1 if first and s == 1 else wu, up_mm[L])
                        if not (isinstance(e, int) and e == E - 1):
                            rows_T(i + s, 1 - s)
                        pe.wait_ge(hid_ok[L], e + 1)
                        wait(pe, hidT_ok[L], e)
                        for q in range(4):
                            last = tr(PS[:, 3, q * P:(q + 1) * P], hid[:, q * P:(q + 1) * P], ident)
                        last.then_inc(hid_T[L], 1)
                        pe.wait_ge(wd_in[s], loads)
                        pe.wait_ge(hidT_ok[L], e + 1)
                        wait(pe, y_ok[L], e)
                        halves(2, hidT, wd if first else wds[s], down_mm[L])

                rows_T(0, 0)
                first_then_loop(pe, two_experts, E // 2, last=1)

            mixer_out(0)
            experts(0)

            pe.wait_ge(xn_in, NT + XT)
            for g in range(KC):
                if g >= 4:
                    pe.wait_ge(inT_a, KC + g - 3)
                for t in range(XT):
                    last = tr(PS[:, g % 4, t * P:(t + 1) * P], xnc[:, t, g * P:(g + 1) * P], ident)
                last.then_inc(inT, 1)
            pe.wait_ge(inT_a, 2 * KC)
            pe.wait_ge(cc_in, 32)
            for n in range(KC):
                if n >= 2:
                    pe.wait_ge(z_ready, n - 1)
                for m, w in ((1, w_cc), (2, w_cv), (0, w_cb)):
                    if n % 4 == 0 and m != 1:
                        pe.wait_ge((cv_in if m == 2 else cb_in)[n // 4], 16)
                    for k in range(KC):
                        last = mm(PS[:, 3 * (n % 2) + m, :], w[:, k, n * P:(n + 1) * P], hT1[:, k, :],
                                  start=k == 0, stop=k == KC - 1)
                    if m == 2:
                        last.then_inc(cv_mm, 1)
                last.then_inc(conv_mm, 1)

            mixer_out(1)
            experts(1)

        @block.scalar
        def _(act):
            f = nc.scalar.activation
            own = Chain(act, act_step)
            act.dma_start(cond_rows[0:KC, :], c.rearrange("a (k p) -> (a k) p", p=P)).then_inc(cond_in, 16)
            act.dma_start(cond_rows[KC:2 * KC, :], c_ctx.rearrange("(k p) -> k p", p=P)).then_inc(cond_in, 16)
            act.dma_start(ident, ident_in).then_inc(cond_in, 16)
            vecs = [(V_NM, norm_mix.rearrange("a (k p) -> (a k) p", p=P)), (V_NF, norm_ffn.rearrange("a (k p) -> (a k) p", p=P)),
                    (V_QN, mla_q_norm.rearrange("a (k p) -> (a k) p", p=P)), (V_KVN, mla_kv_norm.rearrange("a (k p) -> (a k) p", p=P)),
                    (V_GQ, mla_q_gain[:, 0:NOPE]), (V_GK, mla_k_gain[:, 0:NOPE]),
                    (V_CONV, conv_w.rearrange("a j (k p) -> (a j k) p", p=P))]
            for L in range(2):
                for m in range(2):
                    vecs.append((V_ADA + 32 * L + 16 * m,
                                 ada_b[L, 3 * D * m:3 * D * m + 2 * D].rearrange("(k p) -> k p", p=P)))
            for lo, src in vecs:
                act.dma_start(vec_rows[lo:lo + src.shape[0], :], src).then_inc(vec_in, 16)
            act.dma_start(vec_rows[NR:P, :], ident_in[0:1, :]).then_inc(vec_in, 16)
            act.wait_ge(cond_in, 48)
            f(cond_rows[0:2 * KC, :], cond_rows[0:2 * KC, :], ACT.Silu).then_inc(silu_c, 1)
            act.wait_ge(rows_in_s[0], 16)
            for j in range(NT):
                if j == CT:
                    act.wait_ge(rows_in_s[1], 16)
                own.link(f(junk_in, rows_in[:, j, :], ACT.Square, accum_out=stat[:, j:j + 1]))
            act.wait_ge(consts, 3)
            f(stat[:, 8:8 + NT], stat[:, 0:NT], ACT.Sqrt, bias=eps, scale=1.0 / D).then_inc(std_in, 1)

            def ada_copy(u):
                act.wait_ge(ada_main, u + 1)
                if u >= 2:
                    act.wait_ge(ada_sum, u - 1)
                f(ada_part[:, u % 2, :], PS[:, ADA_BANKS[u % 2], :], ACT.Copy).then_inc(ada_rows, 1)

            for u in range(FIRST_UNITS):
                ada_copy(u)
            act.wait_ge(mod_ready, 1)
            for g in range(KC):
                act.wait_ge(inT, g + 1)
                f(hT[:, g, CX:KEYS], PS[:, T_BANKS[g % 5], :], ACT.Identity, bias=modv[0][0][:, 0, g, 0:1],
                  scale=scl[0][0][:, g, 0:1]).then_inc(inT_a, 1)
            for n, j in enumerate(TILES):
                act.wait_ge(lat_done, n + 1)
                if n >= 2:
                    act.wait_ge(latT, n - 1)
                if j >= CT:
                    own.link(f(lat[:, n % 2, 0:BANK], PS[:, LAT_BANKS[n % 2], :], ACT.Copy))
                    act.sem_inc(lat_a, 1)
                    act.wait_ge(lat_d, n + 1)
                    own.link(f(junk_in[:, 0:QL], lat[:, n % 2, 0:QL], ACT.Square, accum_out=stat[:, 16 + j:17 + j]))
                else:
                    own.link(f(lat[:, n % 2, QL:LAT], PS[:, LAT_BANKS[n % 2], 0:LAT - QL], ACT.Copy))
                    act.sem_inc(lat_a, 1)
                own.link(f(junk_in[:, 0:KVL], lat[:, n % 2, QL:QL + KVL], ACT.Square, accum_out=stat[:, 24 + j:25 + j]))
                own.link(f(junk_in[:, 0:ROPE], lat[:, n % 2, QL + KVL:LAT], ACT.Square, accum_out=stat[:, 32 + j:33 + j]))
                if j >= CT:
                    f(stat[:, 40 + j:41 + j], stat[:, 16 + j:17 + j], ACT.Sqrt, bias=eps, scale=1.0 / QL)
                f(stat[:, 48 + j:49 + j], stat[:, 24 + j:25 + j], ACT.Sqrt, bias=eps, scale=1.0 / KVL).then_inc(lat_std, 1)

            act.wait_ge(lat_n, NT)
            def pair(i):
                def copy_unit(q):
                    act.wait_ge(unit_mm, UP * i + q + 1)
                    wait(act, unit_stored[q % 2], 16 * ((3, 2)[q % 2] * i + q // 2))
                    f(ada_part[:, q % 2, :], PS[:, PAIR_BANKS[q], :], ACT.Copy).then_inc(unit_copied, 1)

                def take(s):
                    act.wait_ge(proj, 10 * i + s + 1)
                    dst = qtok[:, s, :] if s < XT else kvtok[:, s - XT, :]
                    f(dst, PS[:, PROJ_BANKS[s % 4], 0:dst.shape[1]], ACT.Copy).then_inc(proj_a, 1)

                take(0)
                take(2)
                act.wait_ge(proj_a, 5 * i + 2)
                act.wait_ge(proj_d, 5 * i + 2)
                f(sqq, qtok.rearrange("p t (h n) -> p (t h) n", h=2), ACT.Square).then_inc(sq_ready, 1)
                take(4)
                act.wait_ge(ss_ready, 3 * i + 1)
                f(smal[:, 40:48], smal[:, 32:40], ACT.Sqrt, bias=eps, scale=1.0 / QK).then_inc(std_ready, 1)
                copy_unit(0)
                take(6)

                def square_k(m):
                    act.wait_ge(proj_a, 5 * i + 4 + m)
                    act.wait_ge(proj_d, 5 * i + 4 + m)
                    lo, hi = K_PARTS[m]
                    f(sqk[:, lo:hi, :], kvtok.rearrange("p t (h n) -> p (t h) n", h=2)[:, lo:hi, 0:NOPE],
                      ACT.Square).then_inc(sq_ready, 1)

                def root_k(m):
                    act.wait_ge(ss_ready, 3 * i + 2 + m)
                    lo, hi = K_PARTS[m]
                    f(smal[:, 16 + lo:16 + hi], smal[:, lo:hi], ACT.Sqrt, bias=eps, scale=1.0 / QK).then_inc(std_ready, 1)

                square_k(0)
                take(8)
                root_k(0)
                square_k(1)
                root_k(1)
                copy_unit(1)
                for g in (0, 2, 4, 6):
                    act.wait_ge(trn, 8 * i + g + 1)
                    if g == 0:
                        ins = f(qT[:, 0, :], PS[:, 4, :], ACT.Copy, scale=gqk)
                    elif g == 2:
                        ins = f(qTr, PS[:, 4, :], ACT.Copy)
                    elif g == 4:
                        ins = f(kT[:, 1, 0:BANK], PS[:, 4, :], ACT.Copy)
                    else:
                        ins = f(kTr[:, 0:BANK], PS[:, 4, :], ACT.Copy)
                    ins.then_inc(trn_a, 1)

                def take_pT(r):
                    act.wait_ge(pT_done, 8 * i + r + 1)
                    f(pT[r // XT][:, 0:4, (r % XT) * P:(r % XT + 1) * P], PS[:, 4, :].rearrange("p (a b) -> p a b", a=4),
                      ACT.Copy).then_inc(pT_a, 1)

                def take_o(j):
                    act.wait_ge(pv_done, 2 * i + j + 1)
                    f(oT[:, bass.ds(2 * i + j, 1), :].rearrange("p a t -> p (a t)"), PS[:, 6 + j, :], ACT.Copy).then_inc(oT_ready, 1)

                for r in range(2 * XT):
                    if r == 6:
                        take_o(0)
                    if r >= 1:
                        take_pT(r - 1)
                    act.wait_ge(nmax, 8 * i + r + 1)
                    f(prob[:, r % 2, :].rearrange("p (a b) -> p a b", a=2), PS[:, 2 * (r % 2):2 * (r % 2) + 2, 0:SCR], ACT.Exp,
                      bias=stat[:, 64 + r % 2:65 + r % 2], scale=SCALE,
                      accum_out=stat[:, 68 + r % 2:69 + r % 2]).then_inc(exp_done, 1)
                    if r in BEHIND:
                        copy_unit(BEHIND[r])
                take_pT(2 * XT - 1)
                take_o(1)

            first_then_loop(act, pair, PAIRS)

            def router_part(L):
                for t in range(XT + 2):
                    if t < XT:
                        act.wait_ge(x_new[L], t + 1)
                        own.link(f(PS[:, 2 * (t % 2):2 * (t % 2) + 2, :], xres[L][:, t, :].rearrange("p (a b) -> p a b", a=2), ACT.Square, accum_out=stat[:, t:t + 1]))
                        f(stat[:, 8 + t:9 + t], stat[:, t:t + 1], ACT.Sqrt, bias=eps, scale=1.0 / D).then_inc(x_std[L], 1)
                    if t >= 2:
                        v = t - 2
                        act.wait_ge(lg_neg[L], v + 1)
                        f(probs, PS[:, 6, 0:E], ACT.Exp, bias=stat[:, 16:17], accum_out=stat[:, 17:18]).then_inc(lg_exp[L], 1)

            def experts(L):
                def expert(e):
                    act.wait_ge(gate_mm[L], e + 1)
                    wait(act, hid_ok[L], e)
                    f(silu_a, PS[:, 0, :], ACT.Silu).then_inc(silu_ok[L], 1)
                    act.wait_ge(hid_T[L], e + 1)
                    wait(act, down_mm[L], e)
                    f(hidT, PS[:, 3, :], ACT.Copy).then_inc(hidT_ok[L], 1)

                first_then_loop(act, expert, E)

            router_part(0)
            experts(0)

            f(stat[:, 95:96], eps, ACT.Sqrt)
            for h in range(2):
                act.wait_ge(rows_in_s[h], 32)
                for t in (2 * h, 2 * h + 1):
                    own.link(f(junk, xres[1][:, t, :], ACT.Square, accum_out=stat[:, t:t + 1]))
                f(stat[:, 8 + 2 * h:10 + 2 * h], stat[:, 2 * h:2 * h + 2], ACT.Sqrt, bias=eps, scale=1.0 / D).then_inc(std_in, 1)
            for g in range(KC):
                act.wait_ge(inT, 12 + g + 1)
                f(hT1[:, g, :], PS[:, g % 4, :], ACT.Identity, bias=modv[1][0][:, 0, g, 0:1],
                  scale=scl[1][0][:, g, 0:1]).then_inc(inT_a, 1)
            for n in range(KC):
                act.wait_ge(cv_mm, n + 1)
                if n >= 2:
                    act.wait_ge(z_ready, n - 1)
                f(c_sb[:, n % 2, :], PS[:, 3 * (n % 2) + 1, :], ACT.Copy).then_inc(c_copied, 1)
            act.wait_ge(z_ready, KC)
            router_part(1)
            experts(1)

        @block.vector
        def _(dve):
            v = nc.vector
            own = Chain(dve, dve_step)
            v.memset(cond_T, 0.0).then_inc(consts, 1)
            v.memset(eps, EPS).then_inc(consts, 1)
            dve.wait_ge(cond_in, 48)
            v.tensor_reduce(sel2, ident.rearrange("p (a b) -> p b a", a=4)[:, 0:2, :], AX.X, ALU.add).then_inc(consts, 1)
            dve.wait_ge(consts, 3)
            v.tensor_copy(selx, sel2[:, 0:1].to_broadcast([P, P])).then_inc(consts, 1)
            dve.wait_ge(setup_T, 1)
            v.tensor_copy(cond_T[:, :, 0:2], PS[:, 7, 0:2 * KC].rearrange("p (r k) -> p k r", r=2)).then_inc(setup_out, 1)
            dve.wait_ge(std_in, 1)
            own.link(v.reciprocal(stat[:, 8:8 + NT], stat[:, 8:8 + NT]))
            for j in range(NT):
                v.tensor_scalar(rows_in[:, j, :], rows_in[:, j, :], stat[:, 8 + j:9 + j], None, ALU.mult).then_inc(xn_in, 1)
            dve.wait_ge(setup_T, 2)
            v.tensor_copy(vec[:, 0:NR], PS[:, 7, P:P + NR]).then_inc(setup_out, 1)
            dve.wait_ge(setup_out, 2)
            own.link(v.tensor_tensor(gqk, vec[:, V_GQ:V_GQ + 1], vec[:, V_GK:V_GK + 1], ALU.mult))

            def col(lo, n, m):
                return vec[:, lo:lo + n].unsqueeze(2).to_broadcast([P, n, m])

            def ada_take(u):
                L, num = (0, u) if u < FIRST_UNITS else LATER[u - FIRST_UNITS]
                n, half, b = num // 2, num % 2, collect_bank(u)
                dve.wait_ge(ada_sum, u + 1)
                if n == 2:
                    g = gate_mix[L][:, half * BANK:(half + 1) * BANK]
                    v.tensor_tensor(g, PS[:, b, :], g, ALU.add).then_inc(ada_out, 1)
                elif n == 5:
                    g = gate_ffn[L][64 * half:64 * half + 64, :]
                    v.tensor_tensor(g, PS[64 * half:64 * half + 64, b, :], g, ALU.add).then_inc(ada_out, 1)
                else:
                    m, kind = n // 3, n % 3
                    v.tensor_tensor(modv[L][m][:, kind, 4 * half:4 * half + 4, :],
                                    PS[:, b, 0:8].rearrange("p (k r) -> p k r", r=2),
                                    col(V_ADA + 32 * L + 16 * m + KC * kind + 4 * half, 4, 2), ALU.add).then_inc(ada_out, 1)
                    if kind == 1 and half == 1:
                        dve.wait_ge(ada_out, u + 1)
                        v.scalar_tensor_tensor(out=scl[L][m], in0=modv[L][m][:, 1], scalar=1.0,
                                               in1=col((V_NM, V_NF)[m] + KC * L, KC, 2), op0=ALU.add,
                                               op1=ALU.mult).then_inc(mod_ready, 1)

            for u in range(FIRST_UNITS):
                ada_take(u)
            dve.wait_ge(mod_ready, 1)
            for g in range(KC, 12):
                dve.wait_ge(inT, g + 1)
                for q in range(2):
                    k = 2 * (g - KC) + q
                    last = v.tensor_scalar(hT[:, k, 0:CX], PS[:, T_BANKS[g % 5], q * CX:(q + 1) * CX],
                                           scl[0][0][:, k, 1:2], modv[0][0][:, 0, k, 1:2], ALU.mult, ALU.add)
                last.then_inc(inT_d, 1)
            for n, j in enumerate(TILES):
                row = lat[:, n % 2, :]
                if j >= CT:
                    dve.wait_ge(lat_done, n + 1)
                    if n >= 2:
                        dve.wait_ge(latT, n - 1)
                    v.tensor_copy(row[:, BANK:LAT], PS[:, LAT_BANKS[n % 2] + 1, 0:LAT - BANK]).then_inc(lat_d, 1)
                dve.wait_ge(lat_std, n + 1)
                v.tensor_copy(kraw[:, j, :], row[:, QL + KVL:LAT])
                own.link(v.reciprocal(stat[:, 48 + j:49 + j], stat[:, 48 + j:49 + j]))
                last = v.tensor_scalar(row[:, QL:QL + KVL], row[:, QL:QL + KVL], stat[:, 48 + j:49 + j], None, ALU.mult)
                if j >= CT:
                    own.link(v.reciprocal(stat[:, 40 + j:41 + j], stat[:, 40 + j:41 + j]))
                    last = v.tensor_scalar(row[:, 0:QL], row[:, 0:QL], stat[:, 40 + j:41 + j], None, ALU.mult)
                last.then_inc(lat_n, 1)
                dve.wait_ge(latT, n + 1)
                if j >= CT:
                    v.tensor_tensor(qlT[:, :, (j - CT) * P:(j - CT + 1) * P],
                                    PS[:, 0, 0:QL].rearrange("p (a b) -> p a b", b=P), col(V_QN, QC, P), ALU.mult)
                v.tensor_tensor(kvlT[:, :, j * P:(j + 1) * P], PS[:, 1, 0:KVL].rearrange("p (a b) -> p a b", b=P),
                                col(V_KVN, KVC, P), ALU.mult).then_inc(latT_d, 1)

            dve.wait_ge(latT_d, NT)
            dve.wait_ge(misc_in, 16 * 14)
            own.link(v.tensor_tensor(krot, kraw, rope_gain[:, 1:2, :].to_broadcast([P, NT, ROPE]), ALU.mult))
            k4 = krot[:, CT:NT, :].rearrange("p t (a b f) -> p t a b f", a=2, b=2)
            k1, k2 = k4[:, :, :, 0, :], k4[:, :, :, 1, :]
            cs = [rope_cs[:, m, :, :].rearrange("p (t h) (a f) -> p t h a f", h=2, a=2)[:, :, 0] for m in range(2)]
            r4 = kraw[:, CT:NT, :].rearrange("p t (a b f) -> p t a b f", a=2, b=2)
            tm = [ktmp[:, m].rearrange("p t (a f) -> p t a f", a=2) for m in range(2)]
            v.tensor_tensor(tm[0], k1, cs[0], ALU.mult)
            own.link(v.tensor_tensor(tm[1], k2, cs[1], ALU.mult))
            own.link(v.tensor_tensor(r4[:, :, :, 0, :], tm[0], tm[1], ALU.subtract))
            v.tensor_tensor(tm[0], k2, cs[0], ALU.mult)
            own.link(v.tensor_tensor(tm[1], k1, cs[1], ALU.mult))
            own.link(v.tensor_tensor(r4[:, :, :, 1, :], tm[0], tm[1], ALU.add))
            v.tensor_copy(krot[:, CT:NT, :], kraw[:, CT:NT, :]).then_inc(krot_ready, 1)
            dve.wait_ge(krot_ready, 1)

            base = own.n
            STEPS_IN_PAIR = 5 + 4 * XT
            def pair(i):
                def take(s):
                    dve.wait_ge(proj, 10 * i + s + 1)
                    dst = qtok[:, s, :] if s < XT else kvtok[:, s - XT, :]
                    v.tensor_copy(dst, PS[:, PROJ_BANKS[s % 4], 0:dst.shape[1]]).then_inc(proj_d, 1)

                own.n = base + STEPS_IN_PAIR * i
                take(1)
                take(3)
                dve.wait_ge(sq_ready, 3 * i + 1)
                v.tensor_reduce(smal[:, 32:40], sqq, AX.X, ALU.add).then_inc(ss_ready, 1)
                take(5)
                dve.wait_ge(std_ready, 3 * i + 1)
                own.link(v.reciprocal(smal[:, 40:48], smal[:, 40:48]))
                q8 = qtok.rearrange("p t (h n) -> p (t h) n", h=2)
                own.link(v.tensor_tensor(q8, q8, smal[:, 40:48].unsqueeze(2).to_broadcast([P, 8, QK]), ALU.mult))
                qr = q8[:, :, NOPE:QK]
                v.tensor_tensor(qr, qr, rope_gain[:, 0:1, :].to_broadcast([P, 8, ROPE]), ALU.mult).then_inc(qg_ready, 1)
                take(7)
                dve.wait_ge(qg_ready, i + 1)
                q5 = qr.rearrange("p t (a b f) -> p t a b f", a=2, b=2)
                o5 = q_rot.rearrange("p t (h n) -> p (t h) n", h=2).rearrange("p t (a b f) -> p t a b f", a=2, b=2)
                c8 = [rope_cs[:, m].rearrange("p t (a f) -> p t a f", a=2) for m in range(2)]
                t8 = [rtmp[:, m].rearrange("p (t a f) -> p t a f", a=2, f=RF) for m in range(2)]
                v.tensor_tensor(t8[0], q5[:, :, :, 0, :], c8[0], ALU.mult)
                own.link(v.tensor_tensor(t8[1], q5[:, :, :, 1, :], c8[1], ALU.mult))
                v.tensor_tensor(o5[:, :, :, 0, :], t8[0], t8[1], ALU.subtract).then_inc(qrot_d, 1)

                def sum_k(m):
                    lo, hi = K_PARTS[m]
                    ss = smal[:, lo:hi]
                    dve.wait_ge(sq_ready, 3 * i + 2 + m)
                    own.link(v.tensor_reduce(ss, sqk[:, lo:hi, :], AX.X, ALU.add))
                    v.tensor_tensor(ss.rearrange("p (t h) -> p t h", h=2), ss.rearrange("p (t h) -> p t h", h=2),
                                    stat[:, 32 + lo // 2:32 + hi // 2].unsqueeze(2).to_broadcast([P, (hi - lo) // 2, 2]),
                                    ALU.add).then_inc(ss_ready, 1)

                def scale_k(m):
                    lo, hi = K_PARTS[m]
                    dve.wait_ge(std_ready, 3 * i + 2 + m)
                    v.reciprocal(smal[:, 16 + lo:16 + hi], smal[:, 16 + lo:16 + hi]).then_inc(rk_ready, 1)
                    dve.wait_ge(rk_ready, 2 * i + 1 + m)
                    kk = kvtok.rearrange("p t (h n) -> p (t h) n", h=2)[:, lo:hi, 0:NOPE]
                    v.tensor_tensor(kk, kk, smal[:, 16 + lo:16 + hi].unsqueeze(2).to_broadcast([P, hi - lo, NOPE]),
                                    ALU.mult).then_inc(kn_ready, 1)

                sum_k(0)
                take(9)
                scale_k(0)
                sum_k(1)
                scale_k(1)
                for g in (1, 3, 5, 7):
                    dve.wait_ge(trn, 8 * i + g + 1)
                    if g == 1:
                        ins = v.tensor_scalar(qT[:, 1, :], PS[:, 5, :], gqk, None, ALU.mult)
                    elif g == 3:
                        ins = v.tensor_copy(kT[:, 0, 0:BANK], PS[:, 5, :])
                    elif g == 5:
                        ins = v.tensor_copy(kT[:, :, BANK:KEYS], PS[:, 5, :].rearrange("p (a b) -> p a b", a=2))
                    else:
                        ins = v.tensor_copy(kTr[:, BANK:KEYS], PS[:, 5, 0:KEYS - BANK])
                    ins.then_inc(trn_d, 1)

                def norm(r):
                    dve.wait_ge(exp_done, 8 * i + r + 1)
                    own.link(v.reciprocal(stat[:, 70 + r % 2:71 + r % 2], stat[:, 68 + r % 2:69 + r % 2]))
                    v.tensor_scalar(prob[:, r % 2, :], prob[:, r % 2, :], stat[:, 70 + r % 2:71 + r % 2], None,
                                    ALU.mult).then_inc(p_norm, 1)

                def top(r):
                    dve.wait_ge(s_done, 8 * i + r + 1)
                    own.link(v.tensor_reduce(stat[:, 66 + r % 2:67 + r % 2], PS[:, 2 * (r % 2):2 * (r % 2) + 2, 0:SCR], AX.XY, ALU.max))
                    v.tensor_scalar(stat[:, 64 + r % 2:65 + r % 2], stat[:, 66 + r % 2:67 + r % 2], -SCALE, None,
                                    ALU.mult).then_inc(nmax, 1)

                def take_pT(r):
                    dve.wait_ge(pT_done, 8 * i + r + 1)
                    v.tensor_copy(pT[r // XT][:, 4:6, (r % XT) * P:(r % XT + 1) * P],
                                  PS[:, 5, 0:2 * P].rearrange("p (a b) -> p a b", a=2)).then_inc(pT_d, 1)

                for r in range(2 * XT):
                    if r >= 1:
                        norm(r - 1)
                    top(r)
                    if r >= 1:
                        take_pT(r - 1)
                norm(2 * XT - 1)
                take_pT(2 * XT - 1)

            first_then_loop(dve, pair, PAIRS)
            own.n = base + STEPS_IN_PAIR * PAIRS

            def router_part(L):
                A = scl[L][1]
                for t in range(XT + 3):
                    if L == 0 and t == 0:
                        for u in later_units(0):
                            ada_take(u)
                        dve.wait_ge(ada_out, UNITS)
                    if t < XT:
                        dve.wait_ge(mo_done[L], t + 1)
                        if t >= 1:
                            dve.wait_ge(x_new[L], t)
                        v.tensor_tensor(mo_tmp.rearrange("p (a b) -> p a b", a=2), PS[:, 2 * (t % 2):2 * (t % 2) + 2, :],
                                        gate_mix[L].rearrange("p (a b) -> p a b", a=2), ALU.mult).then_inc(mo_mul[L], 1)
                    if L == 0 and t == 1:
                        for u in later_units(1):
                            ada_take(u)
                        dve.wait_ge(mod_ready, 4)
                    if 1 <= t <= XT:
                        w = t - 1
                        dve.wait_ge(xnT[L], w + 1)
                        if w >= 1:
                            dve.wait_ge(hf_ready[L], w)
                        v.tensor_tensor(hf_tmp.rearrange("p (k m) -> p k m", k=KC),
                                        PS[:, 4:6, :].rearrange("p a (k m) -> p (a k) m", k=4),
                                        A[:, :, 0:1].to_broadcast([P, KC, P]), ALU.mult).then_inc(hf_mul[L], 1)
                    if t < XT:
                        dve.wait_ge(x_std[L], t + 1)
                        if t >= 2:
                            dve.wait_ge(xnT[L], t - 1)
                            dve.wait_ge((xn_st0, xn_st1)[t % 2][L], 16 * (t // 2))
                        own.link(v.reciprocal(stat[:, 8 + t:9 + t], stat[:, 8 + t:9 + t]))
                        v.tensor_scalar(xnt[:, t % 2, :], xres[L][:, t, :], stat[:, 8 + t:9 + t], None, ALU.mult).then_inc(xn_ready[L], 1)
                    if 2 <= t <= XT + 1:
                        w = t - 2
                        dve.wait_ge(lg_done[L], w + 1)
                        own.link(v.tensor_reduce(stat[:, 18:19], PS[:, 6, 0:E], AX.X, ALU.max))
                        v.tensor_scalar(stat[:, 16:17], stat[:, 18:19], -1.0, None, ALU.mult).then_inc(lg_neg[L], 1)
                        dve.wait_ge(lg_exp[L], w + 1)
                        own.link(v.reciprocal(stat[:, 19:20], stat[:, 17:18]))
                        v.tensor_scalar(aff[:, w, :], probs, stat[:, 19:20], None, ALU.mult).then_inc(lg_aff[L], 1)
                    if t >= 3:
                        w = t - 3
                        dve.wait_ge(affT_ps[L], w + 1)
                        v.tensor_copy(affT[:, w * P:(w + 1) * P], PS[0:E, 7, 0:P]).then_inc(affT_sb[L], 1)
                dve.wait_ge(affT_sb[L], XT)
                for r in range(CAP // 8):
                    now, nxt = (affT[:, (r + m) % 2 * T:((r + m) % 2 + 1) * T] for m in range(2))
                    best = top_v[:, 8 * r:8 * r + 8]
                    own.link(v.max(best, now))
                    v.max_index(top_i[:, 8 * r:8 * r + 8], best, now)
                    if r < CAP // 8 - 1:
                        own.link(v.match_replace(nxt, best, now, -1.0))
                    else:
                        own.link(v.tensor_copy(slots_v[:, 0:CAP], top_v))
                v.tensor_copy(slots_v[:, CAP:P], top_v)
                v.tensor_scalar(slots_i[:, 0:CAP], top_i, 2.0, None, ALU.mult)
                own.link(v.tensor_scalar(slots_i[:, CAP:P], top_i, 2.0, 1.0, ALU.mult, ALU.add))
                dve.sem_inc(slots_f[L], 1)
                dve.wait_ge(slots_T[L], 1)
                v.tensor_copy(row_no, PS[:, 7, 0:E])
                v.tensor_copy(gate_e, PS[:, 7, E:2 * E]).then_inc(slots_ready[L], 1)

            def experts(L):
                A, B = scl[L][1], modv[L][1]

                def modulate(e, s):
                    dve.wait_ge(xs_T[L], e + 1)
                    a = A[:, :, 0].rearrange("p (h q) -> p q h", h=2).unsqueeze(3).to_broadcast([P, 4, 2, CAP])
                    b = B[:, 0, :, 0].rearrange("p (h q) -> p q h", h=2).unsqueeze(3).to_broadcast([P, 4, 2, CAP])
                    own.link(v.tensor_tensor(xs_m.rearrange("p (q h m) -> p q h m", q=4, h=2),
                                             PS[:, 4, :].rearrange("p (q h m) -> p q h m", q=4, h=2), a, ALU.mult))
                    v.tensor_tensor(xsT[:, s, :].rearrange("p (q h m) -> p q h m", q=4, h=2),
                                    xs_m.rearrange("p (q h m) -> p q h m", q=4, h=2), b, ALU.add).then_inc(xs_mod[L], 1)

                def two_experts(i):
                    own.n = base + 2 * i
                    for s in range(2):
                        e = 2 * i + s
                        dve.wait_ge(silu_ok[L], e + 1)
                        dve.wait_ge(up_mm[L], e + 1)
                        wait(dve, hid_T[L], e)
                        v.tensor_tensor(hid, silu_a, PS[:, 1, :], ALU.mult).then_inc(hid_ok[L], 1)
                        if not (isinstance(e, int) and e == E - 1):
                            modulate(e + 1, 1 - s)
                        dve.wait_ge(down_mm[L], e + 1)
                        wait(dve, scattered[L], 16 * (e - 1))
                        v.scalar_tensor_tensor(out=y_s[:, s, :], in0=PS[:, 2, :], scalar=gate_e[:, bass.ds(e, 1)],
                                               in1=gate_ffn[L], op0=ALU.mult, op1=ALU.mult).then_inc(y_ok[L], 1)

                modulate(0, 0)
                base = own.n
                first_then_loop(dve, two_experts, E // 2, last=1)
                own.n = base + E - 1

            router_part(0)
            experts(0)

            for h in range(2):
                dve.wait_ge(std_in, 2 + h)
                own.link(v.reciprocal(stat[:, 8 + 2 * h:10 + 2 * h], stat[:, 8 + 2 * h:10 + 2 * h]))
                for t in (2 * h, 2 * h + 1):
                    v.tensor_scalar(xnc[:, t, :], xres[1][:, t, :], stat[:, 8 + t:9 + t], None, ALU.mult).then_inc(xn_in, 1)
            v.memset(u_pad[:, 0:1], 0.0)
            own.link(v.memset(u_pad[:, T + 1:T + 2], 0.0))
            for n in range(KC):
                w3 = [vec[:, V_CONV + m * KC + n:V_CONV + m * KC + n + 1] for m in range(3)]
                dve.wait_ge(cv_mm, n + 1)
                dve.wait_ge(c_copied, n + 1)
                own.link(v.tensor_tensor(u_pad[:, 1:T + 1], PS[:, 3 * (n % 2) + 2, :], c_sb[:, n % 2, :], ALU.mult))
                own.link(v.tensor_scalar(y_sb, u_pad[:, 0:T], w3[0], None, ALU.mult))
                for m in (1, 2):
                    own.link(v.scalar_tensor_tensor(out=y_sb, in0=u_pad[:, m:T + m], scalar=w3[m], in1=y_sb,
                                                    op0=ALU.mult, op1=ALU.add))
                dve.wait_ge(conv_mm, n + 1)
                v.tensor_tensor(zT[:, n, :], PS[:, 3 * (n % 2), :], y_sb, ALU.mult).then_inc(z_ready, 1)
            router_part(1)
            experts(1)

        @block.gpsimd
        def _(pool):
            g = nc.gpsimd
            own = Chain(pool, pool_step)
            pool.wait_ge(krot_ready, 1)
            base = 0
            def pair(i):
                own.n = base + i
                pool.wait_ge(qg_ready, i + 1)
                q5 = qtok.rearrange("p t (h n) -> p (t h) n", h=2)[:, :, NOPE:QK].rearrange("p t (a b f) -> p t a b f", a=2, b=2)
                o5 = q_rot.rearrange("p t (h n) -> p (t h) n", h=2).rearrange("p t (a b f) -> p t a b f", a=2, b=2)
                c8 = [rope_cs[:, m].rearrange("p t (a f) -> p t a f", a=2) for m in range(2)]
                t8 = [rtmp[:, 2 + m].rearrange("p (t a f) -> p t a f", a=2, f=RF) for m in range(2)]
                g.tensor_tensor(t8[0], q5[:, :, :, 1, :], c8[0], ALU.mult)
                own.link(g.tensor_tensor(t8[1], q5[:, :, :, 0, :], c8[1], ALU.mult))
                g.tensor_tensor(o5[:, :, :, 1, :], t8[0], t8[1], ALU.add).then_inc(qrot_p, 1)
                pool.wait_ge(rk_ready, 2 * i + 2)
                g.tensor_tensor(kr_s.rearrange("p t (h n) -> p t h n", h=2),
                                krot.unsqueeze(2).to_broadcast([P, NT, 2, ROPE]),
                                smal[:, 16:28].rearrange("p (t h) -> p t h", h=2).unsqueeze(3).to_broadcast([P, NT, 2, ROPE]),
                                ALU.mult).then_inc(krs_ready, 1)

            first_then_loop(pool, pair, PAIRS)
            own.n = base + PAIRS

            def router_part(L):
                B = modv[L][1]
                if L == 0:
                    pool.wait_ge(xres_in, 16)
                for t in range(XT + 1):
                    if t < XT:
                        pool.wait_ge(mo_mul[L], t + 1)
                        g.tensor_tensor(xres[L][:, t, :], xres[L][:, t, :], mo_tmp, ALU.add).then_inc(x_new[L], 1)
                    if t >= 1:
                        w = t - 1
                        pool.wait_ge(hf_mul[L], w + 1)
                        if w >= 2:
                            pool.wait_ge(lg_done[L], w - 1)
                        g.tensor_tensor(hfT[:, w % 2, :].rearrange("p (k m) -> p k m", k=KC),
                                        hf_tmp.rearrange("p (k m) -> p k m", k=KC),
                                        B[:, 0, :, 0:1].to_broadcast([P, KC, P]), ALU.add).then_inc(hf_ready[L], 1)

            def experts(L):
                xn_half = xn_dram.rearrange("t (h d) -> (t h) d", h=2)
                acc_half = acc_dram[L].rearrange("t (h d) -> (t h) d", h=2)

                def gather(e, s):
                    g.tensor_copy(row_in[s], row_no[:, bass.ds(e, 1)]).then_inc(row_copied[L], 1)
                    pool.wait_ge(row_copied[L], e + 1)
                    pool.sem_inc(turn, 1)
                    g.indirect_dma_start(out=xs[:, s, :], out_offset=None, in_=xn_half,
                                         in_offset=bass.IndirectOffsetOnAxis(ap=row_in[s], axis=0)
                                         ).then_inc((xs_in0, xs_in1)[s][L], 16)

                def two_experts(i):
                    for s in range(2):
                        e = 2 * i + s
                        if not (isinstance(e, int) and e >= E - 2):
                            pool.wait_ge(xs_T[L], e + 1)
                            gather(e + 2, s)
                        wait(pool, scattered[L], 16 * e)
                        g.tensor_copy(row_out, row_no[:, bass.ds(e, 1)]).then_inc(row_out_ok[L], 1)
                        pool.wait_ge(row_out_ok[L], e + 1)
                        pool.wait_ge(y_ok[L], e + 1)
                        pool.sem_inc(turn, 1)
                        g.indirect_dma_start(out=acc_half, out_offset=bass.IndirectOffsetOnAxis(ap=row_out, axis=0),
                                             in_=y_s[:, s, :], in_offset=None, compute_op=ALU.add).then_inc(scattered[L], 16)

                pool.wait_ge(slots_ready[L], 1)
                pool.wait_ge(acc_stored[L], 16 * XT)
                pool.wait_ge(xn_st0[L], 16 * XT // 2)
                pool.wait_ge(xn_st1[L], 16 * XT // 2)
                gather(0, 0)
                gather(1, 1)
                first_then_loop(pool, two_experts, E // 2, last=1)

            router_part(0)
            experts(0)
            router_part(1)
            experts(1)


_INS = ["x", "c", "ctx", "c_ctx", "norm_mix", "norm_ffn", "ada_w", "ada_b", "mla_w_in", "mla_q_norm", "mla_w_qb",
        "mla_kv_norm", "mla_w_kvb", "mla_q_gain", "mla_k_gain", "mla_w_out", "conv_w_in", "conv_w", "conv_w_out",
        "router_w", "exp_w_gate", "exp_w_up", "exp_w_down"]


def rope_tables(tokens, freqs):
    n = np.arange(tokens)
    pos = np.stack([n // GRID_W, n % GRID_W], axis=-1).astype(np.float32)
    inv = np.float32(ROPE_THETA) ** (-np.arange(freqs, dtype=np.float32) / np.float32(freqs))
    ang = (pos[:, :, None] * inv).astype(np.float32).reshape(tokens, 2 * freqs)
    return np.stack([np.cos(ang), np.sin(ang)]).astype(np.float32)


def kernel(**inputs):
    import concourse.bacc as bacc
    from concourse.bass_utils import run_bass_kernel_spmd

    nc = bacc.Bacc("TRN2", target_bir_lowering=False, num_devices=1)
    host = {name: np.ascontiguousarray(inputs[name]) for name in _INS}
    host["ident"] = np.eye(P, dtype=np.float32)
    host["rope"] = rope_tables(host["x"].shape[1], (host["mla_q_gain"].shape[1] - P) // 4)
    arrays, args = {}, []
    for name, a in host.items():
        arrays[f"in_{name}_dram"] = a
        args.append(nc.dram_tensor(f"in_{name}_dram", a.shape, mybir.dt.from_np(a.dtype), kind="ExternalInput").ap())
    args.append(nc.dram_tensor("out_0_dram", host["x"].shape, F32, kind="ExternalOutput").ap())
    build(nc, *args)
    r = run_bass_kernel_spmd(nc, [arrays], core_ids=[0])
    return r.results[0]["out_0_dram"]
```
